# Optimizing a Trainium2 kernel written in Bass

```python
import jax
import jax.numpy as jnp
from jax import lax
import numpy as np
import math
import jax, jax.numpy as jnp

D_MODEL = 1024
BATCH = 1
SEQ = 512
DEPTH = 1

N_META = 16
EPS = 1e-6

ATT_HEADS = 8
ATT_HEAD_DIM = 64
ATT_WIDTH = ATT_HEADS * ATT_HEAD_DIM
Q_BLOCK = 128

HGRN_HEADS = 8
HGRN_K = 128
HGRN_V = 128
HGRN_KEY_WIDTH = HGRN_HEADS * HGRN_K
HGRN_WIDTH = HGRN_HEADS * HGRN_V
HGRN_CHUNK = 64

N_GROUPS = 4
EXPERTS_PER_GROUP = 8
N_EXPERTS = N_GROUPS * EXPERTS_PER_GROUP
TOP_K = 2
EXPERT_FF = 512
MOE_BLOCK = 128

IN_SIZES = (ATT_WIDTH, ATT_WIDTH, ATT_WIDTH, ATT_HEADS, HGRN_KEY_WIDTH, HGRN_KEY_WIDTH, HGRN_WIDTH, HGRN_WIDTH, D_MODEL, D_MODEL)
IN_WIDTH = sum(IN_SIZES)


def split_points(sizes):
    pts, acc = [], 0
    for s in sizes[:-1]:
        acc += s
        pts.append(acc)
    return pts

def rms_norm(x, w):
    xf = x.astype(jnp.float32)
    y = xf * lax.rsqrt(jnp.mean(xf * xf, axis=-1, keepdims=True) + EPS)
    return (y * w.astype(jnp.float32)).astype(x.dtype)

def forgetting_attention(q, k, v, log_f):
    B, L, H, Dh = q.shape
    scale = Dh ** -0.5
    c = jnp.cumsum(log_f, axis=1)
    c_k = jnp.transpose(c, (0, 2, 1))

    def attend(q_blk, c_q, q_pos, k_blk, v_blk, c_kb, k_pos):
        s = jnp.einsum('bqhd,bkhd->bhqk', q_blk, k_blk).astype(jnp.float32) * scale
        s = s + jnp.transpose(c_q, (0, 2, 1))[..., :, None] - c_kb[:, :, None, :]
        mask = k_pos[None, :] <= q_pos[:, None]
        s = jnp.where(mask[None, None], s, -jnp.inf)
        p = jax.nn.softmax(s, axis=-1).astype(v_blk.dtype)
        return jnp.einsum('bhqk,bkhd->bqhd', p, v_blk)

    meta_pos = jnp.arange(N_META)
    o_meta = attend(q[:, :N_META], c[:, :N_META], meta_pos, k[:, :N_META], v[:, :N_META], c_k[:, :, :N_META], meta_pos)

    n_blk = (L - N_META) // Q_BLOCK
    k_pos = jnp.arange(L)

    def real_block(i):
        start = N_META + i * Q_BLOCK
        q_blk = lax.dynamic_slice_in_dim(q, start, Q_BLOCK, axis=1)
        c_q = lax.dynamic_slice_in_dim(c, start, Q_BLOCK, axis=1)
        q_pos = start + jnp.arange(Q_BLOCK)
        return attend(q_blk, c_q, q_pos, k, v, c_k, k_pos)

    o_real = lax.map(real_block, jnp.arange(n_blk))
    o_real = jnp.moveaxis(o_real, 0, 1).reshape(B, n_blk * Q_BLOCK, H, Dh)
    return jnp.concatenate([o_meta, o_real], axis=1)

def hgrn2_chunk(state, chunk):
    q, log_f, k, v = chunk
    C = q.shape[1]
    b = jnp.cumsum(log_f, axis=1)
    o_inter = jnp.einsum('bchk,bhkv->bchv', q * jnp.exp(b), state)
    causal = jnp.tril(jnp.ones((C, C), dtype=bool))
    diff = b[:, :, None] - b[:, None, :]
    decay = jnp.exp(jnp.where(causal[None, :, :, None, None], diff, -jnp.inf))
    scores = jnp.sum(q[:, :, None] * k[:, None] * decay, axis=-1)
    o_intra = jnp.einsum('btsh,bshv->bthv', scores, v)
    b_last = b[:, -1]
    k_dec = k * jnp.exp(b_last[:, None] - b)
    new_state = jnp.exp(b_last)[..., None] * state + jnp.einsum('bshk,bshv->bhkv', k_dec, v)
    return new_state, o_inter + o_intra

def hgrn2_recurrence(q, log_f, k, v):
    B, L, H, K = q.shape
    V = v.shape[-1]
    state0 = jnp.zeros((B, H, K, V), jnp.float32)
    state1, o_meta = hgrn2_chunk(state0, (q[:, :N_META], log_f[:, :N_META], k[:, :N_META], v[:, :N_META]))
    n_chunks = (L - N_META) // HGRN_CHUNK

    def to_chunks(a):
        return jnp.moveaxis(a[:, N_META:].reshape(B, n_chunks, HGRN_CHUNK, H, a.shape[-1]), 1, 0)

    _, o_real = lax.scan(hgrn2_chunk, state1, (to_chunks(q), to_chunks(log_f), to_chunks(k), to_chunks(v)))
    o_real = jnp.moveaxis(o_real, 0, 1).reshape(B, L - N_META, H, V)
    return jnp.concatenate([o_meta, o_real], axis=1)

def hierarchical_moe(v2d, w_rg, b_rg, w_re, b_re, w_e_in, w_e_out):
    T, D = v2d.shape
    dtype = v2d.dtype
    vf = v2d.astype(jnp.float32)
    g_logits = vf @ w_rg.astype(jnp.float32) + b_rg.astype(jnp.float32)
    g_prob = jax.nn.softmax(g_logits, axis=-1)
    g_idx = jnp.argmax(g_logits, axis=-1)
    p_g = jnp.take_along_axis(g_prob, g_idx[:, None], axis=1)[:, 0]
    e_logits = (vf @ w_re.astype(jnp.float32) + b_re.astype(jnp.float32)).reshape(T, N_GROUPS, EXPERTS_PER_GROUP)
    e_sel = jnp.take_along_axis(e_logits, g_idx[:, None, None], axis=1)[:, 0]
    top_v, top_i = lax.top_k(e_sel, TOP_K)
    gate = jax.nn.softmax(top_v, axis=-1) * p_g[:, None]
    expert_id = (g_idx[:, None] * EXPERTS_PER_GROUP + top_i).astype(jnp.int32)

    A = T * TOP_K
    eid = expert_id.reshape(-1)
    tok = jnp.repeat(jnp.arange(T, dtype=jnp.int32), TOP_K)
    wt = gate.reshape(-1)
    order = jnp.argsort(eid)
    se, st, sw = eid[order], tok[order], wt[order]
    counts = jnp.bincount(eid, length=N_EXPERTS).astype(jnp.int32)
    starts = jnp.cumsum(counts) - counts
    pcounts = (counts + MOE_BLOCK - 1) // MOE_BLOCK * MOE_BLOCK
    pends = jnp.cumsum(pcounts)
    pstarts = pends - pcounts
    dest = pstarts[se] + jnp.arange(A, dtype=jnp.int32) - starts[se]
    n_blocks = -(-A // MOE_BLOCK) + N_EXPERTS
    rows_tok = jnp.full((n_blocks * MOE_BLOCK,), T, jnp.int32).at[dest].set(st)
    rows_w = jnp.zeros((n_blocks * MOE_BLOCK,), jnp.float32).at[dest].set(sw)
    blk_exp = jnp.clip(jnp.searchsorted(pends, jnp.arange(n_blocks, dtype=jnp.int32) * MOE_BLOCK, side='right'), 0, N_EXPERTS - 1)
    v_pad = jnp.concatenate([v2d, jnp.zeros((1, D), dtype)], axis=0)

    def run(args):
        tok_b, e = args
        xb = v_pad[tok_b]
        hu = xb @ w_e_in[e]
        a, u = jnp.split(hu, 2, axis=-1)
        return (jax.nn.silu(a) * u) @ w_e_out[e]

    ys = lax.map(run, (rows_tok.reshape(n_blocks, MOE_BLOCK), blk_exp)).reshape(-1, D)
    ys = ys * rows_w[:, None].astype(ys.dtype)
    out = jnp.zeros((T + 1, D), ys.dtype).at[rows_tok].add(ys)
    return out[:T].astype(dtype)

def first_inputs(seed: int = 0) -> dict:
    key = jax.random.key(seed)
    ks = jax.random.split(key, 18)
    n = jax.random.normal
    f32 = jnp.float32
    return {
        'x': n(ks[0], (BATCH, SEQ, D_MODEL), f32),
        'meta_tokens': n(ks[1], (N_META, D_MODEL), f32),
        'norm_mix_w': 1.0 + 0.02 * n(ks[2], (DEPTH, D_MODEL), f32),
        'w_in': n(ks[3], (DEPTH, D_MODEL, IN_WIDTH), f32) * D_MODEL ** -0.5,
        'attn_forget_b': 3.0 + 0.5 * n(ks[4], (DEPTH, ATT_HEADS), f32),
        'hgrn_lb_logits': 0.1 * n(ks[5], (DEPTH + 1, HGRN_KEY_WIDTH), f32),
        'hgrn_norm_w': 1.0 + 0.02 * n(ks[6], (DEPTH, HGRN_V), f32),
        'w_attn_out': n(ks[7], (DEPTH, ATT_WIDTH, D_MODEL), f32) * ATT_WIDTH ** -0.5,
        'w_hgrn_out': n(ks[8], (DEPTH, HGRN_WIDTH, D_MODEL), f32) * HGRN_WIDTH ** -0.5,
        'w_o': n(ks[9], (DEPTH, D_MODEL, D_MODEL), f32) * D_MODEL ** -0.5,
        'norm_ffn_w': 1.0 + 0.02 * n(ks[10], (DEPTH, D_MODEL), f32),
        'w_router_group': n(ks[11], (DEPTH, D_MODEL, N_GROUPS), f32) * D_MODEL ** -0.5,
        'b_router_group': 0.01 * n(ks[12], (DEPTH, N_GROUPS), f32),
        'w_router_expert': n(ks[13], (DEPTH, D_MODEL, N_EXPERTS), f32) * D_MODEL ** -0.5,
        'b_router_expert': 0.01 * n(ks[14], (DEPTH, N_EXPERTS), f32),
        'w_expert_in': n(ks[15], (DEPTH, N_EXPERTS, D_MODEL, 2 * EXPERT_FF), f32) * D_MODEL ** -0.5,
        'w_expert_out': n(ks[16], (DEPTH, N_EXPERTS, EXPERT_FF, D_MODEL), f32) * EXPERT_FF ** -0.5,
        'norm_final_w': 1.0 + 0.02 * n(ks[17], (D_MODEL,), f32),
    }

def first_block(x, meta_tokens, norm_mix_w, w_in, attn_forget_b, hgrn_lb_logits, hgrn_norm_w, w_attn_out, w_hgrn_out, w_o, norm_ffn_w, w_router_group, b_router_group, w_router_expert, b_router_expert, w_expert_in, w_expert_out, norm_final_w):
    B, S, D = x.shape
    L = S + N_META
    meta = jnp.broadcast_to(meta_tokens.astype(x.dtype)[None], (B, N_META, D))
    h = jnp.concatenate([meta, x], axis=1)
    lb_all = jnp.cumsum(jax.nn.softmax(hgrn_lb_logits.astype(jnp.float32), axis=0), axis=0)
    for layer in range(DEPTH):
        u = rms_norm(h, norm_mix_w[layer])
        proj = u @ w_in[layer]
        q_a, k_a, v_a, f_a, q_h, f_h, i_h, g_h, gate_a, gate_h = jnp.split(proj, split_points(IN_SIZES), axis=-1)

        log_f_a = jax.nn.log_sigmoid(f_a.astype(jnp.float32) + attn_forget_b[layer].astype(jnp.float32))
        att_shape = (B, L, ATT_HEADS, ATT_HEAD_DIM)
        o_a = forgetting_attention(q_a.reshape(att_shape), k_a.reshape(att_shape), v_a.reshape(att_shape), log_f_a)
        y_a = o_a.reshape(B, L, ATT_WIDTH) @ w_attn_out[layer]

        lb = lb_all[layer]
        f_val = lb + (1.0 - lb) * jax.nn.sigmoid(f_h.astype(jnp.float32))
        key_shape = (B, L, HGRN_HEADS, HGRN_K)
        log_f_h = jnp.log(f_val).reshape(key_shape)
        k_h = (1.0 - f_val).reshape(key_shape)
        q_hr = q_h.astype(jnp.float32).reshape(key_shape) * HGRN_K ** -0.5
        v_h = i_h.astype(jnp.float32).reshape(B, L, HGRN_HEADS, HGRN_V)
        o_h = hgrn2_recurrence(q_hr, log_f_h, k_h, v_h)
        o_h = rms_norm(o_h, hgrn_norm_w[layer]) * jax.nn.sigmoid(g_h.astype(jnp.float32)).reshape(B, L, HGRN_HEADS, HGRN_V)
        y_h = o_h.reshape(B, L, HGRN_WIDTH).astype(x.dtype) @ w_hgrn_out[layer]

        mixed = jax.nn.sigmoid(gate_a) * y_a + jax.nn.sigmoid(gate_h) * y_h
        h = h + mixed @ w_o[layer]

        v_in = rms_norm(h, norm_ffn_w[layer]).reshape(B * L, D)
        moe_out = hierarchical_moe(v_in, w_router_group[layer], b_router_group[layer], w_router_expert[layer], b_router_expert[layer], w_expert_in[layer], w_expert_out[layer])
        h = h + moe_out.reshape(B, L, D)
    return rms_norm(h, norm_final_w)[:, N_META:]


D_FF = 2816
FOURIER_GROUPS = 8
FOURIER_GROUP_DIM = 64
D_FOURIER = FOURIER_GROUPS * FOURIER_GROUP_DIM
D_SCONV = 512
SCONV_WIDTH = 3
DN_HEADS = 4
DN_HEAD_DIM = 128
D_DN = DN_HEADS * DN_HEAD_DIM
DN_CONV_WIDTH = 3
CHUNK = 64
N_BRANCH = 3
PROJ_SIZES = (D_FOURIER, 3 * D_SCONV, 3 * D_DN, D_DN, 2 * DN_HEADS, 2 * DN_HEADS, N_BRANCH * D_MODEL)
D_IN_PROJ = D_FOURIER + 3 * D_SCONV + 3 * D_DN + D_DN + 4 * DN_HEADS + N_BRANCH * D_MODEL


def rmsnorm(x, g):
    xf = x.astype(jnp.float32)
    y = xf * lax.rsqrt(jnp.mean(xf * xf, axis=-1, keepdims=True) + EPS)
    return (y * g.astype(jnp.float32)).astype(x.dtype)

def swiglu(x, wi, wo):
    a, b = jnp.split(x @ wi, 2, axis=-1)
    return (jax.nn.silu(a) * b) @ wo

def conv3_centred(x, w):
    xp = jnp.pad(x, ((0, 0), (1, 1), (0, 0)))
    return w[0] * xp[:, :-2] + w[1] * xp[:, 1:-1] + w[2] * xp[:, 2:]

def fourier_mix(u):
    B, L, _ = u.shape
    ug = u.astype(jnp.float32).reshape(B, L, FOURIER_GROUPS, FOURIER_GROUP_DIM)
    y = jnp.fft.fft2(ug, axes=(1, 3), norm="ortho").real
    return y.reshape(B, L, D_FOURIER).astype(u.dtype)

def short_conv_mix(u, w):
    b, c, h = jnp.split(u, 3, axis=-1)
    return b * conv3_centred(c * h, w)

def l2norm(x):
    return x * lax.rsqrt(jnp.sum(x * x, axis=-1, keepdims=True) + EPS)

def chunk_gated_delta(q, k, v, beta, g):
    B, H, N, C, DK = q.shape
    DV = v.shape[-1]
    lower = jnp.tril(jnp.ones((C, C), bool))
    strict = jnp.tril(jnp.ones((C, C), bool), -1)
    gc = jnp.cumsum(g, axis=-1)
    diff = gc[..., :, None] - gc[..., None, :]
    decay_mask = jnp.exp(jnp.where(lower, diff, -jnp.inf))
    k_beta = k * beta[..., None]
    v_beta = v * beta[..., None]
    m = jnp.where(strict, jnp.einsum('bhnck,bhnsk->bhncs', k_beta, k) * decay_mask, 0.0)
    eye = jnp.eye(C, dtype=q.dtype)
    t = lax.linalg.triangular_solve(eye + m, jnp.broadcast_to(eye, m.shape), left_side=True,
                                    lower=True, unit_diagonal=True)
    u = t @ v_beta
    w = t @ (k_beta * jnp.exp(gc)[..., None])
    attn = jnp.einsum('bhnck,bhnsk->bhncs', q, k) * decay_mask
    q_dec = q * jnp.exp(gc)[..., None]
    k_dec = k * jnp.exp(gc[..., -1:] - gc)[..., None]
    g_last = jnp.exp(gc[..., -1])

    def step(S, xs):
        attn_n, u_n, w_n, qd_n, kd_n, gl_n = xs
        v_new = u_n - w_n @ S
        o = qd_n @ S + attn_n @ v_new
        S = S * gl_n[..., None, None] + jnp.swapaxes(kd_n, -1, -2) @ v_new
        return S, o

    xs = tuple(jnp.moveaxis(a, 2, 0) for a in (attn, u, w, q_dec, k_dec, g_last))
    S0 = jnp.zeros((B, H, DK, DV), q.dtype)
    _, o = lax.scan(step, S0, xs)
    return jnp.moveaxis(o, 0, 2)

def deltanet_branch(qkv, z, beta_logit, alpha_logit, conv_w, A_log, dt_bias, norm_w):
    B, L, _ = qkv.shape
    f32 = jnp.float32
    qkv = jax.nn.silu(conv3_centred(qkv, conv_w)).astype(f32)
    q, k, v = jnp.split(qkv, 3, axis=-1)
    q = l2norm(q.reshape(B, L, DN_HEADS, DN_HEAD_DIM)) * (DN_HEAD_DIM ** -0.5)
    k = l2norm(k.reshape(B, L, DN_HEADS, DN_HEAD_DIM))
    v = v.reshape(B, L, DN_HEADS, DN_HEAD_DIM)
    beta = jax.nn.sigmoid(beta_logit.astype(f32)).reshape(B, L, 2, DN_HEADS)
    g = -jnp.exp(A_log.astype(f32)) * jax.nn.softplus(
        alpha_logit.astype(f32).reshape(B, L, 2, DN_HEADS) + dt_bias.astype(f32))
    pad = CHUNK - N_META
    padt = lambda a: jnp.pad(a, ((0, 0), (pad, 0)) + ((0, 0),) * (a.ndim - 2))
    q, k, v, beta, g = padt(q), padt(k), padt(v), padt(beta), padt(g)
    Lp = L + pad
    N = Lp // CHUNK

    def chunks4(a):
        return a.reshape(B, N, CHUNK, DN_HEADS, -1).transpose(0, 3, 1, 2, 4)

    def chunks3(a):
        return a.reshape(B, N, CHUNK, DN_HEADS).transpose(0, 3, 1, 2)

    def unchunk(o):
        return o.transpose(0, 2, 3, 1, 4).reshape(B, Lp, DN_HEADS, DN_HEAD_DIM)

    o_fwd = unchunk(chunk_gated_delta(chunks4(q), chunks4(k), chunks4(v),
                                      chunks3(beta[:, :, 0]), chunks3(g[:, :, 0])))
    fl = lambda a: jnp.flip(a, axis=1)
    o_bwd = fl(unchunk(chunk_gated_delta(chunks4(fl(q)), chunks4(fl(k)), chunks4(fl(v)),
                                         chunks3(fl(beta[:, :, 1])), chunks3(fl(g[:, :, 1])))))
    o = (o_fwd + o_bwd)[:, pad:]
    o = o * lax.rsqrt(jnp.mean(o * o, axis=-1, keepdims=True) + EPS) * norm_w.astype(f32)
    o = o * jax.nn.silu(z.astype(f32).reshape(B, L, DN_HEADS, DN_HEAD_DIM))
    return o.reshape(B, L, D_DN).astype(z.dtype)

def hybrid_mixer(h, w_in, sconv_w, dn_conv_w, dn_A_log, dn_dt_bias, dn_norm,
                 w_fourier, w_sconv_out, w_dn_out, w_out):
    B, L, D = h.shape
    proj = h @ w_in
    idx = [int(s) for s in np.cumsum(PROJ_SIZES)[:-1]]
    u_f, u_sc, u_qkv, z, b_logit, a_logit, gate_logit = jnp.split(proj, idx, axis=-1)
    y_f = fourier_mix(u_f) @ w_fourier
    y_sc = short_conv_mix(u_sc, sconv_w) @ w_sconv_out
    y_dn = deltanet_branch(u_qkv, z, b_logit, a_logit, dn_conv_w, dn_A_log, dn_dt_bias,
                           dn_norm) @ w_dn_out
    gates = jax.nn.sigmoid(gate_logit).reshape(B, L, N_BRANCH, D)
    merged = gates[:, :, 0] * y_f + gates[:, :, 1] * y_sc + gates[:, :, 2] * y_dn
    return merged @ w_out

def second_inputs(seed: int = 0) -> dict:
    key = jax.random.key(seed)
    ks = jax.random.split(key, 20)
    f32 = jnp.float32

    def dense(k, shape, fan_in):
        return jax.random.normal(k, shape, f32) * fan_in ** -0.5

    x = jax.random.normal(ks[0], (BATCH, SEQ, D_MODEL), f32)
    meta_tokens = jax.random.normal(ks[1], (N_META, D_MODEL), f32)
    norm_gains = 1.0 + 0.05 * jax.random.normal(ks[2], (DEPTH, 6, D_MODEL), f32)
    ffn1_wi = dense(ks[3], (DEPTH, D_MODEL, 2 * D_FF), D_MODEL)
    ffn1_wo = dense(ks[4], (DEPTH, D_FF, D_MODEL), D_FF)
    ffn2_wi = dense(ks[5], (DEPTH, D_MODEL, 2 * D_FF), D_MODEL)
    ffn2_wo = dense(ks[6], (DEPTH, D_FF, D_MODEL), D_FF)
    w_in = dense(ks[7], (DEPTH, D_MODEL, D_IN_PROJ), D_MODEL)
    sconv_w = dense(ks[8], (DEPTH, SCONV_WIDTH, D_SCONV), SCONV_WIDTH)
    dn_conv_w = dense(ks[9], (DEPTH, DN_CONV_WIDTH, 3 * D_DN), DN_CONV_WIDTH)
    dn_A_log = jnp.log(jax.random.uniform(ks[10], (DEPTH, 2, DN_HEADS), f32, 1.0, 16.0))
    dt = jnp.exp(jax.random.uniform(ks[11], (DEPTH, 2, DN_HEADS), f32,
                                    math.log(1e-3), math.log(1e-1)))
    dn_dt_bias = dt + jnp.log(-jnp.expm1(-dt))
    dn_norm = 1.0 + 0.05 * jax.random.normal(ks[12], (DEPTH, DN_HEAD_DIM), f32)
    w_fourier = dense(ks[13], (DEPTH, D_FOURIER, D_MODEL), D_FOURIER)
    w_sconv_out = dense(ks[14], (DEPTH, D_SCONV, D_MODEL), D_SCONV)
    w_dn_out = dense(ks[15], (DEPTH, D_DN, D_MODEL), D_DN)
    w_out = dense(ks[16], (DEPTH, D_MODEL, D_MODEL), D_MODEL)
    return {"x": x, "meta_tokens": meta_tokens, "norm_gains": norm_gains,
            "ffn1_wi": ffn1_wi, "ffn1_wo": ffn1_wo, "ffn2_wi": ffn2_wi, "ffn2_wo": ffn2_wo,
            "w_in": w_in, "sconv_w": sconv_w, "dn_conv_w": dn_conv_w, "dn_A_log": dn_A_log,
            "dn_dt_bias": dn_dt_bias, "dn_norm": dn_norm, "w_fourier": w_fourier,
            "w_sconv_out": w_sconv_out, "w_dn_out": w_dn_out, "w_out": w_out}

def second_block(x, meta_tokens, norm_gains, ffn1_wi, ffn1_wo, ffn2_wi, ffn2_wo, w_in, sconv_w,
              dn_conv_w, dn_A_log, dn_dt_bias, dn_norm, w_fourier, w_sconv_out, w_dn_out, w_out):
    B = x.shape[0]
    meta = jnp.broadcast_to(meta_tokens[None].astype(x.dtype), (B, N_META, D_MODEL))
    h = jnp.concatenate([meta, x], axis=1)
    for l in range(DEPTH):
        n = norm_gains[l]
        h = h + 0.5 * rmsnorm(swiglu(rmsnorm(h, n[0]), ffn1_wi[l], ffn1_wo[l]), n[1])
        h = h + rmsnorm(hybrid_mixer(rmsnorm(h, n[2]), w_in[l], sconv_w[l], dn_conv_w[l],
                                     dn_A_log[l], dn_dt_bias[l], dn_norm[l], w_fourier[l],
                                     w_sconv_out[l], w_dn_out[l], w_out[l]), n[3])
        h = h + 0.5 * rmsnorm(swiglu(rmsnorm(h, n[4]), ffn2_wi[l], ffn2_wo[l]), n[5])
    return h[:, N_META:]


def setup_inputs(seed=0):
    out = dict(first_inputs(seed))
    for name, value in second_inputs(seed + 1).items():
        if name != "x":
            out[name + "_2"] = value
    return out


def reference(
    x, meta_tokens, norm_mix_w, w_in, attn_forget_b, hgrn_lb_logits, hgrn_norm_w, w_attn_out,
    w_hgrn_out, w_o, norm_ffn_w, w_router_group, b_router_group, w_router_expert,
    b_router_expert, w_expert_in, w_expert_out, norm_final_w, meta_tokens_2, norm_gains_2,
    ffn1_wi_2, ffn1_wo_2, ffn2_wi_2, ffn2_wo_2, w_in_2, sconv_w_2, dn_conv_w_2, dn_A_log_2,
    dn_dt_bias_2, dn_norm_2, w_fourier_2, w_sconv_out_2, w_dn_out_2, w_out_2,
):
    x = first_block(
        x, meta_tokens, norm_mix_w, w_in, attn_forget_b, hgrn_lb_logits, hgrn_norm_w,
        w_attn_out, w_hgrn_out, w_o, norm_ffn_w, w_router_group, b_router_group,
        w_router_expert, b_router_expert, w_expert_in, w_expert_out, norm_final_w,
    )
    return second_block(
        x, meta_tokens_2, norm_gains_2, ffn1_wi_2, ffn1_wo_2, ffn2_wi_2, ffn2_wo_2, w_in_2,
        sconv_w_2, dn_conv_w_2, dn_A_log_2, dn_dt_bias_2, dn_norm_2, w_fourier_2, w_sconv_out_2,
        w_dn_out_2, w_out_2,
    )


_drawn_inputs = setup_inputs


def setup_inputs(seed=0):
    import zlib

    import numpy as np

    out = dict(_drawn_inputs(seed))
    spreads = {}
    factors = {'hgrn_norm_w': 3.416, 'b_router_group': 6.093, 'b_router_expert': 4.662, 'dn_norm_2': 3.91}
    for name, (base, spread) in spreads.items():
        noise = np.random.default_rng([zlib.crc32(name.encode()), seed]).standard_normal(out[name].shape)
        drawn = base * np.exp(spread * noise) if base else spread * noise
        out[name] = jnp.asarray(drawn.astype(out[name].dtype))
    for name, factor in factors.items():
        out[name] = (out[name] * factor).astype(out[name].dtype)
    return out
```

```python
from contextlib import ExitStack

import numpy as np
import concourse.bass as bass
from concourse import mybir

F32 = mybir.dt.float32
I32 = mybir.dt.int32
U32 = mybir.dt.uint32
ALU = mybir.AluOpType
ACT = mybir.ActivationFunctionType
AX = mybir.AxisListType.X
MUL, ADD, SUB, MAX = ALU.mult, ALU.add, ALU.subtract, ALU.max

D, NM, S, L = 1024, 16, 512, 528
HF = 264
FF, NE, EFF = 2816, 32, 512
CAP = 64
NOV = 16
NBLK = NE + NOV
C2, NC2 = 88, 6
EPS = 1e-6
SLOT = 2048
NSLOT = 6
BIG = 1e30

VEC = {}
_n = 0
for _k, _w in (("mix", 8), ("lb", 16), ("hn", 1), ("ffn", 8), ("fin", 8), ("g", 48), ("sc", 12), ("dc", 36),
               ("dn", 1), ("fb", 1), ("al", 8), ("dt", 8), ("rb", 36)):
    VEC[_k] = _n
    _n += _w
NVEC = _n

CON = {}
_n = 0
for _k, _w in (("id", 128), ("u", 128), ("ui", 128), ("li", 128), ("tri", 128), ("mf", 128), ("mb", 128),
               ("lv", 7 * 64), ("rst", L), ("io", 64), ("tok", 4)):
    CON[_k] = _n
    _n += _w
NCON = _n


def constants():
    c = np.zeros((128, NCON), np.float32)
    p = np.arange(128)[:, None]
    f = np.arange(128)[None, :]

    def put(k, a):
        c[:a.shape[0], CON[k]:CON[k] + a.shape[1]] = a

    put("id", (p == f) * 1.0)
    put("u", (p < f) * 1.0)
    put("ui", (p <= f) * 1.0)
    put("li", (p >= f) * 1.0)
    put("tri", np.where(f <= p, 0.0, -BIG))
    put("mf", np.where(p <= f, 0.0, -BIG))
    put("mb", np.where(p >= f, 0.0, -BIG))
    for n in range(7):
        h = 64 >> n
        j = np.arange(64)
        t = j // h * 2 * h + h + j % h
        put_at = CON["lv"] + 64 * n
        c[:, put_at:put_at + 64] = (p // (2 * h) == t[None] // (2 * h)) & (p % (2 * h) < h)
    r = np.ones((128, L), np.float32)
    r[:, [0, 16, 144, 272, 400]] = 0.0
    put("rst", r)
    put("io", np.broadcast_to(np.arange(64.0), (128, 64)))
    put("tok", np.arange(128.0)[:, None] + 128 * np.arange(4)[None])
    lv2 = np.zeros((128, 2, 7, 128), np.float32)
    for n in range(7):
        b = 1 << n
        m = (p // (2 * b) == f // (2 * b)) & (p % (2 * b) < b) & (f % (2 * b) >= b)
        lv2[:, 0, n] = m
        lv2[:, 1, n] = m.T
    order = np.arange(L)
    k = np.outer(order, order) % L
    dft = np.stack([np.cos(2 * np.pi * k / L), -np.sin(2 * np.pi * k / L)]) / np.sqrt(L * 64.0)
    dft = dft.reshape(2, NC2, C2, L).transpose(1, 2, 0, 3)
    full = np.zeros((NC2, 128, 2, L), np.float32)
    full[:, :C2] = dft
    k = np.outer(np.arange(64), np.arange(64)) % 64
    small = np.zeros((128, 256), np.float32)
    for g in range(2):
        small[64 * g:64 * g + 64, 64 * g:64 * g + 64] = np.cos(2 * np.pi * k / 64)
        small[64 * g:64 * g + 64, 128 + 64 * g:192 + 64 * g] = np.sin(2 * np.pi * k / 64)
    return {"con": c, "lv2": lv2.reshape(128, -1), "dft": full.reshape(NC2, 128, 2 * L), "dfs": small}


class Queue:

    def __init__(self, nc, eng, name):
        self.eng, self.sem, self.n, self.name = eng, nc.alloc_semaphore("q_" + name), 0, name
        self.seen = {}

    def __call__(self, ins):
        self.n += 1
        ins.then_inc(self.sem, 1)
        return (self.sem, self.n, self.name)

    def wait(self, *toks):
        for t in toks:
            if t is None:
                continue
            if isinstance(t, list):
                self.wait(*t)
            elif self.seen.get(t[2], 0) < t[1]:
                self.eng.wait_ge(t[0], t[1])
                self.seen[t[2]] = t[1]

    def last(self):
        return (self.sem, self.n, self.name) if self.n else None


class Dma:

    def __init__(self, nc, name):
        self.sem, self.n, self.name = nc.alloc_semaphore("d_" + name), 0, "d_" + name

    def __call__(self, ins):
        ins.then_inc(self.sem, 16)
        self.n += 16
        return (self.sem, self.n, self.name)


class K:
    def __init__(self, nc, a, out):
        self.nc, self.a, self.out = nc, a, out
        self.PE = Queue(nc, nc.tensor, "pe")
        self.V = Queue(nc, nc.vector, "v")
        self.A = Queue(nc, nc.scalar, "a")
        self.G = Queue(nc, nc.gpsimd, "g")
        self.SP = Queue(nc, nc.sync, "sp")
        self.ps = nc.alloc_psum_tensor("ps", [128, 8, 512], F32).ap()
        self.bank = [None] * 8
        self.pr = 0
        self.nsb = 0
        self.stream = []
        self.ring = nc.alloc_sbuf_tensor("ring", [128, NSLOT, SLOT], F32).ap()
        self.rd = [Dma(nc, f"r{i}") for i in range(NSLOT)]
        self.issued = self.taken = 0
        self.arrive = {}
        self.freed = {}

    def sb(self, name, shape, dt=F32):
        return self.nc.alloc_sbuf_tensor(name, shape, dt).ap()

    def mm(self, out, lhsT, rhs, start, stop):
        return self.nc.tensor.matmul(out, lhsT, rhs, start=start, stop=stop, skip_group_check=True)

    def tt(self, q, out, a, b, op, *after):
        q.wait(*after)
        return q(q.eng.tensor_tensor(out, a, b, op))

    def ts(self, q, out, a, s1, s2, op0, op1=None, *after):
        q.wait(*after)
        if op1 is None:
            return q(q.eng.tensor_scalar(out, a, s1, None, op0))
        return q(q.eng.tensor_scalar(out, a, s1, s2, op0, op1))

    def stt(self, q, out, a, s, b, op0, op1, *after):
        q.wait(*after)
        return q(q.eng.scalar_tensor_tensor(out=out, in0=a, scalar=s, in1=b, op0=op0, op1=op1))

    def cp(self, q, out, a, *after):
        q.wait(*after)
        if q is self.A:
            return q(q.eng.copy(out, a))
        return q(q.eng.tensor_copy(out, a))

    def act(self, out, a, func, *after, **kw):
        self.A.wait(*after)
        return self.A(self.nc.scalar.activation(out, a, func, **kw))

    def take(self, *banks):
        for b in banks:
            self.PE.wait(self.bank[b])
            self.bank[b] = None

    def give(self, tok, *banks):
        for b in banks:
            self.bank[b] = tok

    def pair(self, n=3):
        b = 2 * (self.pr % n)
        self.pr += 1
        self.take(b, b + 1)
        return b

    def wide(self, b, lo=0, hi=HF):
        return self.ps[:, b:b + 2, lo:hi]

    def plan(self, src, n):
        self.stream.append((src, n))

    def feed(self):
        while self.issued < len(self.stream) and self.issued < self.taken_done() + NSLOT:
            i = self.issued
            s = i % NSLOT
            src, n = self.stream[i]
            if i >= NSLOT:
                self.SP.wait(self.freed[i - NSLOT])
            self.arrive[i] = self.rd[s](self.nc.sync.dma_start(self.ring[:, s, 0:n], src))
            self.issued += 1

    def taken_done(self):
        n = 0
        while n in self.freed:
            n += 1
        return n

    def weight(self):
        i = self.taken
        self.taken += 1
        self.feed()
        self.PE.wait(self.arrive[i])
        return i, self.ring[:, i % NSLOT, :]

    def release(self, i):
        self.freed[i] = self.PE.last()
        self.feed()

    def sync_all(self):
        toks = [q.last() for q in (self.PE, self.V, self.A, self.G)]
        for q in (self.PE, self.V, self.A, self.G):
            q.wait(*[t for t in toks])


def split(r0, r1):
    return [(r0, r1)] if r1 - r0 <= 512 else [(0, HF), (HF, L)]


def plan_weights(k):
    a = k.a
    for p in range(4):
        k.plan(a["w_att"][p, :, 0:2048], 2048)
        k.plan(a["w_att"][p, :, 2048:3072], 1024)
    for h in range(8):
        k.plan(a["w_hg"][h, :, 0:2048], 2048)
        k.plan(a["w_hg"][h, :, 2048:4096], 2048)
    for m in range(8):
        k.plan(a["w_out1"][m, :, 0:2048], 2048)
        k.plan(a["w_out1"][m, :, 2048:3584], 1536)
    for c in range(4):
        k.plan(a["w_o"][c], 2048)
    for e in range(NE):
        for c in range(4):
            k.plan(a["w_ein"][e, c], 2048)
        for c in range(2):
            k.plan(a["w_eout"][e, c], 2048)
    plan_ffn(k, "1")
    for j in range(4):
        k.plan(a["w_sf"][j, :, 0:2048], 2048)
        k.plan(a["w_sf"][j, :, 2048:4096], 2048)
    for j in range(4):
        k.plan(a["w_dn"][j, :, 0:2048], 2048)
        k.plan(a["w_dn"][j, :, 2048:4096], 2048)
    for m in range(8):
        k.plan(a["w_out2"][m, :, 0:2048], 2048)
        k.plan(a["w_out2"][m, :, 2048:4096], 2048)
        k.plan(a["w_out2"][m, :, 4096:4608], 512)
    for c in range(4):
        k.plan(a["w_o2"][c], 2048)
    plan_ffn(k, "2")


def plan_ffn(k, n):
    for j in range(22):
        k.plan(k.a["w_fi" + n][j], 2048)
    for c in range(4):
        for g in range(3):
            w = 2048 if g < 2 else 1536
            k.plan(k.a["w_fo" + n][c, g, :, 0:w], w)


def linear(k, b, w, rhs, r0, r1, start=True, stop=True):
    n = len(w)
    for t in range(n):
        for j, (c0, c1) in enumerate(split(r0, r1)):
            ins = k.mm(k.ps[:w[t].shape[-1], b + j, 0:c1 - c0], w[t], rhs[t][:, c0:c1],
                       start and t == 0, stop and t == n - 1)
    return k.PE(ins)


def tiles(ap, n):
    return [ap[:, t, :] for t in range(n)]


def rms(k, x, w, out, r0, after, width=8, scale=None):
    n = L - r0
    sq, rb = k.sq, k.rb
    b = k.pair()
    one = k.ones1024 if width == 8 else k.ones128
    for t in range(width):
        a = k.act(sq[:, t % 2, r0:L], x[:, t, r0:L], ACT.Square, after, k.sqfree[t % 2])
        k.PE.wait(a)
        for j, (c0, c1) in enumerate(split(r0, L)):
            ins = k.mm(k.ps[:, b + j, 0:c1 - c0], one, sq[:, t % 2, c0:c1], t == 0, t == width - 1)
        p = k.PE(ins)
        k.sqfree[t % 2] = p
    src = k.wide(b) if n > 512 else k.ps[:, b, 0:n]
    dst = rb[:, 0:n].rearrange("p (a c) -> p a c", a=2) if n > 512 else rb[:, 0:n]
    a = k.act(dst, src, ACT.Sqrt, p, k.rbfree, bias=k.eps[:, 0:1])
    k.give(a, b, b + 1)
    v = k.V
    v.wait(a)
    t0 = v(k.nc.vector.reciprocal(rb[:, 0:n], rb[:, 0:n]))
    for t in range(width):
        last = k.stt(v, out[:, t, r0:L], x[:, t, r0:L], w[t], rb[:, 0:n], MUL, MUL, t0)
    k.rbfree = last
    return last


def attention(k, uT, u_tok, oaT):
    nc, V, A, G, PE = k.nc, k.V, k.A, k.G, k.PE
    with ExitStack() as st:
        def sb(name, shape):
            return st.enter_context(nc.sbuf_tensor(name, shape, F32)).ap()

        fx = sb("fx", [8, 3, L])
        one8 = sb("one8", [8, L])
        qa = sb("qa", [65, 2, 2, S])
        ka = sb("ka", [65, 2, 2, L])
        va = sb("va", [128, 2, 5, 128])
        P = sb("P", [128, 3, L])
        PT = sb("PT", [128, 3, 5, 128])
        sm = sb("sm", [128, 3, 4])
        PE.wait(u_tok, k.ld_wf)
        b = k.pair()
        t = linear(k, b, tiles(k.wf, 8), tiles(uT, 8), 0, L)
        f0, f1, f2 = (fx[:, i, :] for i in range(3))
        v2 = lambda x: x.rearrange("p (a c) -> p a c", a=2)
        t = k.ts(V, v2(f0), k.wide(b)[0:8], k.vec["fb"][0:8, 0:1], None, ADD, None, t, k.ld)
        k.give(t, b, b + 1)
        ta = k.act(f1, f0, ACT.Abs, t)
        ta = k.act(f1, f1, ACT.Exp, ta, scale=-1.0)
        ta = k.act(f1, f1, ACT.Ln, ta, bias=1.0)
        t = k.ts(V, f0, f0, 0.0, None, ALU.min, None, ta)
        t = k.tt(V, f0, f1, f0, SUB, t)
        t1 = V(nc.vector.memset(one8, 1.0))
        V.wait(t, t1)
        tc = V(nc.vector.tensor_tensor_scan(f2, one8, f0, 0.0, MUL, ADD))
        tq = [V(nc.vector.memset(qa[64:65, i], 1.0)) for i in range(2)]
        buf = [None, None]
        kd = [Dma(nc, "ka0"), Dma(nc, "ka1")]
        kfree = [None, None]
        units = []

        def project(p):
            i = p % 2
            c, w = k.weight()
            wv = w.rearrange("p (t c) -> p t c", t=8)
            PE.wait(u_tok)
            b = k.pair()
            t = linear(k, b, [wv[:, x, 0:128] for x in range(8)], tiles(uT, 8), NM, L)
            ts = []
            for j in range(2):
                A.wait(t, kfree[i])
                ts.append(A(nc.scalar.mul(qa[0:64, i, j, :], k.ps[64 * j:64 * j + 64, b, :], 0.125)))
            k.give(ts[-1], b, b + 1)
            b = k.pair()
            t = linear(k, b, [wv[:, x, 128:256] for x in range(8)], tiles(uT, 8), 0, L)
            k.release(c)
            for j in range(2):
                ts.append(k.cp(V, ka[0:64, i, j, :].rearrange("p (a c) -> p a c", a=2),
                               k.wide(b)[64 * j:64 * j + 64], t, kfree[i]))
            k.give(ts[-1], b, b + 1)
            G.wait(tc, kfree[i])
            ts.append(kd[i](nc.gpsimd.dma_start(ka[64:65, i], f2[2 * p:2 * p + 2, :])))
            c, w = k.weight()
            wv = w[:, 0:1024].rearrange("p (t c) -> p t c", t=8)
            b = k.pair()
            for m in range(5):
                n = NM if m == 0 else 128
                o = 0 if m == 0 else NM + 128 * (m - 1)
                dst = k.ps[0:n, b + 1, 0:128] if m == 0 else k.ps[:, b, 128 * (m - 1):128 * m]
                for x in range(8):
                    ins = k.mm(dst, uT[:, x, o:o + n], wv[:, x, :], x == 0, x == 7)
            t = PE(ins)
            k.release(c)
            ts.append(k.cp(A, va[:, i, 1:5, :].rearrange("p a c -> p (a c)"), k.ps[:, b, :], t, kfree[i]))
            ts.append(k.cp(A, va[0:NM, i, 0, :], k.ps[0:NM, b + 1, 0:128], t, kfree[i]))
            k.give(ts[-1], b, b + 1)
            buf[i] = ts

        def scores(p, j, q):
            i = p % 2
            u = len(units) % 3
            na = NM + 128 * q
            nk = na + 128
            b = k.pair()
            PE.wait(buf[i], tq[i])
            lhs = qa[:, i, j, 128 * q:128 * q + 128]
            k.mm(k.ps[:, b, 512 - na:512], lhs, ka[:, i, j, 0:na], True, True)
            k.mm(k.ps[:, b + 1, 0:128], lhs, ka[:, i, j, na:nk], True, False)
            t = PE(k.mm(k.ps[:, b + 1, 0:128], k.ident, k.con["tri"], False, True))
            src = k.ps[:, b:b + 2, :].rearrange("p a c -> p (a c)")[:, 512 - na:640]
            V.wait(t, units[-3][4] if len(units) >= 3 else None)
            t = V(nc.vector.tensor_reduce(sm[:, u, 0:1], src, AX, MAX, negate=True))
            t = k.act(P[:, u, 0:nk], src, ACT.Exp, t, bias=sm[:, u, 0:1], accum_out=sm[:, u, 1:2])
            k.give(t, b, b + 1)
            V.wait(t)
            t = V(nc.vector.reciprocal(sm[:, u, 2:3], sm[:, u, 1:2]))
            t = k.ts(V, P[:, u, 0:nk], P[:, u, 0:nk], sm[:, u, 2:3], None, MUL, None, t)
            units.append([p, j, q, t, None, u])

        def turn(n):
            p, j, q, t, _, u = units[n]
            PE.wait(t)
            b = k.pair()
            for m in range(q + 1):
                k.tr(k.ps[:, b, 128 * m:128 * m + 128], P[:, u, NM + 128 * m:NM + 128 * m + 128])
            t = PE(k.tr(k.ps[0:NM, b + 1, 0:128], P[:, u, 0:NM]))
            free = units[n - 3][4] if n >= 3 else None
            t1 = k.cp(V, PT[:, u, 1:q + 2, :].rearrange("p a c -> p (a c)"), k.ps[:, b, 0:128 * (q + 1)], t, free)
            t2 = k.cp(A, PT[0:NM, u, 0, :], k.ps[0:NM, b + 1, 0:128], t, free)
            k.give([t1, t2], b, b + 1)
            units[n][3] = [t1, t2]

        def values(n):
            p, j, q, t, _, u = units[n]
            i = p % 2
            PE.wait(t, buf[i])
            if j == 0 and q == 0:
                k.take(6)
            dst = k.ps[64 * j:64 * j + 64, 6, 128 * q:128 * q + 128]
            k.mm(dst, va[0:NM, i, 0, 64 * j:64 * j + 64], PT[0:NM, u, 0, :], True, False)
            for m in range(q + 1):
                ins = k.mm(dst, va[:, i, m + 1, 64 * j:64 * j + 64], PT[:, u, m + 1, :], False, m == q)
            t = PE(ins)
            units[n][4] = t
            if j == 1 and q == 3:
                kfree[i] = t
                t = k.cp(A, oaT[:, p, :], k.ps[:, 6, :], t)
                k.give(t, 6)
            return t

        project(0)
        todo = [(p, j, q) for p in range(4) for j in range(2) for q in range(4)]
        for n in range(len(todo) + 2):
            if n < len(todo):
                if n % 8 == 3 and todo[n][0] < 3:
                    project(todo[n][0] + 1)
                scores(*todo[n])
            if 1 <= n <= len(todo):
                turn(n - 1)
            if n >= 2:
                last = values(n - 2)
        k.sync_all()
    return last


def hgrn(k, uT, u_tok, oh):
    nc, V, A, G, PE = k.nc, k.V, k.A, k.G, k.PE
    with ExitStack() as st:
        def sb(name, shape):
            return st.enter_context(nc.sbuf_tensor(name, shape, F32)).ap()

        q_ = sb("hq", [128, 2, S])
        g_ = sb("hg", [128, 3, S])
        fs = sb("hfs", [128, L])
        kk = sb("hk", [128, 2, L])
        lf = sb("hlf", [128, L])
        bb = sb("hb", [128, 2, L])
        vv = sb("hv", [128, 3, 5, 128])
        E = sb("hE", [128, 2, L])
        qe = sb("hqe", [128, 2, S])
        kd = sb("hkd", [128, 2, L])
        kdt = sb("hkdt", [128, 2, 5, 128])
        dd = sb("hdd", [128, 2, S])
        Kl = sb("hKl", [128, 7, S])
        Ql = sb("hQl", [128, 7, 256])
        sc = sb("hsc", [128, 2, S])
        St = sb("hS", [128, 2, 128])
        oo = sb("ho", [128, 2, S])
        lbv = sb("lbv", [128, 3, 8])
        omv = sb("omv", [128, 8])
        l0, l1 = k.vec["lb"][:, 0:8], k.vec["lb"][:, 8:16]
        m, x0, x1 = lbv[:, 0, :], lbv[:, 1, :], lbv[:, 2, :]
        t = k.tt(V, m, l0, l1, MAX, k.ld)
        ta = k.tt(V, x0, l0, m, SUB, t)
        tb = k.tt(V, x1, l1, m, SUB, t)
        ta = k.act(x0, x0, ACT.Exp, ta)
        tb = k.act(x1, x1, ACT.Exp, tb)
        t = k.tt(V, x1, x0, x1, ADD, ta, tb)
        V.wait(t)
        t = V(nc.vector.reciprocal(x1, x1))
        t = k.tt(V, x0, x0, x1, MUL, t)
        lb = x0
        t_lb = k.ts(V, omv, lb, -1.0, 1.0, MUL, ADD, t)
        t_z = V(nc.vector.memset(Kl, 0.0))
        t_zs = V(nc.vector.memset(sc, 0.0))
        H = [dict() for _ in range(8)]

        def project(h):
            s = H[h]
            i, i3 = h % 2, h % 3
            old = H[h - 2] if h >= 2 else {}
            old3 = H[h - 3] if h >= 3 else {}
            c, w = k.weight()
            wv = w.rearrange("p (t c) -> p t c", t=8)
            PE.wait(u_tok)
            b = k.pair()
            t = linear(k, b, [wv[:, x, 0:128] for x in range(8)], tiles(uT, 8), NM, L)
            A.wait(t, old.get("lvl"), old.get("qe"), old.get("diag"))
            s["q"] = A(nc.scalar.mul(q_[:, i, :], k.ps[:, b, :], 128.0 ** -0.5))
            k.give(s["q"], b, b + 1)
            b = k.pair()
            t = linear(k, b, [wv[:, x, 128:256] for x in range(8)], tiles(uT, 8), 0, L)
            k.release(c)
            fs2 = fs.rearrange("p (a c) -> p a c", a=2)
            t = k.act(fs2, k.wide(b), ACT.Sigmoid, t, H[h - 1].get("k") if h else None)
            k.give(t, b, b + 1)
            t = k.ts(V, fs, fs, omv[:, h:h + 1], lb[:, h:h + 1], MUL, ADD, t, t_lb)
            tl = k.act(lf, fs, ACT.Ln, t, H[h - 1].get("b") if h else None)
            s["k"] = k.ts(V, kk[:, i, :], fs, -1.0, 1.0, MUL, ADD, t, old.get("diag"), old.get("kd"))
            V.wait(tl, old.get("lvl"))
            s["b"] = V(nc.vector.tensor_tensor_scan(bb[:, i, :], k.con["rst"], lf, 0.0, MUL, ADD))
            c, w = k.weight()
            wv = w.rearrange("p (t c) -> p t c", t=8)
            b = k.pair()
            for m in range(5):
                n = NM if m == 0 else 128
                o = 0 if m == 0 else NM + 128 * (m - 1)
                dst = k.ps[0:n, b + 1, 0:128] if m == 0 else k.ps[:, b, 128 * (m - 1):128 * m]
                for x in range(8):
                    ins = k.mm(dst, uT[:, x, o:o + n], wv[:, x, 0:128], x == 0, x == 7)
            t = PE(ins)
            ta = k.cp(A, vv[:, i3, 1:5, :].rearrange("p a c -> p (a c)"), k.ps[:, b, :], t, old3.get("o"))
            ta = k.cp(A, vv[0:NM, i3, 0, :], k.ps[0:NM, b + 1, 0:128], t)
            k.give(ta, b, b + 1)
            s["v"] = ta
            b = k.pair()
            t = linear(k, b, [wv[:, x, 128:256] for x in range(8)], tiles(uT, 8), NM, L)
            k.release(c)
            s["g"] = k.act(g_[:, i3, :], k.ps[:, b, :], ACT.Sigmoid, t, old3.get("fin"))
            k.give(s["g"], b, b + 1)

        def prepare(h):
            s = H[h]
            i = h % 2
            old = H[h - 2] if h >= 2 else {}
            s["E"] = k.act(E[:, i, :], bb[:, i, :], ACT.Exp, s["b"], old.get("S"))
            s["qe"] = k.tt(V, qe[:, i, :], q_[:, i, :], E[:, i, NM:L], MUL, s["E"], s["q"], old.get("o"))
            last = bb[:, i, NM:L].rearrange("p (c x) -> p c x", c=4)
            e = last[:, :, 127:128].to_broadcast([128, 4, 128])
            t1 = k.tt(V, kd[:, i, NM:L].rearrange("p (c x) -> p c x", c=4), e, last, SUB, s["b"], old.get("kt"))
            t2 = k.tt(V, kd[:, i, 0:NM], bb[:, i, NM - 1:NM].to_broadcast([128, NM]), bb[:, i, 0:NM], SUB, s["b"])
            t = k.act(kd[:, i, :], kd[:, i, :], ACT.Exp, t1, t2)
            s["kd"] = k.tt(V, kd[:, i, :], kd[:, i, :], kk[:, i, :], MUL, t, s["k"])
            dfree = H[h - 1].get("dfree", [None, None]) if h else [None, None]
            s["L"] = []
            prevmm = H[h - 1].get("mml") if h else None
            for n in range(7):
                hs = 64 >> n
                nb = S // (2 * hs)
                B = bb[:, i, NM:L].rearrange("p (n x) -> p n x", n=nb)
                ref = B[:, :, hs - 1:hs].to_broadcast([128, nb, hs])
                d = dd[:, n % 2, :]
                d3 = d.rearrange("p (n x) -> p n x", n=nb)
                t1 = k.tt(V, d3[:, :, 0:hs], ref, B[:, :, 0:hs], SUB, s["b"], dfree[n % 2])
                t2 = k.tt(V, d3[:, :, hs:2 * hs], B[:, :, hs:2 * hs], ref, SUB)
                t = k.act(d, d, ACT.Exp, t1, t2)
                K3 = kk[:, i, NM:L].rearrange("p (n x) -> p n x", n=nb)
                Q3 = q_[:, i, :].rearrange("p (n x) -> p n x", n=nb)
                ta = k.tt(V, Kl[:, n, :].rearrange("p (n x) -> p n x", n=nb)[:, :, 0:hs], d3[:, :, 0:hs],
                          K3[:, :, 0:hs], MUL, t, t_z, prevmm, s["k"])
                tb = k.tt(V, Ql[:, n, :].rearrange("p (n x) -> p n x", n=nb), d3[:, :, hs:2 * hs],
                          Q3[:, :, hs:2 * hs], MUL, t, s["q"])
                dfree[n % 2] = tb
                s["L"].append([ta, tb])
            s["dfree"] = dfree
            s["lvl"] = tb

        def level(h):
            s = H[h]
            i = h % 2
            old = H[h - 2] if h >= 2 else {}
            tok = [old.get("o"), t_zs]
            for n in range(7):
                hs = 64 >> n
                if n % 2 == 0:
                    b = k.pair()
                bk = b + n % 2
                PE.wait(s["L"][n])
                for c in range(4):
                    ins = k.mm(k.ps[:, bk, 64 * c:64 * c + 64], Kl[:, n, 128 * c:128 * c + 128],
                               Ql[:, n, 64 * c:64 * c + 64], True, True)
                t = PE(ins)
                s["mml"] = t
                nb = 64 // hs
                V.wait(t, tok)
                dst = sc[:, i, :].rearrange("p (c n x) -> p c n x", c=4, n=nb)[:, :, :, hs:2 * hs]
                src = k.ps[:, bk, 0:256].rearrange("p (c n x) -> p c n x", c=4, n=nb)
                for c in range(4):
                    mask = k.con["lv"][:, 64 * n:64 * n + 64].rearrange("p (n x) -> p n x", n=nb).bitcast(I32)
                    tw = V(nc.vector.copy_predicated(dst[:, c], mask, src[:, c]))
                tok = tw
                if n % 2 == 1 or n == 6:
                    k.give(tw, b, b + 1)
            b = k.pair()
            PE.wait(s["q"], s["k"])
            for c in range(4):
                ins = k.mm(k.ps[:, b, 128 * c:128 * c + 128], kk[:, i, NM + 128 * c:NM + 128 * c + 128],
                           q_[:, i, 128 * c:128 * c + 128], True, True)
            t = PE(ins)
            s["diag"] = t
            V.wait(t, tok)
            for c in range(4):
                tw = V(nc.vector.copy_predicated(sc[:, i, 128 * c:128 * c + 128], k.ident.bitcast(I32),
                                                 k.ps[:, b, 128 * c:128 * c + 128]))
            k.give(tw, b, b + 1)
            s["sc"] = tw
            b = k.pair()
            PE.wait(s["kd"])
            for c in range(4):
                k.tr(k.ps[:, b, 128 * c:128 * c + 128], kd[:, i, NM + 128 * c:NM + 128 * c + 128])
            t = PE(k.tr(k.ps[0:NM, b + 1, 0:128], kd[:, i, 0:NM]))
            s["kt"] = t
            ta = k.cp(A, kdt[:, i, 1:5, :].rearrange("p a c -> p (a c)"), k.ps[:, b, :], t, old.get("S"))
            ta = k.cp(A, kdt[0:NM, i, 0, :], k.ps[0:NM, b + 1, 0:128], t)
            k.give(ta, b, b + 1)
            s["kdt"] = ta

        def output(h):
            s = H[h]
            i, i3 = h % 2, h % 3
            old = H[h - 2] if h >= 2 else {}
            k.take(6, 7)
            PE.wait(s["kdt"], s["v"])
            k.mm(k.ps[:, 7, 0:128], kdt[0:NM, i, 0, :], vv[0:NM, i3, 0, :], True, True)
            for c in range(3):
                o = 128 * (c + 1)
                t = PE(k.mm(k.ps[:, 7, o:o + 128], kdt[:, i, c + 1, :], vv[:, i3, c + 1, :], True, True))
            tS = k.cp(V, St[:, i, :], k.ps[:, 7, 0:128], t, old.get("o"))
            PE.wait(s["qe"], s["sc"])
            for c in range(4):
                dst = k.ps[:, 6, 128 * c:128 * c + 128]
                k.mm(dst, vv[:, i3, c + 1, :], sc[:, i, 128 * c:128 * c + 128], True, False)
                PE.wait(tS)
                s["o"] = PE(k.mm(dst, St[:, i, :], qe[:, i, 128 * c:128 * c + 128], False, True))
                if c < 3:
                    o = 128 * (c + 1)
                    e = E[:, i, NM + 128 * c + 127:NM + 128 * c + 128]
                    tS = k.stt(V, St[:, i, :], St[:, i, :], e, k.ps[:, 7, o:o + 128], MUL, ADD, t, s["o"])
            s["S"] = tS
            k.give(tS, 7)
            to = k.cp(V, oo[:, i, :], k.ps[:, 6, :], s["o"], old.get("fin"))
            k.give(to, 6)
            ta = k.act(k.sq[:, 0, 0:S], oo[:, i, :], ACT.Square, to, k.sqfree[0])
            PE.wait(ta)
            b = k.pair()
            t = PE(k.mm(k.ps[:, b, :], k.ones128, k.sq[:, 0, 0:S], True, True))
            k.sqfree[0] = t
            ta = k.act(k.rb[:, 0:S], k.ps[:, b, :], ACT.Sqrt, t, k.rbfree, bias=k.eps[:, 0:1])
            k.give(ta, b, b + 1)
            V.wait(ta)
            t = V(nc.vector.reciprocal(k.rb[:, 0:S], k.rb[:, 0:S]))
            t = k.stt(V, k.rb[:, 0:S], k.rb[:, 0:S], k.vec["hn"], g_[:, i3, :], MUL, MUL, t, s["g"])
            s["fin"] = k.tt(V, oh[:, h, :], oo[:, i, :], k.rb[:, 0:S], MUL, t)
            k.rbfree = s["fin"]

        for h in range(10):
            if h < 8:
                project(h)
            if 1 <= h < 9:
                level(h - 1)
            if h >= 2:
                output(h - 2)
            if h < 8:
                prepare(h)
        k.sync_all()


def mix_out(k, uT, oaT, oh, hT, mix, gt):
    nc, V, A, PE = k.nc, k.V, k.A, k.PE
    free = [None, None]
    mt = []
    for m in range(8):
        i = m % 2
        c, w = k.weight()
        wv = w.rearrange("p (t c) -> p t c", t=8)
        b = k.pair()
        t = linear(k, b, [wv[:, x, 0:128] for x in range(8)], tiles(uT, 8), NM, L)
        ta = k.act(gt[:, i, 0, :], k.ps[:, b, :], ACT.Sigmoid, t, free[i])
        k.give(ta, b, b + 1)
        b = k.pair()
        t = linear(k, b, [wv[:, x, 128:256] for x in range(8)], tiles(uT, 8), NM, L)
        tb = k.act(gt[:, i, 1, :], k.ps[:, b, :], ACT.Sigmoid, t)
        k.give(tb, b, b + 1)
        k.release(c)
        c, w = k.weight()
        wa = w[:, 0:512].rearrange("p (t c) -> p t c", t=4)
        wh = w[:, 512:1536].rearrange("p (t c) -> p t c", t=8)
        b = k.pair()
        t = linear(k, b, tiles(wa, 4), tiles(oaT, 4), 0, S)
        ta = k.tt(V, gt[:, i, 0, :], k.ps[:, b, :], gt[:, i, 0, :], MUL, t, ta)
        k.give(ta, b, b + 1)
        b = k.pair()
        t = linear(k, b, tiles(wh, 8), tiles(oh, 8), 0, S)
        tb = k.tt(V, gt[:, i, 1, :], k.ps[:, b, :], gt[:, i, 1, :], MUL, t, tb)
        k.give(tb, b, b + 1)
        k.release(c)
        free[i] = k.tt(V, mix[:, m, :], gt[:, i, 0, :], gt[:, i, 1, :], ADD, ta, tb)
    PE.wait(free[0], free[1])
    for m in range(8):
        if m % 2 == 0:
            c, w = k.weight()
            wv = w.rearrange("p (t c) -> p t c", t=8)
        b = k.pair()
        o = 128 * (m % 2)
        t = linear(k, b, [wv[:, x, o:o + 128] for x in range(8)], tiles(mix, 8), 0, S)
        if m % 2:
            k.release(c)
        t = k.tt(V, hT[:, m, NM:L], hT[:, m, NM:L], k.ps[:, b, :], ADD, t)
        k.give(t, b, b + 1)
    return t


def setup(k):
    nc = k.nc
    k.ident = None
    con = k.sb("con", [128, NCON])
    vec = k.sb("vec", [128, NVEC])
    k.wf = k.sb("wf", [128, 8, 8])
    k.wba = k.sb("wba", [128, 8, 16])
    k.wr = k.sb("wr", [128, 8, 36])
    k.hT = k.sb("hT", [128, 8, L])
    k.uT = k.sb("uT", [128, 8, L])
    k.sq = k.sb("sq", [128, 2, L])
    k.rb = k.sb("rb", [128, L])
    k.ones1024 = k.sb("o1024", [128, 128])
    k.ones128 = k.sb("o128", [128, 128])
    k.ones = k.sb("o1", [128, 128])
    k.eps = k.sb("eps", [128, 1])
    k.sqfree = [None, None]
    k.rbfree = None
    k.con = {n: con[:, o:o + w] for n, o, w in
             ((n, CON[n], w) for n, w in (("id", 128), ("u", 128), ("ui", 128), ("li", 128), ("tri", 128),
                                          ("mf", 128), ("mb", 128), ("lv", 448), ("rst", L), ("io", 64),
                                          ("tok", 4)))}
    k.vec = {n: vec[:, VEC[n]:VEC[n] + w] for n, w in
             (("mix", 8), ("lb", 16), ("hn", 1), ("ffn", 8), ("fin", 8), ("g", 48), ("sc", 12), ("dc", 36),
              ("dn", 1), ("fb", 1), ("al", 8), ("dt", 8), ("rb", 36))}
    k.ident = k.con["id"]
    k.tr = lambda out, in_: nc.tensor.transpose(out, in_, k.ident[:in_.shape[0], :in_.shape[0]])
    d = [Dma(nc, f"ld{i}") for i in range(6)]
    a = k.a
    t1 = d[0](nc.scalar.dma_start(k.hT, a["hT"]))
    t2 = d[1](nc.scalar.dma_start(vec, a["vec"]))
    t3 = d[2](nc.scalar.dma_start(con, a["con"]))
    t4 = d[3](nc.scalar.dma_start(k.wf, a["w_f"]))
    t5 = d[4](nc.scalar.dma_start(k.wba, a["w_ba"]))
    t6 = d[5](nc.scalar.dma_start(k.wr, a["w_r"]))
    k.ld_h, k.ld, k.ld_wf, k.ld_wr, k.ld_wba = t1, [t2, t3], t4, t6, t5
    V = k.V
    toks = [V(nc.vector.memset(k.ones1024, 1.0 / 1024)), V(nc.vector.memset(k.ones128, 1.0 / 128)),
            V(nc.vector.memset(k.ones, 1.0)), V(nc.vector.memset(k.eps, EPS))]
    for q in (k.PE, k.V, k.A, k.G):
        q.wait(toks, k.ld)
    k.ys = nc.dram_tensor("ys", [NBLK * CAP, D], F32, kind="Internal").ap()
    zero = k.sb("zero", [128, 256])
    z = V(nc.vector.memset(zero, 0.0))
    k.A.wait(z)
    k.ysz = []
    for j in range(NOV * CAP // 128):
        dz = Dma(nc, f"ysz{j}")
        r = NE * CAP + 128 * j
        k.ysz.append(dz(nc.scalar.dma_start(k.ys[r:r + 128, :].rearrange("p (a c) -> p a c", c=256),
                                            zero.unsqueeze(1).to_broadcast([128, 4, 256]))))
    plan_weights(k)
    k.feed()


def block1(k):
    t = rms(k, k.hT, [k.vec["mix"][:, i:i + 1] for i in range(8)], k.uT, 0, k.ld_h)
    with ExitStack() as st:
        oaT = st.enter_context(k.nc.sbuf_tensor("oaT", [128, 4, S], F32)).ap()
        attention(k, k.uT, t, oaT)
        oh = st.enter_context(k.nc.sbuf_tensor("oh", [128, 8, S], F32)).ap()
        hgrn(k, k.uT, t, oh)
        mix = st.enter_context(k.nc.sbuf_tensor("mix", [128, 8, S], F32)).ap()
        gt = st.enter_context(k.nc.sbuf_tensor("gt", [128, 2, 2, S], F32)).ap()
        mix_out(k, k.uT, oaT, oh, k.hT, mix, gt)
        k.sync_all()


def ktiles(w):
    return w.reshape(w.shape[0] // 128, 128, w.shape[1]).transpose(1, 0, 2)


def side(*parts):
    a = np.concatenate(parts, axis=2)
    return a.reshape(128, -1)


def layout(i):
    A = np.asarray
    i = {n: A(v) for n, v in i.items()}
    o = {}
    o["hT"] = np.concatenate([i["meta_tokens"], i["x"][0]], 0).T.reshape(8, 128, L).transpose(1, 0, 2)
    o["m2T"] = i["meta_tokens_2"].T.reshape(8, 128, NM).transpose(1, 0, 2)
    col = lambda v: v.reshape(-1, 128).T
    vec = np.zeros((128, NVEC), np.float32)

    def put(n, a):
        vec[:a.shape[0], VEC[n]:VEC[n] + a.shape[1]] = a

    put("mix", col(i["norm_mix_w"][0]))
    put("lb", np.concatenate([col(i["hgrn_lb_logits"][0]), col(i["hgrn_lb_logits"][1])], 1))
    put("hn", col(i["hgrn_norm_w"][0]))
    put("ffn", col(i["norm_ffn_w"][0]))
    put("fin", col(i["norm_final_w"]))
    put("g", np.concatenate([col(i["norm_gains_2"][0, j]) for j in range(6)], 1))
    put("sc", np.concatenate([col(i["sconv_w_2"][0, j]) for j in range(3)], 1))
    put("dc", np.concatenate([col(i["dn_conv_w_2"][0, j]) for j in range(3)], 1))
    put("dn", col(i["dn_norm_2"][0]))
    put("fb", i["attn_forget_b"][0][:, None])
    put("al", np.broadcast_to(i["dn_A_log_2"][0].reshape(1, 8), (128, 8)))
    put("dt", np.broadcast_to(i["dn_dt_bias_2"][0].reshape(1, 8), (128, 8)))
    put("rb", np.broadcast_to(np.concatenate([i["b_router_group"][0], i["b_router_expert"][0]])[None], (128, 36)))
    o["vec"] = vec
    w = ktiles(i["w_in"][0])
    s = np.cumsum([0, 512, 512, 512, 8, 1024, 1024, 1024, 1024, 1024, 1024])
    at = lambda j, t: w[:, :, s[j] + 128 * t:s[j] + 128 * t + 128]
    o["w_att"] = np.stack([np.concatenate([side(at(0, p), at(1, p)), side(at(2, p))], 1) for p in range(4)])
    o["w_f"] = w[:, :, s[3]:s[4]]
    o["w_hg"] = np.stack([np.concatenate([side(at(4, h), at(5, h)), side(at(6, h), at(7, h))], 1) for h in range(8)])
    wa, wh = ktiles(i["w_attn_out"][0]), ktiles(i["w_hgrn_out"][0])
    t = lambda x, m: x[:, :, 128 * m:128 * m + 128]
    o["w_out1"] = np.stack([np.concatenate([side(at(8, m), at(9, m)), side(t(wa, m)), side(t(wh, m))], 1)
                            for m in range(8)])
    halves = lambda x, n, c: np.stack([side(x[:, :, c * j:c * j + c]) for j in range(n)])
    o["w_o"] = halves(ktiles(i["w_o"][0]), 4, 256)
    o["w_r"] = np.concatenate([ktiles(i["w_router_group"][0]), ktiles(i["w_router_expert"][0])], 2)
    e = i["w_expert_in"][0]
    o["w_ein"] = e.reshape(NE, 8, 128, 4, 256).transpose(0, 3, 2, 1, 4).reshape(NE, 4, 128, 2048)
    e = i["w_expert_out"][0]
    o["w_eout"] = e.reshape(NE, 4, 128, 2, 512).transpose(0, 3, 2, 1, 4).reshape(NE, 2, 128, 2048)
    for n in "12":
        wi = ktiles(i[f"ffn{n}_wi_2"][0])
        o["w_fi" + n] = np.stack([side(t(wi, j), t(wi, 22 + j)) for j in range(22)])
        wo = ktiles(i[f"ffn{n}_wo_2"][0])
        f = np.zeros((4, 3, 128, 2048), np.float32)
        for c in range(4):
            for g in range(3):
                x = side(wo[:, 8 * g:8 * g + 8, 256 * c:256 * c + 256])
                f[c, g, :, :x.shape[1]] = x
        o["w_fo" + n] = f
    w = ktiles(i["w_in_2"][0])
    s2 = {"f": 0, "b": 512, "c": 1024, "h": 1536, "q": 2048, "k": 2560, "v": 3072, "z": 3584,
          "gf": 4112, "gs": 5136, "gd": 6160}
    at = lambda j, m: w[:, :, s2[j] + 128 * m:s2[j] + 128 * m + 128]
    o["w_ba"] = w[:, :, 4096:4112]
    o["w_sf"] = np.stack([np.concatenate([side(at("b", j), at("c", j)), side(at("h", j), at("f", j))], 1)
                          for j in range(4)])
    o["w_dn"] = np.stack([np.concatenate([side(at("q", j), at("k", j)), side(at("v", j), at("z", j))], 1)
                          for j in range(4)])
    f, c, d = (ktiles(i[n][0]) for n in ("w_fourier_2", "w_sconv_out_2", "w_dn_out_2"))
    o["w_out2"] = np.stack([np.concatenate([side(at("gf", m), at("gs", m)), side(at("gd", m)), side(t(f, m)),
                                            side(t(c, m)), side(t(d, m))], 1) for m in range(8)])
    o["w_o2"] = halves(ktiles(i["w_out_2"][0]), 4, 256)
    o.update(constants())
    return {n: np.ascontiguousarray(v) for n, v in o.items()}


def route(k, sb, uT, tv):
    nc, V, A, G, PE = k.nc, k.V, k.A, k.G, k.PE
    lg = sb("lg", [128, 4, 36])
    oh = sb("roh", [128, 2, 4, 32])
    ee = sb("ree", [128, 4, 32])
    e2 = sb("re2", [128, 4, 32])
    g4 = sb("rg4", [128, 3, 16])
    s = sb("rs", [128, 16, 8])
    nb = sb("rnb", [128, 3, 32])
    io = sb("rio", [128, 2, 64])
    gate = sb("gate", [128, 2, 4])
    dst = sb("dst", [128, 2, 4], U32)
    R = sb("rR", [128, 8, 64])
    B = sb("rB", [128, 8, NBLK])
    idx = sb("idx", [64, NBLK], U32)
    ov = sb("ov", [1, 1 + NOV], I32)
    cmp_ = sb("rcmp", [1, NOV, 32])
    ovf = sb("rovf", [1, NOV])

    def red(out, in_, op, *after):
        V.wait(*after)
        return V(nc.vector.tensor_reduce(out, in_, AX, op))

    def first(out, eq, w, m, t):
        t = k.tt(V, eq, eq, w, MUL, t)
        t = red(m, eq, MAX, t)
        return k.tt(V, out, eq, m.unsqueeze(2).to_broadcast(list(eq.shape)), ALU.is_equal, t)

    PE.wait(tv, k.ld_wr)
    b = k.pair()
    for i in range(4):
        for x in range(8):
            ins = k.mm(k.ps[:, b, 36 * i:36 * i + 36], uT[:, x, NM + 128 * i:NM + 128 * i + 128],
                       k.wr[:, x, :], x == 0, x == 7)
    t = PE(ins)
    t = k.tt(V, lg, k.ps[:, b, 0:144].rearrange("p (a c) -> p a c", a=4),
             k.vec["rb"].unsqueeze(1).to_broadcast([128, 4, 36]), ADD, t)
    k.give(t, b, b + 1)
    down, iota = io[:, 0, :], k.con["io"]
    tw = k.ts(V, down, iota, -1.0, 64.0, MUL, ADD)
    gl = lg[:, :, 0:4]
    gm, gsum, pg, m = (s[:, j, 0:4] for j in range(4))
    up = lambda x, n: x.unsqueeze(2).to_broadcast([128, 4, n])
    row = lambda x, n: x[:, 0:n].unsqueeze(1).to_broadcast([128, 4, n])
    g1, gx, gd = (g4[:, j, :].rearrange("p (a c) -> p a c", a=4) for j in range(3))
    t = red(gm, gl, MAX, t, tw)
    t1 = k.tt(V, gd, gl, up(gm, 4), SUB, t)
    t2 = k.act(gd, gd, ACT.Exp, t1)
    t = k.tt(V, gx, gl, up(gm, 4), ALU.is_equal, t)
    t = first(g1, gx, row(down, 4), m, t)
    ts_ = red(gsum, gd, ADD, t2)
    V.wait(ts_)
    tp = V(nc.vector.reciprocal(pg, gsum))
    t = k.ts(V, gx, g1, -1.0, BIG, ADD, MUL, t)
    for i in range(4):
        t0 = k.tt(V, ee[:, i, :].rearrange("p (g e) -> p g e", g=4),
                  lg[:, i, 4:36].rearrange("p (g e) -> p g e", g=4),
                  gx[:, i, :].unsqueeze(2).to_broadcast([128, 4, 8]), ADD, t)
    t = t0
    v1, v2 = s[:, 4, 0:4], s[:, 5, 0:4]
    t = red(v1, ee, MAX, t)
    t = k.tt(V, e2, ee, up(v1, 32), ALU.is_equal, t)
    t = first(oh[:, 0], e2, row(down, 32), m, t)
    t = k.stt(V, ee, oh[:, 0], -BIG, ee, MUL, ADD, t)
    t = red(v2, ee, MAX, t)
    t = k.tt(V, e2, ee, up(v2, 32), ALU.is_equal, t)
    t = first(oh[:, 1], e2, row(down, 32), m, t)
    ta = k.tt(V, v2, v2, v1, SUB, t)
    ta = k.act(v2, v2, ACT.Exp, ta)
    ta = k.ts(V, v1, v2, 1.0, None, ADD, None, ta)
    V.wait(ta)
    ta = V(nc.vector.reciprocal(v1, v1))
    ta = k.tt(V, gate[:, 0, :], v1, pg, MUL, ta, tp)
    t_gate = k.tt(V, gate[:, 1, :], v2, gate[:, 0, :], MUL, ta)
    t = k.tt(V, e2, oh[:, 0], oh[:, 1], ADD, t)
    PE.wait(t)
    b = k.pair()
    for i in range(4):
        for j in range(i):
            k.mm(k.ps[:, b, 32 * i:32 * i + 32], k.ones, e2[:, j, :], j == 0, False)
        k.mm(k.ps[:, b, 32 * i:32 * i + 32], k.con["u"], e2[:, i, :], i == 0, True)
    for j in range(4):
        ins = k.mm(k.ps[:, b + 1, 0:32], k.ones, e2[:, j, :], j == 0, j == 3)
    t = PE(ins)
    rank = k.ps[:, b, 0:128].rearrange("p (a e) -> p a e", a=4)
    two = lambda j: s[:, j, :].rearrange("p (k a) -> p k a", k=2)
    rk, eid, obk, q, blk, u1 = (two(j) for j in (6, 7, 8, 9, 10, 11))
    cnt, nob, end = (nb[:, j, :] for j in range(3))
    t1 = k.cp(V, cnt, k.ps[:, b + 1, 0:32], t)
    for c in range(2):
        t = k.tt(V, ee, oh[:, c], rank, MUL, t, t1)
        t = red(rk[:, c, :], ee, ADD, t)
    k.give(t, b, b + 1)
    t = k.ts(V, nob, cnt, 64.0, None, ALU.is_gt, None, t)
    for n in range(2, 8):
        t = k.stt(V, nob, cnt, 64.0 * n, nob, ALU.is_gt, ADD, t)
    V.wait(t)
    t = V(nc.vector.tensor_tensor_scan(end, k.ones[:, 0:32], nob, 0.0, MUL, ADD))
    t = k.tt(V, nob, end, nob, SUB, t)
    for c in range(2):
        t = k.tt(V, ee, oh[:, c], row(nob, 32), MUL, t)
        t = red(obk[:, c, :], ee, ADD, t)
        t = k.tt(V, ee, oh[:, c], row(iota, 32), MUL, t)
        t = red(eid[:, c, :], ee, ADD, t)
    f = lambda j: s[:, j, :]
    t = k.ts(V, f(9), f(6), 64.0, None, ALU.is_ge, None, t)
    for n in range(2, 8):
        t = k.stt(V, f(9), f(6), 64.0 * n, f(9), ALU.is_ge, ADD, t)
    t = k.stt(V, f(6), f(9), -64.0, f(6), MUL, ADD, t)
    t = k.tt(V, f(11), f(9), f(8), ADD, t)
    t = k.stt(V, f(11), f(11), NE - 1.0, f(7), ADD, SUB, t)
    t = k.ts(V, f(10), f(9), 1.0, None, ALU.min, None, t)
    t = k.tt(V, f(10), f(10), f(11), MUL, t)
    t = k.tt(V, f(10), f(10), f(7), ADD, t)
    t_d = k.stt(V, dst.rearrange("p a c -> p (a c)"), f(10), 64.0, f(6), MUL, ADD, t)
    for j in range(8):
        ta = k.ts(V, R[:, j, :], iota, f(6)[:, j:j + 1], None, ALU.is_equal, None, t)
        tb = k.ts(V, B[:, j, :], iota[:, 0:NBLK], f(10)[:, j:j + 1], k.con["tok"][:, j % 4:j % 4 + 1],
                  ALU.is_equal, MUL)
    PE.wait(tb)
    b = k.pair()
    for j in range(8):
        ins = k.mm(k.ps[0:64, b, 0:NBLK], R[:, j, :], B[:, j, :], j == 0, j == 7)
    tp = PE(ins)
    t_i = k.cp(V, idx, k.ps[0:64, b, 0:NBLK], tp)
    k.give(t_i, b, b + 1)
    t = k.tt(V, cmp_, end[0:1].unsqueeze(1).to_broadcast([1, NOV, 32]),
             iota[0:1, 0:NOV].unsqueeze(2).to_broadcast([1, NOV, 32]), ALU.is_le, t)
    t = red(ovf, cmp_, ADD, t)
    t = k.ts(V, ov[:, 1:1 + NOV], ovf, NE - 1.0, None, ALU.min, None, t)
    t_o = k.cp(V, ov[:, 0:1], end[0:1, 31:32], t)
    return gate, dst, idx, ov, [t_gate, t_d, t_i, t_o]


def expert(k, xg, tg, xT, hb, w_in, done):
    nc, V, A, PE = k.nc, k.V, k.A, k.PE
    PE.wait(tg)
    b = k.pair(4)
    for x in range(8):
        ins = k.tr(k.ps[:, b, 64 * x:64 * x + 64], xg[:, 128 * x:128 * x + 128])
    t = PE(ins)
    tx = k.cp(V, xT.rearrange("p a c -> p (a c)"), k.ps[:, b, :], t)
    k.give(tx, b, b + 1)
    b = k.pair(4)
    PE.wait(tx)
    for c in range(4):
        w = w_in(c)
        for m in range(2):
            o = 64 * (2 * (c % 2) + m)
            for x in range(8):
                ins = k.mm(k.ps[:, b + c // 2, o:o + 64], w[:, x, 128 * m:128 * m + 128], xT[:, x, :],
                           x == 0, x == 7)
        t = PE(ins)
        done(c)
        if c == 1:
            ta = k.act(hb[:, 0, :], k.ps[:, b, 0:256], ACT.Silu, t)
    th = k.tt(V, hb[:, 1, :], hb[:, 0, :], k.ps[:, b + 1, 0:256], MUL, t, ta)
    k.give(th, b, b + 1)
    return th


def expert_out(k, hb, yb, th, w_out, yfree, done):
    nc, V, A, PE = k.nc, k.V, k.A, k.PE
    b = k.pair(4)
    PE.wait(th)
    for c in range(2):
        w = w_out(c)
        for x in range(4):
            ins = k.mm(k.ps[0:64, b + c, :], hb[:, 1, 64 * x:64 * x + 64], w[:, x, :], x == 0, x == 3)
        t = PE(ins)
        done(c)
    t1 = k.cp(A, yb[:, 0:512], k.ps[0:64, b, :], t, yfree)
    t2 = k.cp(V, yb[:, 512:1024], k.ps[0:64, b + 1, :], t, yfree)
    k.give([t1, t2], b, b + 1)
    return [t1, t2]


def moe(k):
    nc, V, A, G, PE = k.nc, k.V, k.A, k.G, k.PE
    uT, hT = k.uT, k.hT
    vrow = nc.dram_tensor("vrow", [S, D], F32, kind="Internal").ap()
    ys = k.ys
    with ExitStack() as st:
        def sb(name, shape, dt=F32):
            return st.enter_context(nc.sbuf_tensor(name, shape, dt)).ap()

        tv = rms(k, hT, [k.vec["ffn"][:, i:i + 1] for i in range(8)], uT, NM, k.ld_h)
        vt = sb("vt", [128, 2, D])
        dv = [Dma(nc, "vr0"), Dma(nc, "vr1")]
        tok = [None, None]
        PE.wait(tv)
        for i in range(4):
            b = k.pair()
            for x in range(8):
                ins = k.tr(k.ps[:, b + x // 4, 128 * (x % 4):128 * (x % 4) + 128],
                           uT[:, x, NM + 128 * i:NM + 128 * i + 128])
            t = PE(ins)
            t1 = k.cp(A, vt[:, i % 2, 0:512], k.ps[:, b, :], t, tok[i % 2])
            t2 = k.cp(A, vt[:, i % 2, 512:1024], k.ps[:, b + 1, :], t, tok[i % 2])
            k.give(t2, b, b + 1)
            G.wait(t1, t2, tok[i % 2])
            tok[i % 2] = dv[i % 2](nc.gpsimd.dma_start(vrow[128 * i:128 * i + 128, :], vt[:, i % 2, :]))
        gate, dst, idx, ov, rt = route(k, sb, uT, tv)
        xg = sb("xg", [64, 4, D])
        xT = sb("exT", [128, 3, 8, 64])
        hb = sb("ehb", [128, 3, 2, 256])
        yb = sb("yb", [64, 4, D])
        dg = [Dma(nc, f"xg{i}") for i in range(4)]
        dy = [Dma(nc, f"yb{i}") for i in range(4)]
        G.wait(rt, tok)

        def gather(blk, i, free):
            G.wait(free)
            return dg[i](nc.gpsimd.indirect_dma_start(
                out=xg[:, i, :], out_offset=None, in_=vrow,
                in_offset=bass.IndirectOffsetOnAxis(ap=idx[:, blk:blk + 1], axis=0),
                bounds_check=S - 1, oob_is_err=False))

        tg = [gather(e, e, None) for e in range(3)]
        ths = []
        ty = [None] * 4
        for e in range(NE):
            if e < NE:
                held = []

                def w_in(c):
                    i, w = k.weight()
                    held.append(i)
                    return w.rearrange("p (t c) -> p t c", t=8)

                th = expert(k, xg[:, e % 4, :], tg[e], xT[:, e % 3], hb[:, e % 3], w_in,
                            lambda c: k.release(held[-1]))
                ths.append(th)
                if e + 3 < NE:
                    tg.append(gather(e + 3, (e + 3) % 4, ths[e - 1] if e else None))
            if e < NE:
                def w_out(c):
                    i, w = k.weight()
                    held.append(i)
                    return w.rearrange("p (t c) -> p t c", t=4)

                t = expert_out(k, hb[:, e % 3], yb[:, e % 4, :], ths[e], w_out, ty[e % 4],
                               lambda c: k.release(held[-1]))
                A.wait(t)
                ty[e % 4] = dy[e % 4](nc.scalar.dma_start(ys[CAP * e:CAP * e + CAP, :], yb[:, e % 4, :]))
        k.sync_all()
        G.wait(tg)
        for q in (V, PE, A, G, k.SP):
            q.wait(rt[3], ty, k.ysz)
        overflow(k, idx, ov, vrow, ys, xg[:, 0, :], xT[:, 0], hb[:, 0], yb[:, 0, :])
        with ExitStack() as st2:
            gy = st2.enter_context(nc.sbuf_tensor("gy", [128, 2, 2, D], F32)).ap()
            dc = [[Dma(nc, f"gy{i}{c}") for c in range(2)] for i in range(2)]
            free = [None, None]
            for i in range(4):
                j = i % 2
                tc = []
                for c in range(2):
                    G.wait(free[j])
                    tc.append(dc[j][c](nc.gpsimd.indirect_dma_start(
                        out=gy[:, j, c, :], out_offset=None, in_=ys,
                        in_offset=bass.IndirectOffsetOnAxis(ap=dst[:, c, i:i + 1], axis=0),
                        bounds_check=NBLK * CAP - 1, oob_is_err=False)))
                t = k.ts(V, gy[:, j, 0, :], gy[:, j, 0, :], gate[:, 0, i:i + 1], None, MUL, None, tc[0])
                t = k.stt(V, gy[:, j, 0, :], gy[:, j, 1, :], gate[:, 1, i:i + 1], gy[:, j, 0, :], MUL, ADD, t, tc[1])
                PE.wait(t)
                for g in range(2):
                    b = k.pair()
                    for x in range(4):
                        ins = k.tr(k.ps[:, b, 128 * x:128 * x + 128],
                                   gy[:, j, 0, 512 * g + 128 * x:512 * g + 128 * x + 128])
                    t = PE(ins)
                    h = hT[:, 4 * g:4 * g + 4, NM + 128 * i:NM + 128 * i + 128]
                    th = k.tt(V, h, h, k.ps[:, b, :].rearrange("p (a c) -> p a c", a=4), ADD, t)
                    k.give(th, b, b + 1)
                free[j] = t
            k.sync_all()


def sem_number(sem):
    return sem.num


def overflow(k, idx, ov, vrow, ys, xg, xT, hb, yb):
    nc = k.nc
    with ExitStack() as st:
        wo = st.enter_context(nc.sbuf_tensor("ovw", [128, 4, SLOT], F32)).ap()
        ix = st.enter_context(nc.sbuf_tensor("ovi", [64, 1], U32)).ap()
        before = k.PE, k.V, k.A, k.G, k.SP, k.bank
        k.PE, k.V, k.A, k.G, k.SP = (Queue(nc, e, "o" + n) for e, n in (
            (nc.tensor, "pe"), (nc.vector, "v"), (nc.scalar, "a"), (nc.gpsimd, "g"), (nc.sync, "sp")))
        k.bank = [None] * 8
        d = [Dma(nc, f"ov{i}") for i in range(8)]
        count = nc.values_load(ov[0:1, 0:1], min_val=0, max_val=NOV - 1)
        with nc.Fori(0, NOV) as j:
            with nc.If(j < count):
                e = nc.sync.value_load(ov[0:1, bass.ds(j + 1, 1)], min_val=0, max_val=NE - 1)
                tw = []

                def load(c):
                    src = k.a["w_ein"][bass.ds(e, 1), c] if c < 4 else k.a["w_eout"][bass.ds(e, 1), c - 4]
                    tw.append(d[c](nc.sync.dma_start(wo[:, c % 4, :], src.rearrange("a p m -> (a p) m"))))

                for c in range(4):
                    load(c)
                t = k.cp(k.V, ix, idx[:, bass.ds(j + NE, 1)])
                k.G.wait(t)
                tg = d[6](nc.gpsimd.indirect_dma_start(
                    out=xg, out_offset=None, in_=vrow,
                    in_offset=bass.IndirectOffsetOnAxis(ap=ix, axis=0), bounds_check=S - 1, oob_is_err=False))

                def w_in(c):
                    k.PE.wait(tw[c])
                    return wo[:, c, :].rearrange("p (t c) -> p t c", t=8)

                def w_out(c):
                    k.PE.wait(tw[4 + c])
                    return wo[:, c, :].rearrange("p (t c) -> p t c", t=4)

                def used(c):
                    if c < 2:
                        k.SP.wait(k.PE.last())
                        load(4 + c)

                k.G.wait(tg)
                th = expert(k, xg, tg, xT, hb, w_in, used)
                t = expert_out(k, hb, yb, th, w_out, None, lambda c: None)
                k.SP.wait(t)
                t = d[7](nc.sync.dma_start(ys[bass.ds(j * CAP + NE * CAP, CAP), :], yb))
                k.SP.wait(t)
                nc.all_engine_barrier()
                n = sem_number(d[6].sem)
                nc.gpsimd.dma_reset(range(n, n + 1))
                nc.gpsimd.sem_clear(d[6].sem)
                for q in (k.PE, k.V, k.A, k.G, k.SP):
                    if q.n:
                        nc.sync.sem_clear(q.sem)
                for x in d[:6] + d[7:]:
                    nc.sync.sem_clear(x.sem)
                nc.all_engine_barrier()
        k.PE, k.V, k.A, k.G, k.SP, k.bank = before


def block1_end(k):
    m2 = Dma(k.nc, "m2")
    k.G.wait(k.V.last())
    t2 = m2(k.nc.gpsimd.dma_start(k.hT[:, :, 0:NM], k.a["m2T"]))
    t = rms(k, k.hT, [k.vec["fin"][:, i:i + 1] for i in range(8)], k.hT, NM, k.V.last())
    return [t, t2]


def post(k, y, w, r0, half, after):
    V = k.V
    t = rms(k, y, w, y, r0, after)
    for m in range(8):
        if half:
            t1 = k.stt(V, k.hT[:, m, r0:L], y[:, m, r0:L], 0.5, k.hT[:, m, r0:L], MUL, ADD, t)
        else:
            t1 = k.tt(V, k.hT[:, m, r0:L], k.hT[:, m, r0:L], y[:, m, r0:L], ADD, t)
    return t1


def ffn(k, r0, w0, w1, after):
    nc, V, A, PE = k.nc, k.V, k.A, k.PE
    n = L - r0
    with ExitStack() as st:
        hf = st.enter_context(nc.sbuf_tensor(f"hf{r0}", [128, 22, L], F32)).ap()
        sg = st.enter_context(nc.sbuf_tensor(f"sg{r0}", [128, 2, L], F32)).ap()
        y = st.enter_context(nc.sbuf_tensor(f"yf{r0}", [128, 8, L], F32)).ap()
        tu = rms(k, k.hT, w0, k.uT, r0, after)
        PE.wait(tu)
        two = (lambda x: x.rearrange("p (a c) -> p a c", a=2)) if n > 512 else (lambda x: x)
        acc = (lambda b: k.wide(b)) if n > 512 else (lambda b: k.ps[:, b, 0:n])
        free = [None, None]
        for j in range(22):
            c, w = k.weight()
            wv = w.rearrange("p (t c) -> p t c", t=8)
            b = k.pair(4)
            t = linear(k, b, [wv[:, x, 0:128] for x in range(8)], tiles(k.uT, 8), r0, L)
            ts = k.act(two(sg[:, j % 2, r0:L]), acc(b), ACT.Silu, t, free[j % 2])
            k.give(ts, b, b + 1)
            b = k.pair(4)
            t = linear(k, b, [wv[:, x, 128:256] for x in range(8)], tiles(k.uT, 8), r0, L)
            k.release(c)
            tv = k.tt(V, two(hf[:, j, r0:L]), acc(b), two(sg[:, j % 2, r0:L]), MUL, t, ts)
            k.give(tv, b, b + 1)
            free[j % 2] = tv
        PE.wait(tv)
        for c in range(4):
            b0, b1 = k.pair(4), k.pair(4)
            for g in range(3):
                i, w = k.weight()
                nt = 8 if g < 2 else 6
                wv = w[:, 0:256 * nt].rearrange("p (t c) -> p t c", t=nt)
                for m, b in enumerate((b0, b1)):
                    t = linear(k, b, [wv[:, x, 128 * m:128 * m + 128] for x in range(nt)],
                               [hf[:, 8 * g + x, :] for x in range(nt)], r0, L, g == 0, g == 2)
                    if g == 2:
                        ty = k.cp(A if m else V, two(y[:, 2 * c + m, r0:L]), acc(b), t)
                        k.give(ty, b, b + 1)
                k.release(i)
        t = post(k, y, w1, r0, True, [V.last(), A.last()])
        k.sync_all()
    return t


def conv(k, out, xb, w, tx, free):
    V = k.V
    t = k.ts(V, out, xb[:, 0:L], w[0], None, MUL, None, tx, free)
    t = k.stt(V, out, xb[:, 1:L + 1], w[1], out, MUL, ADD, t)
    return k.stt(V, out, xb[:, 2:L + 2], w[2], out, MUL, ADD, t)


def conv_fourier(k, sc, fo, tu):
    nc, V, A, G, PE = k.nc, k.V, k.A, k.G, k.PE
    uT = k.uT
    two = lambda x: x.rearrange("p (a c) -> p a c", a=2)
    with ExitStack() as st:
        def sb(name, shape):
            return st.enter_context(nc.sbuf_tensor(name, shape, F32)).ap()

        xb = sb("cxb", [128, 2, L + 2])
        bt = sb("cbt", [128, 2, L])
        ct = sb("cct", [128, 2, L])
        uf = sb("cuf", [128, 2, L])
        cs = sb("ccs", [C2, NC2, 4, 256])
        dfs = sb("dfs", [128, 256])
        dft = sb("dft", [128, NC2, 2, L])
        d = [Dma(nc, f"df{i}") for i in range(NC2 + 1)]
        A.wait(k.V.last(), k.PE.last())
        td = [d[i](nc.scalar.dma_start(dft[:, i].rearrange("p a c -> p (a c)"), k.a["dft"][i])) for i in range(NC2)]
        ts_ = d[NC2](nc.scalar.dma_start(dfs, k.a["dfs"]))
        tz = V(nc.vector.memset(xb, 0.0))
        PE.wait(tu)
        hist = []
        tcs = []
        for j in range(4):
            i = j % 2
            old = hist[j - 2] if j >= 2 else (None, None, None)
            c, w = k.weight()
            wv = w.rearrange("p (t c) -> p t c", t=8)
            b = k.pair()
            t = linear(k, b, [wv[:, x, 0:128] for x in range(8)], tiles(uT, 8), 0, L)
            tb = k.cp(A, two(bt[:, i]), k.wide(b), t, old[0])
            k.give(tb, b, b + 1)
            b = k.pair()
            t = linear(k, b, [wv[:, x, 128:256] for x in range(8)], tiles(uT, 8), 0, L)
            k.release(c)
            tc = k.cp(A, two(ct[:, i]), k.wide(b), t, old[1])
            k.give(tc, b, b + 1)
            c, w = k.weight()
            wv = w.rearrange("p (t c) -> p t c", t=8)
            b = k.pair()
            t = linear(k, b, [wv[:, x, 0:128] for x in range(8)], tiles(uT, 8), 0, L)
            tx = k.tt(V, two(xb[:, i, 1:L + 1]), k.wide(b), two(ct[:, i]), MUL, t, tc, tz, old[0])
            k.give(tx, b, b + 1)
            b = k.pair()
            t = linear(k, b, [wv[:, x, 128:256] for x in range(8)], tiles(uT, 8), 0, L)
            k.release(c)
            tf = k.cp(A, two(uf[:, i]), k.wide(b), t, old[2])
            k.give(tf, b, b + 1)
            wv = [k.vec["sc"][:, 4 * x + j:4 * x + j + 1] for x in range(3)]
            t = conv(k, sc[:, j, :], xb[:, i], wv, tx, None)
            t = k.tt(V, sc[:, j, :], sc[:, j, :], bt[:, i], MUL, t, tb)
            PE.wait(tf, ts_)
            for g in range(3):
                b = k.pair()
                for h in range(2):
                    n = 2 * g + h
                    tp = PE(k.mm(k.ps[0:C2, b + h, 0:256], uf[:, i, C2 * n:C2 * n + C2], dfs, True, True))
                ta = k.cp(V, cs[:, 2 * g:2 * g + 2, j, :], k.ps[0:C2, b:b + 2, 0:256], tp)
                k.give(ta, b, b + 1)
            tcs.append(ta)
            hist.append((t, tx, tp))
        PE.wait(tcs, td)
        for j in range(4):
            b = k.pair()
            for n in range(NC2):
                for p in range(2):
                    for h, (c0, c1) in enumerate(split(0, L)):
                        ins = k.mm(k.ps[:, b + h, 0:HF], cs[:, n, j, 128 * p:128 * p + 128],
                                   dft[0:C2, n, p, c0:c1], n == 0 and p == 0, n == NC2 - 1 and p == 1)
            t = PE(ins)
            t = k.cp(A, two(fo[:, j, :]), k.wide(b), t)
            k.give(t, b, b + 1)
        k.sync_all()


def deltanet(k, dn, tu):
    nc, V, A, G, PE = k.nc, k.V, k.A, k.G, k.PE
    uT = k.uT
    two = lambda x: x.rearrange("p (a c) -> p a c", a=2)
    six = lambda x: x.rearrange("p (n c) -> p n c", n=NC2)
    chunk = lambda b, n, p=128: k.ps[0:p, b + n // 3, C2 * (n % 3):C2 * (n % 3) + C2]
    with ExitStack() as st:
        def sb(name, shape):
            return st.enter_context(nc.sbuf_tensor(name, shape, F32)).ap()

        lv = sb("lv2", [128, 2, 7, 128])
        dl = Dma(nc, "lv2")
        A.wait(V.last(), PE.last())
        tlv = dl(nc.scalar.dma_start(lv.rearrange("p a b c -> p (a b c)"), k.a["lv2"]))
        g_ = sb("ng", [C2, NC2, 8])
        be = sb("nbe", [C2, NC2, 8])
        tmp = sb("ntm", [C2, 2, NC2, 8])
        gc = sb("ngc", [C2, NC2, 8])
        eg = sb("neg", [C2, NC2, 8])
        el = sb("nel", [C2, NC2, 8])
        bg = sb("nbg", [C2, NC2, 8])
        ea = sb("nea", [128, 8])
        xb = sb("nxb", [128, 2, L + 2])
        qkv = sb("nqkv", [128, 3, L])
        z_ = sb("nz", [128, L])
        kt = sb("nkt", [C2, NC2, 128])
        vt = sb("nvt", [C2, NC2, 128])
        KK = sb("nKK", [C2, 2, L])
        of = xb[:, 0, 1:L + 1]
        EG = sb("nEG", [128, 2, L])
        DT = sb("nDT", [C2, 2, L])
        MT = sb("nMT", [C2, 2, L])
        AT = DT
        wT = sb("nT", [128, 2, L])
        T = wT[0:C2]
        TT = sb("nTT", [C2, 2, L])
        CP = sb("nCP", [C2, 4, L])
        Cl, P1 = CP[:, 0:2, :], CP[:, 2:4, :]
        u_ = CP.rearrange("p a c -> p (a c)")[:, 0:2 * NC2 * 128].rearrange("p (a n c) -> p a n c", a=2, n=NC2)
        vb = sb("nvb", [C2, 2, NC2, 128])
        kb = sb("nkb", [C2, 2, NC2, 128])
        kdec = sb("nkd", [C2, 2, NC2, 128])
        vn = sb("nvn", [C2, 2, 2, 128])
        Sd = sb("nSd", [128, 2, 128])
        PE.wait(tu, k.ld_wba)
        b = k.pair()
        for n in range(NC2):
            for x in range(8):
                ins = k.mm(k.ps[0:C2, b, 16 * n:16 * n + 16], uT[:, x, C2 * n:C2 * n + C2], k.wba[:, x, :],
                           x == 0, x == 7)
        t = PE(ins)
        src = k.ps[0:C2, b, 0:96].rearrange("p (n c) -> p n c", n=NC2)
        t0 = k.act(be, src[:, :, 0:8], ACT.Sigmoid, t)
        x_, y_ = tmp[:, 0], tmp[:, 1]
        t = k.tt(V, x_, src[:, :, 8:16], k.vec["dt"][0:C2].unsqueeze(1).to_broadcast([C2, NC2, 8]), ADD, t0)
        k.give([t, t0], b, b + 1)
        ta = k.act(y_, x_, ACT.Abs, t)
        ta = k.act(y_, y_, ACT.Exp, ta, scale=-1.0)
        ta = k.act(y_, y_, ACT.Ln, ta, bias=1.0)
        t = k.stt(V, x_, x_, 0.0, y_, MAX, ADD, ta)
        te = k.act(ea, k.vec["al"], ACT.Exp)
        t = k.stt(V, g_, x_, -1.0, ea[0:C2].unsqueeze(1).to_broadcast([C2, NC2, 8]), MUL, MUL, t, te)
        PE.wait(t)
        b = k.pair()
        gf = g_.rearrange("p n c -> p (n c)")
        one = k.ones[0:C2, 0:C2]
        k.mm(k.ps[0:C2, b, 0:48], k.con["ui"][0:C2, 0:C2], gf, True, True)
        k.mm(k.ps[0:C2, b, 48:96], k.con["li"][0:C2, 0:C2], gf, True, True)
        t = PE(k.mm(k.ps[0:C2, b, 96:144], one, gf, True, True))
        v8 = lambda o: k.ps[0:C2, b, o:o + 48].rearrange("p (n c) -> p n c", n=NC2)
        t1 = k.cp(V, gc[:, :, 0:4], v8(0)[:, :, 0:4], t)
        t1 = k.cp(V, gc[:, :, 4:8], v8(48)[:, :, 4:8], t)
        t2 = k.tt(V, el, v8(96), gc, SUB, t1)
        k.give(t2, b, b + 1)
        ta = k.act(el, el, ACT.Exp, t2)
        ta = k.act(eg, gc, ACT.Exp, t1)
        tcol = k.tt(V, bg, be, eg, MUL, ta, t0)
        tz = V(nc.vector.memset(xb, 0.0))
        free = {}
        PE.wait(tcol, tlv)
        for h in range(4):
            tok = []
            for j in range(4):
                if j % 2 == 0:
                    c, w = k.weight()
                    wv = w.rearrange("p (t c) -> p t c", t=8)
                b = k.pair()
                o = 128 * (j % 2)
                t = linear(k, b, [wv[:, x, o:o + 128] for x in range(8)], tiles(uT, 8), 0, L)
                if j % 2:
                    k.release(c)
                if j == 3:
                    tz_ = k.act(two(z_), k.wide(b), ACT.Silu, t, free.get("z"))
                    k.give(tz_, b, b + 1)
                    break
                t = k.cp(A, two(xb[:, j % 2, 1:L + 1]), k.wide(b), t, tz, free.get(("xb", j % 2)))
                k.give(t, b, b + 1)
                wc = [k.vec["dc"][:, 12 * x + 4 * j + h:12 * x + 4 * j + h + 1] for x in range(3)]
                t = conv(k, qkv[:, j, :], xb[:, j % 2], wc, t, free.get(("qkv", j)))
                free[("xb", j % 2)] = t
                tok.append(k.act(qkv[:, j, :], qkv[:, j, :], ACT.Silu, t))
            for j in range(2):
                t = k.act(k.sq[:, j, :], qkv[:, j, :], ACT.Square, tok[j], k.sqfree[j])
                PE.wait(t)
                b = k.pair()
                for x, (c0, c1) in enumerate(split(0, L)):
                    ins = k.mm(k.ps[:, b + x, 0:HF], k.ones, k.sq[:, j, c0:c1], True, True)
                t = PE(ins)
                k.sqfree[j] = t
                t = k.act(two(k.rb), k.wide(b), ACT.Sqrt, t, k.rbfree, bias=k.eps[:, 0:1])
                k.give(t, b, b + 1)
                V.wait(t)
                t = V(nc.vector.reciprocal(k.rb, k.rb))
                tok[j] = k.stt(V, qkv[:, j, :], qkv[:, j, :], 128.0 ** -0.5 if j == 0 else 1.0, k.rb, MUL, MUL, t)
                k.rbfree = tok[j]
            q_, k_, v_ = (qkv[:, j, :] for j in range(3))
            tm = []
            for dst, src, tk in ((kt, k_, tok[1]), (vt, v_, tok[2])):
                PE.wait(tk)
                for g in range(2):
                    b = k.pair()
                    for n in range(3):
                        ins = k.tr(k.ps[0:C2, b, 128 * n:128 * n + 128], src[:, C2 * (3 * g + n):C2 * (3 * g + n) + C2])
                    t = PE(ins)
                    t = k.cp(V, dst[:, 3 * g:3 * g + 3, :].rearrange("p a c -> p (a c)"), k.ps[0:C2, b, 0:384], t)
                    k.give(t, b, b + 1)
                    tm.append(t)
            PE.wait(tok[0])
            for x, other in enumerate((k_, q_)):
                b = k.pair()
                for n in range(NC2):
                    ins = k.mm(chunk(b, n, C2), k_[:, C2 * n:C2 * n + C2], other[:, C2 * n:C2 * n + C2], True, True)
                t = PE(ins)
                tkk = k.cp(V if x else A, two(KK[:, x, :]), k.ps[0:C2, b:b + 2, 0:HF], t, free.get(("KK", x)))
                k.give(tkk, b, b + 1)
                tm.append(tkk)
            D = [dict(), dict()]
            for d in range(2):
                s = D[d]
                hh = 4 * d + h
                tri = k.con["ui" if d == 0 else "li"][0:C2, 0:C2]
                b = k.pair()
                PE.wait(tcol)
                for n in range(NC2):
                    ins = k.mm(chunk(b, n), g_[:, n, hh:hh + 1].to_broadcast([C2, 128]), tri, True, True)
                t = PE(ins)
                s["EG"] = k.act(two(EG[:, d, :]), k.wide(b), ACT.Exp, t)
                mask = k.con["mf" if d == 0 else "mb"][0:C2, 0:C2]
                for n in range(NC2):
                    t1 = k.stt(V, DT[:, d, C2 * n:C2 * n + C2], chunk(b, n, C2), gc[:, n, hh:hh + 1], mask, SUB, ADD, s["EG"])
                k.give([s["EG"], t1], b, b + 1)
                t1 = k.act(DT[:, d, :], DT[:, d, :], ACT.Exp, t1)
                b = k.pair()
                for n in range(NC2):
                    ins = k.mm(chunk(b, n, C2), be[:, n, hh:hh + 1].to_broadcast([C2, C2]), k.ident[0:C2, 0:C2],
                               True, True)
                t = PE(ins)
                t2 = k.tt(V, two(MT[:, d, :]), k.ps[0:C2, b:b + 2, 0:HF], two(DT[:, d, :]), MUL, t, t1)
                k.give(t2, b, b + 1)
                s["MT"] = k.tt(V, MT[:, d, :], MT[:, d, :], KK[:, 0, :], MUL, t2, tm)
                s["AT"] = k.tt(V, AT[:, d, :], DT[:, d, :], KK[:, 1, :], MUL, t2, tm)
                for n in range(NC2):
                    k.ts(V, vb[:, d, n, :], vt[:, n, :], be[:, n, hh:hh + 1], None, MUL, None, tm)
                    k.ts(V, kb[:, d, n, :], kt[:, n, :], bg[:, n, hh:hh + 1], None, MUL)
                    s["cols"] = k.ts(V, kdec[:, d, n, :], kt[:, n, :], el[:, n, hh:hh + 1], None, MUL)
                lvl = lambda m: lv[0:C2, d, m, 0:C2].unsqueeze(1).to_broadcast([C2, NC2, C2])
                t = k.tt(V, six(TT[:, d, :]), six(MT[:, d, :]), lvl(0), MUL, s["MT"])
                idn = k.ident[0:C2, 0:C2].unsqueeze(1).to_broadcast([C2, NC2, C2])
                t = k.tt(V, six(TT[:, d, :]), idn, six(TT[:, d, :]), SUB, t)
                PE.wait(t)
                b = k.pair()
                for n in range(NC2):
                    ins = k.tr(chunk(b, n, C2), TT[:, d, C2 * n:C2 * n + C2])
                t = PE(ins)
                s["T"] = k.cp(A, two(T[:, d, :]), k.ps[0:C2, b:b + 2, 0:HF], t)
                k.give(s["T"], b, b + 1)
            at = lambda X, d, n: X[:, d, C2 * n:C2 * n + C2]
            pv = lambda b: k.ps[0:C2, b:b + 2, 0:HF]
            for m in range(1, 7):
                for d in range(2):
                    s = D[d]
                    t = k.tt(V, six(Cl[:, d, :]), six(MT[:, d, :]),
                             lv[0:C2, d, m, 0:C2].unsqueeze(1).to_broadcast([C2, NC2, C2]), MUL, s.get("mm1"))
                    PE.wait(t, s["T"])
                    b = k.pair()
                    for n in range(NC2):
                        ins = k.mm(chunk(b, n, C2), at(Cl, d, n), at(T, d, n), True, True)
                    s["mm1"] = PE(ins)
                    s["P1"] = k.cp(A, two(P1[:, d, :]), pv(b), s["mm1"], s.get("mm2"))
                    k.give(s["P1"], b, b + 1)
                for d in range(2):
                    s = D[d]
                    PE.wait(s["P1"])
                    b = k.pair()
                    for n in range(NC2):
                        ins = k.mm(chunk(b, n, C2), at(P1, d, n), at(TT, d, n), True, True)
                    t = PE(ins)
                    if m < 6:
                        b2 = k.pair()
                        for n in range(NC2):
                            ins = k.mm(chunk(b2, n, C2), at(TT, d, n), at(P1, d, n), True, True)
                        t2 = PE(ins)
                        s["mm2"] = t2
                        s["T"] = k.tt(V, two(T[:, d, :]), two(T[:, d, :]), pv(b2), SUB, t2, s["mm1"])
                        k.give(s["T"], b2, b2 + 1)
                        t = t2
                    s["T"] = k.tt(V, two(TT[:, d, :]), two(TT[:, d, :]), pv(b), SUB, t)
                    k.give(s["T"], b, b + 1)
            for d in range(2):
                s = D[d]
                PE.wait(s["T"], s["cols"])
                for g in range(2):
                    b = k.pair()
                    for n in range(3):
                        ins = k.mm(k.ps[0:C2, b, 128 * n:128 * n + 128], at(TT, d, 3 * g + n), vb[:, d, 3 * g + n, :],
                                   True, True)
                    t = PE(ins)
                    s["u"] = k.cp(A, u_[:, d, 3 * g:3 * g + 3, :].rearrange("p a c -> p (a c)"),
                                  k.ps[0:C2, b, 0:384], t)
                    k.give(s["u"], b, b + 1)
                b = k.pair()
                for n in range(NC2):
                    ins = k.mm(chunk(b, n), kb[:, d, n, :], at(TT, d, n), True, True)
                t = PE(ins)
                s["w"] = k.cp(A, two(wT[:, d, :]), k.wide(b), t)
                k.give(s["w"], b, b + 1)
            tof = [None] * NC2
            for step in range(NC2):
                for d in range(2):
                    s = D[d]
                    n = step if d == 0 else NC2 - 1 - step
                    cols = slice(C2 * n, C2 * n + C2)
                    if step == 0:
                        vnew, tv = u_[:, d, n, :], s["u"]
                    else:
                        PE.wait(s["S"], s["w"])
                        b = k.pair()
                        t = PE(k.mm(k.ps[0:C2, b, 0:128], wT[:, d, cols], Sd[:, d, :], True, True))
                        tv = k.tt(V, vn[:, d, step % 2, :], u_[:, d, n, :], k.ps[0:C2, b, 0:128], SUB, t, s["u"],
                                  s.get("vfree"))
                        k.give(tv, b, b + 1)
                        vnew = vn[:, d, step % 2, :]
                    b = k.pair()
                    PE.wait(tv, s["AT"])
                    if step:
                        tq = k.tt(V, k.sq[:, d, 0:C2], q_[:, cols], EG[:, d, cols], MUL, s["EG"], s.get("o"),
                                  k.sqfree[d])
                        PE.wait(tq)
                        k.mm(k.ps[:, b, 0:C2], Sd[:, d, :], k.sq[:, d, 0:C2], True, False)
                    s["o"] = PE(k.mm(k.ps[:, b, 0:C2], vnew, AT[:, d, cols], step == 0, True))
                    if step < NC2 - 1:
                        t = PE(k.mm(k.ps[:, b + 1, 0:128], kdec[:, d, n, :], vnew, True, True))
                    s["vfree"] = PE.last()
                    if step < 3:
                        to = k.cp(A, of[:, cols], k.ps[:, b, 0:C2], s["o"])
                        tof[n] = to
                    else:
                        to = k.tt(V, of[:, cols], of[:, cols], k.ps[:, b, 0:C2], ADD, s["o"], tof[n])
                    if step < NC2 - 1:
                        if step == 0:
                            s["S"] = k.cp(V, Sd[:, d, :], k.ps[:, b + 1, 0:128], t)
                        else:
                            e = C2 * n + C2 - 1 if d == 0 else C2 * n
                            s["S"] = k.stt(V, Sd[:, d, :], Sd[:, d, :], EG[:, d, e:e + 1], k.ps[:, b + 1, 0:128],
                                           MUL, ADD, t, s["EG"])
                        k.give([to, s["S"]], b, b + 1)
                    else:
                        k.give(to, b, b + 1)
            for d in range(2):
                k.sqfree[d] = D[d]["o"]
            t = k.act(k.sq[:, 0, :], of, ACT.Square, to, k.sqfree[0])
            PE.wait(t)
            b = k.pair()
            for x, (c0, c1) in enumerate(split(0, L)):
                ins = k.mm(k.ps[:, b + x, 0:HF], k.ones128, k.sq[:, 0, c0:c1], True, True)
            t = PE(ins)
            k.sqfree[0] = t
            t = k.act(two(k.rb), k.wide(b), ACT.Sqrt, t, k.rbfree, bias=k.eps[:, 0:1])
            k.give(t, b, b + 1)
            V.wait(t)
            t = V(nc.vector.reciprocal(k.rb, k.rb))
            t = k.stt(V, k.rb, k.rb, k.vec["dn"], z_, MUL, MUL, t, tz_)
            t = k.tt(V, dn[:, h, :], of, k.rb, MUL, t)
            k.rbfree = t
            k.sync_all()


def mixer(k, w2, w3, after):
    nc, V, A, G, PE = k.nc, k.V, k.A, k.G, k.PE
    two = lambda x: x.rearrange("p (a c) -> p a c", a=2)
    tu = rms(k, k.hT, w2, k.uT, 0, after)
    with ExitStack() as st:
        def sb(name, shape):
            return st.enter_context(nc.sbuf_tensor(name, shape, F32)).ap()

        sc = sb("msc", [128, 4, L])
        fo = sb("mfo", [128, 4, L])
        dn = sb("mdn", [128, 4, L])
        conv_fourier(k, sc, fo, tu)
        deltanet(k, dn, tu)
        mg = sb("mmg", [128, 8, L])
        gt = sb("mgt", [128, 2, L])
        y = sb("my", [128, 8, L])
        gfree = [None, None]
        n = 0
        for m in range(8):
            pieces = []
            for c in range(3):
                i, w = k.weight()
                if c == 0:
                    wv = w.rearrange("p (t c) -> p t c", t=8)
                    gates = [[wv[:, x, 128 * g:128 * g + 128] for x in range(8)] for g in range(2)]
                    ops = [(gates[0], k.uT, "gf"), (gates[1], k.uT, "gs")]
                elif c == 1:
                    w8 = w[:, 0:1024].rearrange("p (t c) -> p t c", t=8)
                    wa = w[:, 1024:1536].rearrange("p (t c) -> p t c", t=4)
                    wb = w[:, 1536:2048].rearrange("p (t c) -> p t c", t=4)
                    ops = [(tiles(wa, 4), fo, "yf"), (tiles(wb, 4), sc, "ys"), (tiles(w8, 8), k.uT, "gd")]
                else:
                    wa = w[:, 0:512].rearrange("p (t c) -> p t c", t=4)
                    ops = [(tiles(wa, 4), dn, "yd")]
                for ws, x, name in ops:
                    b = k.pair()
                    t = linear(k, b, ws, tiles(x, len(ws)), 0, L)
                    if name[0] == "g":
                        j = n % 2
                        n += 1
                        t = k.act(two(gt[:, j, :]), k.wide(b), ACT.Sigmoid, t, gfree[j])
                        k.give(t, b, b + 1)
                        pieces.append((name, j, t))
                    else:
                        g, j, tg = pieces.pop(0)
                        if name == "yf":
                            t = k.tt(V, two(mg[:, m, :]), k.wide(b), two(gt[:, j, :]), MUL, t, tg)
                            gfree[j] = t
                            k.give(t, b, b + 1)
                        else:
                            t = k.tt(V, two(gt[:, j, :]), k.wide(b), two(gt[:, j, :]), MUL, t, tg)
                            k.give(t, b, b + 1)
                            t = k.tt(V, mg[:, m, :], mg[:, m, :], gt[:, j, :], ADD, t)
                            gfree[j] = t
                k.release(i)
        PE.wait(t)
        for m in range(8):
            if m % 2 == 0:
                c, w = k.weight()
                wv = w.rearrange("p (t c) -> p t c", t=8)
            b = k.pair()
            o = 128 * (m % 2)
            t = linear(k, b, [wv[:, x, o:o + 128] for x in range(8)], tiles(mg, 8), 0, L)
            if m % 2:
                k.release(c)
            ty = k.cp(A if m % 2 else V, two(y[:, m, :]), k.wide(b), t)
            k.give(ty, b, b + 1)
        t = post(k, y, w3, 0, False, [V.last(), A.last()])
        k.sync_all()
    return t


def block2(k, t):
    gain = lambda j: [k.vec["g"][:, 8 * j + i:8 * j + i + 1] for i in range(8)]
    t = ffn(k, 0, gain(0), gain(1), t)
    t = mixer(k, gain(2), gain(3), t)
    t = ffn(k, NM, gain(4), gain(5), t)
    return t


def program(nc, a, out):
    k = K(nc, a, out)
    setup(k)
    block1(k)
    moe(k)
    t = block1_end(k)
    for q in (k.V, k.A, k.PE, k.G):
        q.wait(t)
    t = block2(k, t)
    d = Dma(nc, "out")
    k.SP.wait(t, k.ysz)
    k.SP.wait(d(nc.sync.dma_start(out, k.hT[:, :, NM:L])))


def kernel(**inputs):
    import concourse.bacc as bacc
    from concourse.bass_utils import run_bass_kernel_spmd

    nc = bacc.Bacc("TRN2", target_bir_lowering=False, num_devices=1)
    arrays = {"in_" + n: v for n, v in layout(inputs).items()}
    a = {n[3:]: nc.dram_tensor(n, v.shape, mybir.dt.from_np(v.dtype), kind="ExternalInput").ap()
         for n, v in arrays.items()}
    out = nc.dram_tensor("out", (128, 8, S), F32, kind="ExternalOutput").ap()
    program(nc, a, out)
    r = run_bass_kernel_spmd(nc, [arrays], core_ids=[0])
    y = r.results[0]["out"]
    return np.ascontiguousarray(y.transpose(1, 0, 2).reshape(D, S).T)[None]
```

```python
from contextlib import ExitStack

import numpy as np
import concourse.bass as bass
from concourse import mybir

F32 = mybir.dt.float32
F32R = mybir.dt.float32r
I32 = mybir.dt.int32
U32 = mybir.dt.uint32
ALU = mybir.AluOpType
ACT = mybir.ActivationFunctionType
AX = mybir.AxisListType.X
MUL, ADD, SUB, MAX = ALU.mult, ALU.add, ALU.subtract, ALU.max

D, NM, S, L = 1024, 16, 512, 528
HF = 264
FF, NE, EFF = 2816, 32, 512
CAP = 64
NOV = 16
NBLK = NE + NOV
C2, NC2 = 88, 6
EPS = 1e-6
SLOT = 2048
NSLOT = 6
BIG = 1e30

VEC = {}
_n = 0
for _k, _w in (("mix", 8), ("lb", 16), ("hn", 1), ("ffn", 8), ("fin", 8), ("g", 48), ("sc", 12), ("dc", 36),
               ("dn", 1), ("fb", 1), ("al", 8), ("dt", 8), ("rb", 36)):
    VEC[_k] = _n
    _n += _w
NVEC = _n

CON = {}
_n = 0
for _k, _w in (("id", 128), ("u", 128), ("ui", 128), ("li", 128), ("tri", 128), ("mf", 128), ("mb", 128),
               ("lv", 7 * 64), ("rst", L), ("io", 64), ("tok", 4)):
    CON[_k] = _n
    _n += _w
NCON = _n


def constants():
    c = np.zeros((128, NCON), np.float32)
    p = np.arange(128)[:, None]
    f = np.arange(128)[None, :]

    def put(k, a):
        c[:a.shape[0], CON[k]:CON[k] + a.shape[1]] = a

    put("id", (p == f) * 1.0)
    put("u", (p < f) * 1.0)
    put("ui", (p <= f) * 1.0)
    put("li", (p >= f) * 1.0)
    put("tri", np.where(f <= p, 0.0, -BIG))
    put("mf", np.where(p <= f, 0.0, -BIG))
    put("mb", np.where(p >= f, 0.0, -BIG))
    for n in range(7):
        h = 64 >> n
        j = np.arange(64)
        t = j // h * 2 * h + h + j % h
        put_at = CON["lv"] + 64 * n
        c[:, put_at:put_at + 64] = (p // (2 * h) == t[None] // (2 * h)) & (p % (2 * h) < h)
    r = np.ones((128, L), np.float32)
    r[:, [0, 16, 144, 272, 400]] = 0.0
    put("rst", r)
    put("io", np.broadcast_to(np.arange(64.0), (128, 64)))
    put("tok", np.arange(128.0)[:, None] + 128 * np.arange(4)[None])
    lv2 = np.zeros((128, 2, 7, 128), np.float32)
    for n in range(7):
        b = 1 << n
        m = (p // (2 * b) == f // (2 * b)) & (p % (2 * b) < b) & (f % (2 * b) >= b)
        lv2[:, 0, n] = m
        lv2[:, 1, n] = m.T
    order = np.arange(L)
    k = np.outer(order, order) % L
    dft = np.stack([np.cos(2 * np.pi * k / L), -np.sin(2 * np.pi * k / L)]) / np.sqrt(L * 64.0)
    dft = dft.reshape(2, NC2, C2, L).transpose(1, 2, 0, 3)
    full = np.zeros((NC2, 128, 2, L), np.float32)
    full[:, :C2] = dft
    k = np.outer(np.arange(64), np.arange(64)) % 64
    small = np.zeros((128, 256), np.float32)
    for g in range(2):
        small[64 * g:64 * g + 64, 64 * g:64 * g + 64] = np.cos(2 * np.pi * k / 64)
        small[64 * g:64 * g + 64, 128 + 64 * g:192 + 64 * g] = np.sin(2 * np.pi * k / 64)
    return {"con": c, "lv2": lv2.reshape(128, -1), "dft": full.reshape(NC2, 128, 2 * L), "dfs": small}


class Queue:

    def __init__(self, nc, eng, name):
        self.eng, self.sem, self.n, self.name = eng, nc.alloc_semaphore("q_" + name), 0, name
        self.seen = {}

    def __call__(self, ins):
        self.n += 1
        ins.then_inc(self.sem, 1)
        return (self.sem, self.n, self.name)

    def wait(self, *toks):
        for t in toks:
            if t is None:
                continue
            if isinstance(t, list):
                self.wait(*t)
            elif self.seen.get(t[2], 0) < t[1]:
                self.eng.wait_ge(t[0], t[1])
                self.seen[t[2]] = t[1]

    def last(self):
        return (self.sem, self.n, self.name) if self.n else None


class Dma:

    def __init__(self, nc, name):
        self.sem, self.n, self.name = nc.alloc_semaphore("d_" + name), 0, "d_" + name

    def __call__(self, ins):
        ins.then_inc(self.sem, 16)
        self.n += 16
        return (self.sem, self.n, self.name)


class K:
    def __init__(self, nc, a, out):
        self.nc, self.a, self.out = nc, a, out
        self.PE = Queue(nc, nc.tensor, "pe")
        self.V = Queue(nc, nc.vector, "v")
        self.A = Queue(nc, nc.scalar, "a")
        self.G = Queue(nc, nc.gpsimd, "g")
        self.SP = Queue(nc, nc.sync, "sp")
        self.ps = nc.alloc_psum_tensor("ps", [128, 8, 512], F32).ap()
        self.bank = [None] * 8
        self.pr = 0
        self.nsb = 0
        self.stream = []
        self.ring = nc.alloc_sbuf_tensor("ring", [128, NSLOT, SLOT], F32).ap()
        self.rd = [Dma(nc, f"r{i}") for i in range(NSLOT)]
        self.issued = self.taken = 0
        self.arrive = {}
        self.freed = {}

    def sb(self, name, shape, dt=F32):
        return self.nc.alloc_sbuf_tensor(name, shape, dt).ap()

    def mm(self, out, lhsT, rhs, start, stop):
        return self.nc.tensor.matmul(out, lhsT, rhs, start=start, stop=stop, skip_group_check=True)

    def tt(self, q, out, a, b, op, *after):
        q.wait(*after)
        return q(q.eng.tensor_tensor(out, a, b, op))

    def ts(self, q, out, a, s1, s2, op0, op1=None, *after):
        q.wait(*after)
        if op1 is None:
            return q(q.eng.tensor_scalar(out, a, s1, None, op0))
        return q(q.eng.tensor_scalar(out, a, s1, s2, op0, op1))

    def stt(self, q, out, a, s, b, op0, op1, *after):
        q.wait(*after)
        return q(q.eng.scalar_tensor_tensor(out=out, in0=a, scalar=s, in1=b, op0=op0, op1=op1))

    def cp(self, q, out, a, *after):
        q.wait(*after)
        if q is self.A:
            return q(q.eng.copy(out, a))
        return q(q.eng.tensor_copy(out, a))

    def act(self, out, a, func, *after, **kw):
        self.A.wait(*after)
        return self.A(self.nc.scalar.activation(out, a, func, **kw))

    def take(self, *banks):
        for b in banks:
            self.PE.wait(self.bank[b])
            self.bank[b] = None

    def give(self, tok, *banks):
        for b in banks:
            self.bank[b] = tok

    def pair(self, n=3):
        b = 2 * (self.pr % n)
        self.pr += 1
        self.take(b, b + 1)
        return b

    def wide(self, b, lo=0, hi=HF):
        return self.ps[:, b:b + 2, lo:hi]

    def plan(self, src, n):
        self.stream.append((src, n))

    def feed(self):
        while self.issued < len(self.stream) and self.issued < self.taken_done() + NSLOT:
            i = self.issued
            s = i % NSLOT
            src, n = self.stream[i]
            if i >= NSLOT:
                self.SP.wait(self.freed[i - NSLOT])
            self.arrive[i] = self.rd[s](self.nc.sync.dma_start(self.ring[:, s, 0:n], src))
            self.issued += 1

    def taken_done(self):
        n = 0
        while n in self.freed:
            n += 1
        return n

    def weight(self):
        i = self.taken
        self.taken += 1
        self.feed()
        self.PE.wait(self.arrive[i])
        return i, self.ring[:, i % NSLOT, :]

    def release(self, i):
        self.freed[i] = self.PE.last()
        self.feed()

    def raw(self, *readers):
        i = self.taken
        self.taken += 1
        self.feed()
        for q in readers:
            q.wait(self.arrive[i])
        return i, self.ring[:, i % NSLOT, :]

    def read(self, i, toks):
        self.freed[i] = toks
        self.feed()

    def sync_all(self):
        toks = [q.last() for q in (self.PE, self.V, self.A, self.G)]
        for q in (self.PE, self.V, self.A, self.G):
            q.wait(*[t for t in toks])


def split(r0, r1):
    return [(r0, r1)] if r1 - r0 <= 512 else [(0, HF), (HF, L)]


def plan_weights(k):
    a = k.a
    for p in range(4):
        k.plan(a["w_att"][p, :, 0:2048], 2048)
        k.plan(a["w_att"][p, :, 2048:3072], 1024)
    for h in range(8):
        k.plan(a["w_hg"][h, :, 0:2048], 2048)
        k.plan(a["w_hg"][h, :, 2048:4096], 2048)
    for m in range(8):
        k.plan(a["w_out1"][m, :, 0:2048], 2048)
        k.plan(a["w_out1"][m, :, 2048:3584], 1536)
    for c in range(4):
        k.plan(a["w_o"][c], 2048)
    for e in range(NE + 1):
        if e < NE:
            for c in range(4):
                k.plan(a["w_ein"][e, c], 2048)
        if e:
            for c in range(2):
                k.plan(a["w_eout"][e - 1, c], 2048)
    plan_ffn(k, "1")
    for j in range(4):
        k.plan(a["w_sf"][j, :, 0:2048], 2048)
        k.plan(a["w_sf"][j, :, 2048:4096], 2048)
    for j in range(4):
        k.plan(a["w_dn"][j, :, 0:2048], 2048)
        k.plan(a["w_dn"][j, :, 2048:4096], 2048)
    for m in range(8):
        k.plan(a["w_out2"][m, :, 0:2048], 2048)
        k.plan(a["w_out2"][m, :, 2048:4096], 2048)
        k.plan(a["w_out2"][m, :, 4096:4608], 512)
    for c in range(4):
        k.plan(a["w_o2"][c], 2048)
    plan_ffn(k, "2")


def plan_ffn(k, n):
    for g in range(3):
        for j in range(8 * g, min(8 * g + 8, 22)):
            k.plan(k.a["w_fi" + n][j], 2048)
        for c in range(4):
            w = 2048 if g < 2 else 1536
            k.plan(k.a["w_fo" + n][g, c, :, 0:w], w)


def linear(k, b, w, rhs, r0, r1, start=True, stop=True):
    n = len(w)
    for t in range(n):
        for j, (c0, c1) in enumerate(split(r0, r1)):
            ins = k.mm(k.ps[:w[t].shape[-1], b + j, 0:c1 - c0], w[t], rhs[t][:, c0:c1],
                       start and t == 0, stop and t == n - 1)
    return k.PE(ins)


class Halves:

    def __init__(self, k, st, name, slots, sizes, pool=0):
        sb = lambda n: st.enter_context(k.nc.sbuf_tensor(n + name, [128, slots, 1024], F32R)).ap()
        self.k, self.n, self.h, self.l = k, slots, sb("wh"), sb("wl")
        self.sizes, self.pool = sizes, pool
        self.free, self.ready = {}, {}
        self.cut, self.at, self.chunk, self.toks = 0, 0, None, []
        self.pos = 0

    def prepare(self):
        k, i = self.k, self.cut
        if self.chunk is None:
            self.chunk = k.raw(k.A)
            self.pos, self.toks = 0, []
        n, last = self.sizes[i]
        s = i % self.n
        src = self.chunk[1][:, self.pos:self.pos + n]
        ta = k.cp(k.A, self.h[:, s, 0:n], src, self.free.get(i - self.n))
        q = k.G if self.pool and i % self.pool == self.pool - 1 else k.V
        q.wait(k.arrive[self.chunk[0]])
        tv = k.tt(q, self.l[:, s, 0:n], src, self.h[:, s, 0:n].bitcast(F32), SUB, ta, self.free.get(i - self.n))
        self.ready[i] = [ta, tv]
        self.toks = self.toks + [ta, tv]
        self.pos += n
        self.cut += 1
        if last:
            k.read(self.chunk[0], self.toks)
            self.chunk = None

    def get(self):
        i = self.at
        self.at += 1
        while self.cut < min(i + self.n, len(self.sizes)):
            self.prepare()
        self.k.PE.wait(self.ready[i])
        s = i % self.n
        return i, self.h[:, s, :], self.l[:, s, :]

    def done(self, i):
        self.free[i] = self.k.PE.last()


def linear3(k, b, wh, wl, xh, xl, r0, r1, start=True, stop=True):
    n = len(wh)
    cols = list(enumerate(split(r0, r1)))
    for t in range(n):
        for p, (w, x) in enumerate(((wh, xh), (wh, xl), (wl, xh))):
            for j, (c0, c1) in cols:
                ins = k.mm(k.ps[:, b + j, 0:c1 - c0], w[t], x[t][:, c0:c1],
                           start and t == 0 and p == 0, stop and t == n - 1 and p == 2)
    return k.PE(ins)


def part(k, src, h, l, *after):
    ta = k.cp(k.A, h, src, *after)
    return k.tt(k.V, l, src, h.bitcast(F32), SUB, ta, *after)


def tiles(ap, n):
    return [ap[:, t, :] for t in range(n)]


def rms(k, x, w, out, r0, after, width=8, scale=None):
    n = L - r0
    sq, rb = k.sq, k.rb
    b = k.pair()
    one = k.ones1024 if width == 8 else k.ones128
    for t in range(width):
        a = k.act(sq[:, t % 2, r0:L], x[:, t, r0:L], ACT.Square, after, k.sqfree[t % 2])
        k.PE.wait(a)
        for j, (c0, c1) in enumerate(split(r0, L)):
            ins = k.mm(k.ps[:, b + j, 0:c1 - c0], one, sq[:, t % 2, c0:c1], t == 0, t == width - 1)
        p = k.PE(ins)
        k.sqfree[t % 2] = p
    src = k.wide(b) if n > 512 else k.ps[:, b, 0:n]
    dst = rb[:, 0:n].rearrange("p (a c) -> p a c", a=2) if n > 512 else rb[:, 0:n]
    a = k.act(dst, src, ACT.Sqrt, p, k.rbfree, bias=k.eps[:, 0:1])
    k.give(a, b, b + 1)
    v = k.V
    v.wait(a)
    t0 = v(k.nc.vector.reciprocal(rb[:, 0:n], rb[:, 0:n]))
    for t in range(width):
        last = k.stt(v, out[:, t, r0:L], x[:, t, r0:L], w[t], rb[:, 0:n], MUL, MUL, t0)
    k.rbfree = last
    return last


def attention(k, uT, u_tok, oaT):
    nc, V, A, G, PE = k.nc, k.V, k.A, k.G, k.PE
    with ExitStack() as st:
        def sb(name, shape):
            return st.enter_context(nc.sbuf_tensor(name, shape, F32)).ap()

        fx = sb("fx", [8, 3, L])
        one8 = sb("one8", [8, L])
        qa = sb("qa", [65, 2, 2, S])
        ka = sb("ka", [65, 2, 2, L])
        va = sb("va", [128, 2, 5, 128])
        P = sb("P", [128, 3, L])
        PT = sb("PT", [128, 3, 5, 128])
        sm = sb("sm", [128, 3, 4])
        PE.wait(u_tok, k.ld_wf)
        b = k.pair()
        t = linear(k, b, tiles(k.wf, 8), tiles(uT, 8), 0, L)
        f0, f1, f2 = (fx[:, i, :] for i in range(3))
        v2 = lambda x: x.rearrange("p (a c) -> p a c", a=2)
        t = k.ts(V, v2(f0), k.wide(b)[0:8], k.vec["fb"][0:8, 0:1], None, ADD, None, t, k.ld)
        k.give(t, b, b + 1)
        ta = k.act(f1, f0, ACT.Abs, t)
        ta = k.act(f1, f1, ACT.Exp, ta, scale=-1.0)
        ta = k.act(f1, f1, ACT.Ln, ta, bias=1.0)
        t = k.ts(V, f0, f0, 0.0, None, ALU.min, None, ta)
        t = k.tt(V, f0, f1, f0, SUB, t)
        t1 = V(nc.vector.memset(one8, 1.0))
        V.wait(t, t1)
        tc = V(nc.vector.tensor_tensor_scan(f2, one8, f0, 0.0, MUL, ADD))
        tq = [V(nc.vector.memset(qa[64:65, i], 1.0)) for i in range(2)]
        buf = [None, None]
        kd = [Dma(nc, "ka0"), Dma(nc, "ka1")]
        kfree = [None, None]
        units = []

        def project(p):
            i = p % 2
            c, w = k.weight()
            wv = w.rearrange("p (t c) -> p t c", t=8)
            PE.wait(u_tok)
            b = k.pair()
            t = linear(k, b, [wv[:, x, 0:128] for x in range(8)], tiles(uT, 8), NM, L)
            ts = []
            for j in range(2):
                A.wait(t, kfree[i])
                ts.append(A(nc.scalar.mul(qa[0:64, i, j, :], k.ps[64 * j:64 * j + 64, b, :], 0.125)))
            k.give(ts[-1], b, b + 1)
            b = k.pair()
            t = linear(k, b, [wv[:, x, 128:256] for x in range(8)], tiles(uT, 8), 0, L)
            k.release(c)
            for j in range(2):
                ts.append(k.cp(V, ka[0:64, i, j, :].rearrange("p (a c) -> p a c", a=2),
                               k.wide(b)[64 * j:64 * j + 64], t, kfree[i]))
            k.give(ts[-1], b, b + 1)
            G.wait(tc, kfree[i])
            ts.append(kd[i](nc.gpsimd.dma_start(ka[64:65, i], f2[2 * p:2 * p + 2, :])))
            c, w = k.weight()
            wv = w[:, 0:1024].rearrange("p (t c) -> p t c", t=8)
            b = k.pair()
            for m in range(5):
                n = NM if m == 0 else 128
                o = 0 if m == 0 else NM + 128 * (m - 1)
                dst = k.ps[0:n, b + 1, 0:128] if m == 0 else k.ps[:, b, 128 * (m - 1):128 * m]
                for x in range(8):
                    ins = k.mm(dst, uT[:, x, o:o + n], wv[:, x, :], x == 0, x == 7)
            t = PE(ins)
            k.release(c)
            ts.append(k.cp(A, va[:, i, 1:5, :].rearrange("p a c -> p (a c)"), k.ps[:, b, :], t, kfree[i]))
            ts.append(k.cp(A, va[0:NM, i, 0, :], k.ps[0:NM, b + 1, 0:128], t, kfree[i]))
            k.give(ts[-1], b, b + 1)
            buf[i] = ts

        def scores(p, j, q):
            i = p % 2
            u = len(units) % 3
            na = NM + 128 * q
            nk = na + 128
            b = k.pair()
            PE.wait(buf[i], tq[i])
            lhs = qa[:, i, j, 128 * q:128 * q + 128]
            k.mm(k.ps[:, b, 512 - na:512], lhs, ka[:, i, j, 0:na], True, True)
            k.mm(k.ps[:, b + 1, 0:128], lhs, ka[:, i, j, na:nk], True, False)
            t = PE(k.mm(k.ps[:, b + 1, 0:128], k.ident, k.con["tri"], False, True))
            src = k.ps[:, b:b + 2, :].rearrange("p a c -> p (a c)")[:, 512 - na:640]
            V.wait(t, units[-3][4] if len(units) >= 3 else None)
            t = V(nc.vector.tensor_reduce(sm[:, u, 0:1], src, AX, MAX, negate=True))
            t = k.act(P[:, u, 0:nk], src, ACT.Exp, t, bias=sm[:, u, 0:1], accum_out=sm[:, u, 1:2])
            k.give(t, b, b + 1)
            V.wait(t)
            t = V(nc.vector.reciprocal(sm[:, u, 2:3], sm[:, u, 1:2]))
            t = k.ts(V, P[:, u, 0:nk], P[:, u, 0:nk], sm[:, u, 2:3], None, MUL, None, t)
            units.append([p, j, q, t, None, u])

        def turn(n):
            p, j, q, t, _, u = units[n]
            PE.wait(t)
            b = k.pair()
            for m in range(q + 1):
                k.tr(k.ps[:, b, 128 * m:128 * m + 128], P[:, u, NM + 128 * m:NM + 128 * m + 128])
            t = PE(k.tr(k.ps[0:NM, b + 1, 0:128], P[:, u, 0:NM]))
            free = units[n - 3][4] if n >= 3 else None
            t1 = k.cp(V, PT[:, u, 1:q + 2, :].rearrange("p a c -> p (a c)"), k.ps[:, b, 0:128 * (q + 1)], t, free)
            t2 = k.cp(A, PT[0:NM, u, 0, :], k.ps[0:NM, b + 1, 0:128], t, free)
            k.give([t1, t2], b, b + 1)
            units[n][3] = [t1, t2]

        def values(n):
            p, j, q, t, _, u = units[n]
            i = p % 2
            PE.wait(t, buf[i])
            if j == 0 and q == 0:
                k.take(6)
            dst = k.ps[64 * j:64 * j + 64, 6, 128 * q:128 * q + 128]
            k.mm(dst, va[0:NM, i, 0, 64 * j:64 * j + 64], PT[0:NM, u, 0, :], True, False)
            for m in range(q + 1):
                ins = k.mm(dst, va[:, i, m + 1, 64 * j:64 * j + 64], PT[:, u, m + 1, :], False, m == q)
            t = PE(ins)
            units[n][4] = t
            if j == 1 and q == 3:
                kfree[i] = t
                t = k.cp(A, oaT[:, p, :], k.ps[:, 6, :], t)
                k.give(t, 6)
            return t

        project(0)
        todo = [(p, j, q) for p in range(4) for j in range(2) for q in range(4)]
        for n in range(len(todo) + 2):
            if n < len(todo):
                if n % 8 == 3 and todo[n][0] < 3:
                    project(todo[n][0] + 1)
                scores(*todo[n])
            if 1 <= n <= len(todo):
                turn(n - 1)
            if n >= 2:
                last = values(n - 2)
        k.sync_all()
    return last


def hgrn(k, uT, u_tok, oh):
    nc, V, A, G, PE = k.nc, k.V, k.A, k.G, k.PE
    with ExitStack() as st:
        def sb(name, shape):
            return st.enter_context(nc.sbuf_tensor(name, shape, F32)).ap()

        q_ = sb("hq", [128, 2, S])
        g_ = sb("hg", [128, 3, S])
        fs = sb("hfs", [128, L])
        kk = sb("hk", [128, 2, L])
        lf = sb("hlf", [128, L])
        bb = sb("hb", [128, 2, L])
        vv = sb("hv", [128, 3, 5, 128])
        E = sb("hE", [128, 2, L])
        qe = sb("hqe", [128, 2, S])
        kd = sb("hkd", [128, 2, L])
        kdt = sb("hkdt", [128, 2, 5, 128])
        dd = sb("hdd", [128, 2, S])
        Kl = sb("hKl", [128, 7, S])
        Ql = sb("hQl", [128, 7, 256])
        sc = sb("hsc", [128, 2, S])
        St = sb("hS", [128, 2, 128])
        oo = sb("ho", [128, 2, S])
        lbv = sb("lbv", [128, 3, 8])
        omv = sb("omv", [128, 8])
        l0, l1 = k.vec["lb"][:, 0:8], k.vec["lb"][:, 8:16]
        m, x0, x1 = lbv[:, 0, :], lbv[:, 1, :], lbv[:, 2, :]
        t = k.tt(V, m, l0, l1, MAX, k.ld)
        ta = k.tt(V, x0, l0, m, SUB, t)
        tb = k.tt(V, x1, l1, m, SUB, t)
        ta = k.act(x0, x0, ACT.Exp, ta)
        tb = k.act(x1, x1, ACT.Exp, tb)
        t = k.tt(V, x1, x0, x1, ADD, ta, tb)
        V.wait(t)
        t = V(nc.vector.reciprocal(x1, x1))
        t = k.tt(V, x0, x0, x1, MUL, t)
        lb = x0
        t_lb = k.ts(V, omv, lb, -1.0, 1.0, MUL, ADD, t)
        t_z = V(nc.vector.memset(Kl, 0.0))
        t_zs = V(nc.vector.memset(sc, 0.0))
        H = [dict() for _ in range(8)]

        def project(h):
            s = H[h]
            i, i3 = h % 2, h % 3
            old = H[h - 2] if h >= 2 else {}
            old3 = H[h - 3] if h >= 3 else {}
            c, w = k.weight()
            wv = w.rearrange("p (t c) -> p t c", t=8)
            PE.wait(u_tok)
            b = k.pair()
            t = linear(k, b, [wv[:, x, 0:128] for x in range(8)], tiles(uT, 8), NM, L)
            A.wait(t, old.get("lvl"), old.get("qe"), old.get("diag"))
            s["q"] = A(nc.scalar.mul(q_[:, i, :], k.ps[:, b, :], 128.0 ** -0.5))
            k.give(s["q"], b, b + 1)
            b = k.pair()
            t = linear(k, b, [wv[:, x, 128:256] for x in range(8)], tiles(uT, 8), 0, L)
            k.release(c)
            fs2 = fs.rearrange("p (a c) -> p a c", a=2)
            t = k.act(fs2, k.wide(b), ACT.Sigmoid, t, H[h - 1].get("k") if h else None)
            k.give(t, b, b + 1)
            t = k.ts(V, fs, fs, omv[:, h:h + 1], lb[:, h:h + 1], MUL, ADD, t, t_lb)
            tl = k.act(lf, fs, ACT.Ln, t, H[h - 1].get("b") if h else None)
            s["k"] = k.ts(V, kk[:, i, :], fs, -1.0, 1.0, MUL, ADD, t, old.get("diag"), old.get("kd"))
            V.wait(tl, old.get("lvl"))
            s["b"] = V(nc.vector.tensor_tensor_scan(bb[:, i, :], k.con["rst"], lf, 0.0, MUL, ADD))
            c, w = k.weight()
            wv = w.rearrange("p (t c) -> p t c", t=8)
            b = k.pair()
            for m in range(5):
                n = NM if m == 0 else 128
                o = 0 if m == 0 else NM + 128 * (m - 1)
                dst = k.ps[0:n, b + 1, 0:128] if m == 0 else k.ps[:, b, 128 * (m - 1):128 * m]
                for x in range(8):
                    ins = k.mm(dst, uT[:, x, o:o + n], wv[:, x, 0:128], x == 0, x == 7)
            t = PE(ins)
            ta = k.cp(A, vv[:, i3, 1:5, :].rearrange("p a c -> p (a c)"), k.ps[:, b, :], t, old3.get("o"))
            ta = k.cp(A, vv[0:NM, i3, 0, :], k.ps[0:NM, b + 1, 0:128], t)
            k.give(ta, b, b + 1)
            s["v"] = ta
            b = k.pair()
            t = linear(k, b, [wv[:, x, 128:256] for x in range(8)], tiles(uT, 8), NM, L)
            k.release(c)
            s["g"] = k.act(g_[:, i3, :], k.ps[:, b, :], ACT.Sigmoid, t, old3.get("fin"))
            k.give(s["g"], b, b + 1)

        def prepare(h):
            s = H[h]
            i = h % 2
            old = H[h - 2] if h >= 2 else {}
            s["E"] = k.act(E[:, i, :], bb[:, i, :], ACT.Exp, s["b"], old.get("S"))
            s["qe"] = k.tt(V, qe[:, i, :], q_[:, i, :], E[:, i, NM:L], MUL, s["E"], s["q"], old.get("o"))
            last = bb[:, i, NM:L].rearrange("p (c x) -> p c x", c=4)
            e = last[:, :, 127:128].to_broadcast([128, 4, 128])
            t1 = k.tt(V, kd[:, i, NM:L].rearrange("p (c x) -> p c x", c=4), e, last, SUB, s["b"], old.get("kt"))
            t2 = k.tt(V, kd[:, i, 0:NM], bb[:, i, NM - 1:NM].to_broadcast([128, NM]), bb[:, i, 0:NM], SUB, s["b"])
            t = k.act(kd[:, i, :], kd[:, i, :], ACT.Exp, t1, t2)
            s["kd"] = k.tt(V, kd[:, i, :], kd[:, i, :], kk[:, i, :], MUL, t, s["k"])
            dfree = H[h - 1].get("dfree", [None, None]) if h else [None, None]
            s["L"] = []
            prevmm = H[h - 1].get("mml") if h else None
            for n in range(7):
                hs = 64 >> n
                nb = S // (2 * hs)
                B = bb[:, i, NM:L].rearrange("p (n x) -> p n x", n=nb)
                ref = B[:, :, hs - 1:hs].to_broadcast([128, nb, hs])
                d = dd[:, n % 2, :]
                d3 = d.rearrange("p (n x) -> p n x", n=nb)
                t1 = k.tt(V, d3[:, :, 0:hs], ref, B[:, :, 0:hs], SUB, s["b"], dfree[n % 2])
                t2 = k.tt(V, d3[:, :, hs:2 * hs], B[:, :, hs:2 * hs], ref, SUB)
                t = k.act(d, d, ACT.Exp, t1, t2)
                K3 = kk[:, i, NM:L].rearrange("p (n x) -> p n x", n=nb)
                Q3 = q_[:, i, :].rearrange("p (n x) -> p n x", n=nb)
                ta = k.tt(V, Kl[:, n, :].rearrange("p (n x) -> p n x", n=nb)[:, :, 0:hs], d3[:, :, 0:hs],
                          K3[:, :, 0:hs], MUL, t, t_z, prevmm, s["k"])
                tb = k.tt(V, Ql[:, n, :].rearrange("p (n x) -> p n x", n=nb), d3[:, :, hs:2 * hs],
                          Q3[:, :, hs:2 * hs], MUL, t, s["q"])
                dfree[n % 2] = tb
                s["L"].append([ta, tb])
            s["dfree"] = dfree
            s["lvl"] = tb

        def level(h):
            s = H[h]
            i = h % 2
            old = H[h - 2] if h >= 2 else {}
            tok = [old.get("o"), t_zs]
            for n in range(7):
                hs = 64 >> n
                if n % 2 == 0:
                    b = k.pair()
                bk = b + n % 2
                PE.wait(s["L"][n])
                for c in range(4):
                    ins = k.mm(k.ps[:, bk, 64 * c:64 * c + 64], Kl[:, n, 128 * c:128 * c + 128],
                               Ql[:, n, 64 * c:64 * c + 64], True, True)
                t = PE(ins)
                s["mml"] = t
                nb = 64 // hs
                V.wait(t, tok)
                dst = sc[:, i, :].rearrange("p (c n x) -> p c n x", c=4, n=nb)[:, :, :, hs:2 * hs]
                src = k.ps[:, bk, 0:256].rearrange("p (c n x) -> p c n x", c=4, n=nb)
                for c in range(4):
                    mask = k.con["lv"][:, 64 * n:64 * n + 64].rearrange("p (n x) -> p n x", n=nb).bitcast(I32)
                    tw = V(nc.vector.copy_predicated(dst[:, c], mask, src[:, c]))
                tok = tw
                if n % 2 == 1 or n == 6:
                    k.give(tw, b, b + 1)
            b = k.pair()
            PE.wait(s["q"], s["k"])
            for c in range(4):
                ins = k.mm(k.ps[:, b, 128 * c:128 * c + 128], kk[:, i, NM + 128 * c:NM + 128 * c + 128],
                           q_[:, i, 128 * c:128 * c + 128], True, True)
            t = PE(ins)
            s["diag"] = t
            V.wait(t, tok)
            for c in range(4):
                tw = V(nc.vector.copy_predicated(sc[:, i, 128 * c:128 * c + 128], k.ident.bitcast(I32),
                                                 k.ps[:, b, 128 * c:128 * c + 128]))
            k.give(tw, b, b + 1)
            s["sc"] = tw
            b = k.pair()
            PE.wait(s["kd"])
            for c in range(4):
                k.tr(k.ps[:, b, 128 * c:128 * c + 128], kd[:, i, NM + 128 * c:NM + 128 * c + 128])
            t = PE(k.tr(k.ps[0:NM, b + 1, 0:128], kd[:, i, 0:NM]))
            s["kt"] = t
            ta = k.cp(A, kdt[:, i, 1:5, :].rearrange("p a c -> p (a c)"), k.ps[:, b, :], t, old.get("S"))
            ta = k.cp(A, kdt[0:NM, i, 0, :], k.ps[0:NM, b + 1, 0:128], t)
            k.give(ta, b, b + 1)
            s["kdt"] = ta

        def output(h):
            s = H[h]
            i, i3 = h % 2, h % 3
            old = H[h - 2] if h >= 2 else {}
            k.take(6, 7)
            PE.wait(s["kdt"], s["v"])
            k.mm(k.ps[:, 7, 0:128], kdt[0:NM, i, 0, :], vv[0:NM, i3, 0, :], True, True)
            for c in range(3):
                o = 128 * (c + 1)
                t = PE(k.mm(k.ps[:, 7, o:o + 128], kdt[:, i, c + 1, :], vv[:, i3, c + 1, :], True, True))
            tS = k.cp(V, St[:, i, :], k.ps[:, 7, 0:128], t, old.get("o"))
            PE.wait(s["qe"], s["sc"])
            for c in range(4):
                dst = k.ps[:, 6, 128 * c:128 * c + 128]
                k.mm(dst, vv[:, i3, c + 1, :], sc[:, i, 128 * c:128 * c + 128], True, False)
                PE.wait(tS)
                s["o"] = PE(k.mm(dst, St[:, i, :], qe[:, i, 128 * c:128 * c + 128], False, True))
                if c < 3:
                    o = 128 * (c + 1)
                    e = E[:, i, NM + 128 * c + 127:NM + 128 * c + 128]
                    tS = k.stt(V, St[:, i, :], St[:, i, :], e, k.ps[:, 7, o:o + 128], MUL, ADD, t, s["o"])
            s["S"] = tS
            k.give(tS, 7)
            to = k.cp(V, oo[:, i, :], k.ps[:, 6, :], s["o"], old.get("fin"))
            k.give(to, 6)
            ta = k.act(k.sq[:, 0, 0:S], oo[:, i, :], ACT.Square, to, k.sqfree[0])
            PE.wait(ta)
            b = k.pair()
            t = PE(k.mm(k.ps[:, b, :], k.ones128, k.sq[:, 0, 0:S], True, True))
            k.sqfree[0] = t
            ta = k.act(k.rb[:, 0:S], k.ps[:, b, :], ACT.Sqrt, t, k.rbfree, bias=k.eps[:, 0:1])
            k.give(ta, b, b + 1)
            V.wait(ta)
            t = V(nc.vector.reciprocal(k.rb[:, 0:S], k.rb[:, 0:S]))
            t = k.stt(V, k.rb[:, 0:S], k.rb[:, 0:S], k.vec["hn"], g_[:, i3, :], MUL, MUL, t, s["g"])
            s["fin"] = k.tt(V, oh[:, h, :], oo[:, i, :], k.rb[:, 0:S], MUL, t)
            k.rbfree = s["fin"]

        for h in range(10):
            if h < 8:
                project(h)
            if 1 <= h < 9:
                level(h - 1)
            if h >= 2:
                output(h - 2)
            if h < 8:
                prepare(h)
        k.sync_all()


def mix_out(k, uT, oaT, oh, hT, mix, gt):
    nc, V, A, PE = k.nc, k.V, k.A, k.PE
    free = [None, None]
    mt = []
    for m in range(8):
        i = m % 2
        c, w = k.weight()
        wv = w.rearrange("p (t c) -> p t c", t=8)
        b = k.pair()
        t = linear(k, b, [wv[:, x, 0:128] for x in range(8)], tiles(uT, 8), NM, L)
        ta = k.act(gt[:, i, 0, :], k.ps[:, b, :], ACT.Sigmoid, t, free[i])
        k.give(ta, b, b + 1)
        b = k.pair()
        t = linear(k, b, [wv[:, x, 128:256] for x in range(8)], tiles(uT, 8), NM, L)
        tb = k.act(gt[:, i, 1, :], k.ps[:, b, :], ACT.Sigmoid, t)
        k.give(tb, b, b + 1)
        k.release(c)
        c, w = k.weight()
        wa = w[:, 0:512].rearrange("p (t c) -> p t c", t=4)
        wh = w[:, 512:1536].rearrange("p (t c) -> p t c", t=8)
        b = k.pair()
        t = linear(k, b, tiles(wa, 4), tiles(oaT, 4), 0, S)
        ta = k.tt(V, gt[:, i, 0, :], k.ps[:, b, :], gt[:, i, 0, :], MUL, t, ta)
        k.give(ta, b, b + 1)
        b = k.pair()
        t = linear(k, b, tiles(wh, 8), tiles(oh, 8), 0, S)
        tb = k.tt(V, gt[:, i, 1, :], k.ps[:, b, :], gt[:, i, 1, :], MUL, t, tb)
        k.give(tb, b, b + 1)
        k.release(c)
        free[i] = k.tt(V, mix[:, m, :], gt[:, i, 0, :], gt[:, i, 1, :], ADD, ta, tb)
    PE.wait(free[0], free[1])
    for m in range(8):
        if m % 2 == 0:
            c, w = k.weight()
            wv = w.rearrange("p (t c) -> p t c", t=8)
        b = k.pair()
        o = 128 * (m % 2)
        t = linear(k, b, [wv[:, x, o:o + 128] for x in range(8)], tiles(mix, 8), 0, S)
        if m % 2:
            k.release(c)
        t = k.tt(V, hT[:, m, NM:L], hT[:, m, NM:L], k.ps[:, b, :], ADD, t)
        k.give(t, b, b + 1)
    return t


def setup(k):
    nc = k.nc
    k.ident = None
    con = k.sb("con", [128, NCON])
    vec = k.sb("vec", [128, NVEC])
    k.wf = k.sb("wf", [128, 8, 8])
    k.wba = k.sb("wba", [128, 8, 16])
    k.wr = k.sb("wr", [128, 8, 36])
    k.hT = k.sb("hT", [128, 8, L])
    k.uT = k.sb("uT", [128, 8, L])
    k.sq = k.sb("sq", [128, 2, L])
    k.rb = k.sb("rb", [128, L])
    k.ones1024 = k.sb("o1024", [128, 128])
    k.ones128 = k.sb("o128", [128, 128])
    k.ones = k.sb("o1", [128, 128])
    k.eps = k.sb("eps", [128, 1])
    k.sqfree = [None, None]
    k.rbfree = None
    k.con = {n: con[:, o:o + w] for n, o, w in
             ((n, CON[n], w) for n, w in (("id", 128), ("u", 128), ("ui", 128), ("li", 128), ("tri", 128),
                                          ("mf", 128), ("mb", 128), ("lv", 448), ("rst", L), ("io", 64),
                                          ("tok", 4)))}
    k.vec = {n: vec[:, VEC[n]:VEC[n] + w] for n, w in
             (("mix", 8), ("lb", 16), ("hn", 1), ("ffn", 8), ("fin", 8), ("g", 48), ("sc", 12), ("dc", 36),
              ("dn", 1), ("fb", 1), ("al", 8), ("dt", 8), ("rb", 36))}
    k.ident = k.con["id"]
    k.tr = lambda out, in_: nc.tensor.transpose(out, in_, k.ident[:in_.shape[0], :in_.shape[0]])
    d = [Dma(nc, f"ld{i}") for i in range(6)]
    a = k.a
    t1 = d[0](nc.scalar.dma_start(k.hT, a["hT"]))
    t2 = d[1](nc.scalar.dma_start(vec, a["vec"]))
    t3 = d[2](nc.scalar.dma_start(con, a["con"]))
    t4 = d[3](nc.scalar.dma_start(k.wf, a["w_f"]))
    t5 = d[4](nc.scalar.dma_start(k.wba, a["w_ba"]))
    t6 = d[5](nc.scalar.dma_start(k.wr, a["w_r"]))
    k.ld_h, k.ld, k.ld_wf, k.ld_wr, k.ld_wba = t1, [t2, t3], t4, t6, t5
    V = k.V
    toks = [V(nc.vector.memset(k.ones1024, 1.0 / 1024)), V(nc.vector.memset(k.ones128, 1.0 / 128)),
            V(nc.vector.memset(k.ones, 1.0)), V(nc.vector.memset(k.eps, EPS))]
    for q in (k.PE, k.V, k.A, k.G):
        q.wait(toks, k.ld)
    k.ys = nc.dram_tensor("ys", [NBLK * CAP, D], F32, kind="Internal").ap()
    zero = k.sb("zero", [128, 256])
    z = V(nc.vector.memset(zero, 0.0))
    k.A.wait(z)
    k.ysz = []
    for j in range(NOV * CAP // 128):
        dz = Dma(nc, f"ysz{j}")
        r = NE * CAP + 128 * j
        k.ysz.append(dz(nc.scalar.dma_start(k.ys[r:r + 128, :].rearrange("p (a c) -> p a c", c=256),
                                            zero.unsqueeze(1).to_broadcast([128, 4, 256]))))
    plan_weights(k)
    k.feed()


def block1(k):
    t = rms(k, k.hT, [k.vec["mix"][:, i:i + 1] for i in range(8)], k.uT, 0, k.ld_h)
    with ExitStack() as st:
        oaT = st.enter_context(k.nc.sbuf_tensor("oaT", [128, 4, S], F32)).ap()
        attention(k, k.uT, t, oaT)
        oh = st.enter_context(k.nc.sbuf_tensor("oh", [128, 8, S], F32)).ap()
        hgrn(k, k.uT, t, oh)
        mix = st.enter_context(k.nc.sbuf_tensor("mix", [128, 8, S], F32)).ap()
        gt = st.enter_context(k.nc.sbuf_tensor("gt", [128, 2, 2, S], F32)).ap()
        mix_out(k, k.uT, oaT, oh, k.hT, mix, gt)
        k.sync_all()


def ktiles(w):
    return w.reshape(w.shape[0] // 128, 128, w.shape[1]).transpose(1, 0, 2)


def side(*parts):
    a = np.concatenate(parts, axis=2)
    return a.reshape(128, -1)


def layout(i):
    A = np.asarray
    i = {n: A(v) for n, v in i.items()}
    o = {}
    o["hT"] = np.concatenate([i["meta_tokens"], i["x"][0]], 0).T.reshape(8, 128, L).transpose(1, 0, 2)
    o["m2T"] = i["meta_tokens_2"].T.reshape(8, 128, NM).transpose(1, 0, 2)
    col = lambda v: v.reshape(-1, 128).T
    vec = np.zeros((128, NVEC), np.float32)

    def put(n, a):
        vec[:a.shape[0], VEC[n]:VEC[n] + a.shape[1]] = a

    put("mix", col(i["norm_mix_w"][0]))
    put("lb", np.concatenate([col(i["hgrn_lb_logits"][0]), col(i["hgrn_lb_logits"][1])], 1))
    put("hn", col(i["hgrn_norm_w"][0]))
    put("ffn", col(i["norm_ffn_w"][0]))
    put("fin", col(i["norm_final_w"]))
    put("g", np.concatenate([col(i["norm_gains_2"][0, j]) for j in range(6)], 1))
    put("sc", np.concatenate([col(i["sconv_w_2"][0, j]) for j in range(3)], 1))
    put("dc", np.concatenate([col(i["dn_conv_w_2"][0, j]) for j in range(3)], 1))
    put("dn", col(i["dn_norm_2"][0]))
    put("fb", i["attn_forget_b"][0][:, None])
    put("al", np.broadcast_to(i["dn_A_log_2"][0].reshape(1, 8), (128, 8)))
    put("dt", np.broadcast_to(i["dn_dt_bias_2"][0].reshape(1, 8), (128, 8)))
    put("rb", np.broadcast_to(np.concatenate([i["b_router_group"][0], i["b_router_expert"][0]])[None], (128, 36)))
    o["vec"] = vec
    w = ktiles(i["w_in"][0])
    s = np.cumsum([0, 512, 512, 512, 8, 1024, 1024, 1024, 1024, 1024, 1024])
    at = lambda j, t: w[:, :, s[j] + 128 * t:s[j] + 128 * t + 128]
    o["w_att"] = np.stack([np.concatenate([side(at(0, p), at(1, p)), side(at(2, p))], 1) for p in range(4)])
    o["w_f"] = w[:, :, s[3]:s[4]]
    o["w_hg"] = np.stack([np.concatenate([side(at(4, h), at(5, h)), side(at(6, h), at(7, h))], 1) for h in range(8)])
    wa, wh = ktiles(i["w_attn_out"][0]), ktiles(i["w_hgrn_out"][0])
    t = lambda x, m: x[:, :, 128 * m:128 * m + 128]
    o["w_out1"] = np.stack([np.concatenate([side(at(8, m), at(9, m)), side(t(wa, m)), side(t(wh, m))], 1)
                            for m in range(8)])
    halves = lambda x, n, c: np.stack([side(x[:, :, c * j:c * j + c]) for j in range(n)])
    o["w_o"] = halves(ktiles(i["w_o"][0]), 4, 256)
    o["w_r"] = np.concatenate([ktiles(i["w_router_group"][0]), ktiles(i["w_router_expert"][0])], 2)
    e = i["w_expert_in"][0]
    o["w_ein"] = e.reshape(NE, 2, 4, 128, 2, 512).transpose(0, 4, 1, 3, 2, 5).reshape(NE, 4, 128, 2048)
    e = i["w_expert_out"][0]
    o["w_eout"] = e.reshape(NE, 4, 128, 2, 512).transpose(0, 3, 2, 1, 4).reshape(NE, 2, 128, 2048)
    for n in "12":
        wi = ktiles(i[f"ffn{n}_wi_2"][0])
        o["w_fi" + n] = np.stack([np.concatenate([side(t(wi, j)), side(t(wi, 22 + j))], 1) for j in range(22)])
        wo = ktiles(i[f"ffn{n}_wo_2"][0])
        f = np.zeros((3, 4, 128, 2048), np.float32)
        for g in range(3):
            for c in range(4):
                x = np.concatenate([side(t(wo[:, 8 * g:8 * g + 8], 2 * c + m)) for m in range(2)], 1)
                f[g, c, :, :x.shape[1]] = x
        o["w_fo" + n] = f
    w = ktiles(i["w_in_2"][0])
    s2 = {"f": 0, "b": 512, "c": 1024, "h": 1536, "q": 2048, "k": 2560, "v": 3072, "z": 3584,
          "gf": 4112, "gs": 5136, "gd": 6160}
    at = lambda j, m: w[:, :, s2[j] + 128 * m:s2[j] + 128 * m + 128]
    o["w_ba"] = w[:, :, 4096:4112]
    o["w_sf"] = np.stack([np.concatenate([side(at("b", j), at("c", j)), side(at("h", j), at("f", j))], 1)
                          for j in range(4)])
    o["w_dn"] = np.stack([np.concatenate([side(at("q", j), at("k", j)), side(at("v", j), at("z", j))], 1)
                          for j in range(4)])
    f, c, d = (ktiles(i[n][0]) for n in ("w_fourier_2", "w_sconv_out_2", "w_dn_out_2"))
    o["w_out2"] = np.stack([np.concatenate([side(at("gf", m), at("gs", m)), side(at("gd", m)), side(t(f, m)),
                                            side(t(c, m)), side(t(d, m))], 1) for m in range(8)])
    o["w_o2"] = halves(ktiles(i["w_out_2"][0]), 4, 256)
    o.update(constants())
    return {n: np.ascontiguousarray(v) for n, v in o.items()}


def route(k, sb, uT, tv):
    nc, V, A, G, PE = k.nc, k.V, k.A, k.G, k.PE
    lg = sb("lg", [128, 4, 36])
    oh = sb("roh", [128, 2, 4, 32])
    ee = sb("ree", [128, 4, 32])
    e2 = sb("re2", [128, 4, 32])
    g4 = sb("rg4", [128, 3, 16])
    s = sb("rs", [128, 16, 8])
    nb = sb("rnb", [128, 3, 32])
    io = sb("rio", [128, 2, 64])
    gate = sb("gate", [128, 2, 4])
    dst = sb("dst", [128, 2, 4], U32)
    R = sb("rR", [128, 8, 64])
    B = sb("rB", [128, 8, NBLK])
    idx = sb("idx", [64, NBLK], U32)
    ov = sb("ov", [1, 1 + NOV], I32)
    cmp_ = sb("rcmp", [1, NOV, 32])
    ovf = sb("rovf", [1, NOV])

    def red(out, in_, op, *after):
        V.wait(*after)
        return V(nc.vector.tensor_reduce(out, in_, AX, op))

    def first(out, eq, w, m, t):
        t = k.tt(V, eq, eq, w, MUL, t)
        t = red(m, eq, MAX, t)
        return k.tt(V, out, eq, m.unsqueeze(2).to_broadcast(list(eq.shape)), ALU.is_equal, t)

    PE.wait(tv, k.ld_wr)
    b = k.pair()
    for i in range(4):
        for x in range(8):
            ins = k.mm(k.ps[:, b, 36 * i:36 * i + 36], uT[:, x, NM + 128 * i:NM + 128 * i + 128],
                       k.wr[:, x, :], x == 0, x == 7)
    t = PE(ins)
    t = k.tt(V, lg, k.ps[:, b, 0:144].rearrange("p (a c) -> p a c", a=4),
             k.vec["rb"].unsqueeze(1).to_broadcast([128, 4, 36]), ADD, t)
    k.give(t, b, b + 1)
    down, iota = io[:, 0, :], k.con["io"]
    tw = k.ts(V, down, iota, -1.0, 64.0, MUL, ADD)
    gl = lg[:, :, 0:4]
    gm, gsum, pg, m = (s[:, j, 0:4] for j in range(4))
    up = lambda x, n: x.unsqueeze(2).to_broadcast([128, 4, n])
    row = lambda x, n: x[:, 0:n].unsqueeze(1).to_broadcast([128, 4, n])
    g1, gx, gd = (g4[:, j, :].rearrange("p (a c) -> p a c", a=4) for j in range(3))
    t = red(gm, gl, MAX, t, tw)
    t1 = k.tt(V, gd, gl, up(gm, 4), SUB, t)
    t2 = k.act(gd, gd, ACT.Exp, t1)
    t = k.tt(V, gx, gl, up(gm, 4), ALU.is_equal, t)
    t = first(g1, gx, row(down, 4), m, t)
    ts_ = red(gsum, gd, ADD, t2)
    V.wait(ts_)
    tp = V(nc.vector.reciprocal(pg, gsum))
    t = k.ts(V, gx, g1, -1.0, BIG, ADD, MUL, t)
    for i in range(4):
        t0 = k.tt(V, ee[:, i, :].rearrange("p (g e) -> p g e", g=4),
                  lg[:, i, 4:36].rearrange("p (g e) -> p g e", g=4),
                  gx[:, i, :].unsqueeze(2).to_broadcast([128, 4, 8]), ADD, t)
    t = t0
    v1, v2 = s[:, 4, 0:4], s[:, 5, 0:4]
    t = red(v1, ee, MAX, t)
    t = k.tt(V, e2, ee, up(v1, 32), ALU.is_equal, t)
    t = first(oh[:, 0], e2, row(down, 32), m, t)
    t = k.stt(V, ee, oh[:, 0], -BIG, ee, MUL, ADD, t)
    t = red(v2, ee, MAX, t)
    t = k.tt(V, e2, ee, up(v2, 32), ALU.is_equal, t)
    t = first(oh[:, 1], e2, row(down, 32), m, t)
    ta = k.tt(V, v2, v2, v1, SUB, t)
    ta = k.act(v2, v2, ACT.Exp, ta)
    ta = k.ts(V, v1, v2, 1.0, None, ADD, None, ta)
    V.wait(ta)
    ta = V(nc.vector.reciprocal(v1, v1))
    ta = k.tt(V, gate[:, 0, :], v1, pg, MUL, ta, tp)
    t_gate = k.tt(V, gate[:, 1, :], v2, gate[:, 0, :], MUL, ta)
    t = k.tt(V, e2, oh[:, 0], oh[:, 1], ADD, t)
    PE.wait(t)
    b = k.pair()
    for i in range(4):
        for j in range(i):
            k.mm(k.ps[:, b, 32 * i:32 * i + 32], k.ones, e2[:, j, :], j == 0, False)
        k.mm(k.ps[:, b, 32 * i:32 * i + 32], k.con["u"], e2[:, i, :], i == 0, True)
    for j in range(4):
        ins = k.mm(k.ps[:, b + 1, 0:32], k.ones, e2[:, j, :], j == 0, j == 3)
    t = PE(ins)
    rank = k.ps[:, b, 0:128].rearrange("p (a e) -> p a e", a=4)
    two = lambda j: s[:, j, :].rearrange("p (k a) -> p k a", k=2)
    rk, eid, obk, q, blk, u1 = (two(j) for j in (6, 7, 8, 9, 10, 11))
    cnt, nob, end = (nb[:, j, :] for j in range(3))
    t1 = k.cp(V, cnt, k.ps[:, b + 1, 0:32], t)
    for c in range(2):
        t = k.tt(V, ee, oh[:, c], rank, MUL, t, t1)
        t = red(rk[:, c, :], ee, ADD, t)
    k.give(t, b, b + 1)
    t = k.ts(V, nob, cnt, 64.0, None, ALU.is_gt, None, t)
    for n in range(2, 8):
        t = k.stt(V, nob, cnt, 64.0 * n, nob, ALU.is_gt, ADD, t)
    V.wait(t)
    t = V(nc.vector.tensor_tensor_scan(end, k.ones[:, 0:32], nob, 0.0, MUL, ADD))
    t = k.tt(V, nob, end, nob, SUB, t)
    for c in range(2):
        t = k.tt(V, ee, oh[:, c], row(nob, 32), MUL, t)
        t = red(obk[:, c, :], ee, ADD, t)
        t = k.tt(V, ee, oh[:, c], row(iota, 32), MUL, t)
        t = red(eid[:, c, :], ee, ADD, t)
    f = lambda j: s[:, j, :]
    t = k.ts(V, f(9), f(6), 64.0, None, ALU.is_ge, None, t)
    for n in range(2, 8):
        t = k.stt(V, f(9), f(6), 64.0 * n, f(9), ALU.is_ge, ADD, t)
    t = k.stt(V, f(6), f(9), -64.0, f(6), MUL, ADD, t)
    t = k.tt(V, f(11), f(9), f(8), ADD, t)
    t = k.stt(V, f(11), f(11), NE - 1.0, f(7), ADD, SUB, t)
    t = k.ts(V, f(10), f(9), 1.0, None, ALU.min, None, t)
    t = k.tt(V, f(10), f(10), f(11), MUL, t)
    t = k.tt(V, f(10), f(10), f(7), ADD, t)
    t_d = k.stt(V, dst.rearrange("p a c -> p (a c)"), f(10), 64.0, f(6), MUL, ADD, t)
    for j in range(8):
        ta = k.ts(V, R[:, j, :], iota, f(6)[:, j:j + 1], None, ALU.is_equal, None, t)
        tb = k.ts(V, B[:, j, :], iota[:, 0:NBLK], f(10)[:, j:j + 1], k.con["tok"][:, j % 4:j % 4 + 1],
                  ALU.is_equal, MUL)
    PE.wait(tb)
    b = k.pair()
    for j in range(8):
        ins = k.mm(k.ps[0:64, b, 0:NBLK], R[:, j, :], B[:, j, :], j == 0, j == 7)
    tp = PE(ins)
    t_i = k.cp(V, idx, k.ps[0:64, b, 0:NBLK], tp)
    k.give(t_i, b, b + 1)
    t = k.tt(V, cmp_, end[0:1].unsqueeze(1).to_broadcast([1, NOV, 32]),
             iota[0:1, 0:NOV].unsqueeze(2).to_broadcast([1, NOV, 32]), ALU.is_le, t)
    t = red(ovf, cmp_, ADD, t)
    t = k.ts(V, ov[:, 1:1 + NOV], ovf, NE - 1.0, None, ALU.min, None, t)
    t_o = k.cp(V, ov[:, 0:1], end[0:1, 31:32], t)
    return gate, dst, idx, ov, [t_gate, t_d, t_i, t_o]


def expert_rows(k, xg, tg, xS, free):
    PE = k.PE
    PE.wait(tg)
    b = k.pair(4)
    for x in range(8):
        ins = k.tr(k.ps[:, b, 64 * x:64 * x + 64], xg[:, 128 * x:128 * x + 128])
    t = PE(ins)
    tx = part(k, k.ps[:, b, :].rearrange("p (a c) -> p a c", a=8), xS[:, :, 0:64], xS[:, :, 64:128], t, free)
    k.give(tx, b, b + 1)
    return t, tx


def expert_in(k, W, xS, tx, tmp, act, free):
    nc, V, A, PE = k.nc, k.V, k.A, k.PE
    b = k.pair(4)
    PE.wait(tx)
    ts = []
    for c in range(2):
        for p in range(4):
            i, wh, wl = W.get()
            for y in range(2):
                for w in (wh, wl):
                    ins = k.mm(k.ps[:, b + c, :], xS[:, 2 * p + y, :], w[:, 512 * y:512 * y + 512],
                               p == 0 and y == 0 and w is wh, p == 3 and y == 1 and w is wl)
            t = PE(ins)
            W.done(i)
        t = k.cp(A, tmp[:, c, :], k.ps[64:128, b + c, :], t, free)
        t = k.tt(V, act[:, c, :], k.ps[0:64, b + c, :], tmp[:, c, :], ADD, t, free)
        ts.append(t)
        if c == 0:
            ta = k.act(tmp[:, 0, :], act[:, 0, :], ACT.Silu, t)
    th = k.tt(V, act[:, 0, :], tmp[:, 0, :], act[:, 1, :], MUL, t, ta)
    k.give(ts, b, b + 1)
    return th


def expert_turn(k, act, th, hS, free):
    b = k.pair(4)
    k.PE.wait(th)
    for x in range(4):
        ins = k.tr(k.ps[:, b, 64 * x:64 * x + 64], act[:, 0, 128 * x:128 * x + 128])
    t = k.PE(ins)
    tx = part(k, k.ps[:, b, 0:256].rearrange("p (a c) -> p a c", a=4), hS[:, :, 0:64], hS[:, :, 64:128], t, free)
    k.give(tx, b, b + 1)
    return t, tx


def expert_out(k, W, hS, th, tmp, yb, free):
    nc, V, A, PE = k.nc, k.V, k.A, k.PE
    b = k.pair(4)
    PE.wait(th)
    ts = []
    for c in range(2):
        for p in range(2):
            i, wh, wl = W.get()
            for y in range(2):
                for w in (wh, wl):
                    ins = k.mm(k.ps[:, b + c, :], hS[:, 2 * p + y, :], w[:, 512 * y:512 * y + 512],
                               p == 0 and y == 0 and w is wh, p == 1 and y == 1 and w is wl)
            t = PE(ins)
            W.done(i)
        tp = t
        t = k.cp(A, tmp[:, c, :], k.ps[64:128, b + c, :], t, free)
        ts.append(k.tt(V, yb[:, 512 * c:512 * c + 512], k.ps[0:64, b + c, :], tmp[:, c, :], ADD, t, free))
    k.give(ts, b, b + 1)
    return tp, ts


def moe(k):
    nc, V, A, G, PE = k.nc, k.V, k.A, k.G, k.PE
    uT, hT = k.uT, k.hT
    vrow = nc.dram_tensor("vrow", [S, D], F32, kind="Internal").ap()
    ys = k.ys
    with ExitStack() as st:
        def sb(name, shape, dt=F32):
            return st.enter_context(nc.sbuf_tensor(name, shape, dt)).ap()

        tv = rms(k, hT, [k.vec["ffn"][:, i:i + 1] for i in range(8)], uT, NM, k.ld_h)
        with ExitStack() as st0:
            vt = st0.enter_context(nc.sbuf_tensor("vt", [128, 2, D], F32)).ap()
            dv = [Dma(nc, "vr0"), Dma(nc, "vr1")]
            tok = [None, None]
            PE.wait(tv)
            for i in range(4):
                b = k.pair()
                for x in range(8):
                    ins = k.tr(k.ps[:, b + x // 4, 128 * (x % 4):128 * (x % 4) + 128],
                               uT[:, x, NM + 128 * i:NM + 128 * i + 128])
                t = PE(ins)
                t1 = k.cp(A, vt[:, i % 2, 0:512], k.ps[:, b, :], t, tok[i % 2])
                t2 = k.cp(A, vt[:, i % 2, 512:1024], k.ps[:, b + 1, :], t, tok[i % 2])
                k.give(t2, b, b + 1)
                G.wait(t1, t2, tok[i % 2])
                tok[i % 2] = dv[i % 2](nc.gpsimd.dma_start(vrow[128 * i:128 * i + 128, :], vt[:, i % 2, :]))
            for q in (V, A, PE, G):
                q.wait(tok)
        gate, dst, idx, ov, rt = route(k, sb, uT, tv)
        G.wait(rt, tok)
        with ExitStack() as st2:
            def sb2(name, shape, dt=F32):
                return st2.enter_context(nc.sbuf_tensor(name, shape, dt)).ap()

            xg = sb2("xg", [64, 4, D])
            xS = sb2("exS", [128, 2, 8, 128], F32R)
            hS = sb2("ehS", [128, 2, 4, 128], F32R)
            tmp = sb2("etmp", [64, 2, 512])
            tmo = sb2("etmo", [64, 2, 512])
            ac = sb2("eact", [64, 2, 2, 512])
            yb = sb2("yb", [64, 2, D])
            dg = [Dma(nc, f"xg{i}") for i in range(4)]
            dy = [Dma(nc, f"yb{i}") for i in range(2)]
            W = Halves(k, st2, "e", 5, [(1024, i % 2) for i in range(12 * NE)], 4)

            def gather(e, free):
                G.wait(free)
                return dg[e % 4](nc.gpsimd.indirect_dma_start(
                    out=xg[:, e % 4, :], out_offset=None, in_=vrow,
                    in_offset=bass.IndirectOffsetOnAxis(ap=idx[:, e:e + 1], axis=0),
                    bounds_check=S - 1, oob_is_err=False))

            tg = [gather(e, None) for e in range(4)]
            ty = [None] * 2
            turned = [None, None]
            hfree = [None, None]
            th = [None, None]
            gone, rows = [], []
            rows.append(expert_rows(k, xg[:, 0, :], tg[0], xS[:, 0], None))
            out = None
            for e in range(NE + 1):
                if e < NE:
                    if e + 4 < NE:
                        tg.append(gather(e + 4, rows[e][0]))
                    th[e % 2] = expert_in(k, W, xS[:, e % 2], rows[e][1], tmp, ac[:, e % 2],
                                          [turned[e % 2], th[(e + 1) % 2]])
                    gone.append(PE.last())
                if e + 1 < NE:
                    rows.append(expert_rows(k, xg[:, (e + 1) % 4, :], tg[e + 1], xS[:, (e + 1) % 2],
                                            gone[e - 1] if e else None))
                if e:
                    i = (e - 1) % 2
                    turned[i], t = expert_turn(k, ac[:, i], th[i], hS[:, i], hfree[i])
                    hfree[i], out = expert_out(k, W, hS[:, i], t, tmo, yb[:, i, :], [ty[i], out])
                    A.wait(out)
                    r = CAP * (e - 1)
                    ty[i] = dy[i](nc.scalar.dma_start(ys[r:r + CAP, :], yb[:, i, :]))
            k.sync_all()
            G.wait(tg)
            for q in (V, PE, A, G, k.SP):
                q.wait(rt[3], ty, k.ysz)
        overflow(k, idx, ov, vrow, ys)
        with ExitStack() as st2:
            gy = st2.enter_context(nc.sbuf_tensor("gy", [128, 2, 2, D], F32)).ap()
            dc = [[Dma(nc, f"gy{i}{c}") for c in range(2)] for i in range(2)]
            free = [None, None]
            for i in range(4):
                j = i % 2
                tc = []
                for c in range(2):
                    G.wait(free[j])
                    tc.append(dc[j][c](nc.gpsimd.indirect_dma_start(
                        out=gy[:, j, c, :], out_offset=None, in_=ys,
                        in_offset=bass.IndirectOffsetOnAxis(ap=dst[:, c, i:i + 1], axis=0),
                        bounds_check=NBLK * CAP - 1, oob_is_err=False)))
                t = k.ts(V, gy[:, j, 0, :], gy[:, j, 0, :], gate[:, 0, i:i + 1], None, MUL, None, tc[0])
                t = k.stt(V, gy[:, j, 0, :], gy[:, j, 1, :], gate[:, 1, i:i + 1], gy[:, j, 0, :], MUL, ADD, t, tc[1])
                PE.wait(t)
                for g in range(2):
                    b = k.pair()
                    for x in range(4):
                        ins = k.tr(k.ps[:, b, 128 * x:128 * x + 128],
                                   gy[:, j, 0, 512 * g + 128 * x:512 * g + 128 * x + 128])
                    t = PE(ins)
                    h = hT[:, 4 * g:4 * g + 4, NM + 128 * i:NM + 128 * i + 128]
                    th = k.tt(V, h, h, k.ps[:, b, :].rearrange("p (a c) -> p a c", a=4), ADD, t)
                    k.give(th, b, b + 1)
                free[j] = t
            k.sync_all()


def sem_number(sem):
    return sem.num


def overflow(k, idx, ov, vrow, ys):
    nc = k.nc
    with ExitStack() as st:
        def sb(name, shape, dt=F32):
            return st.enter_context(nc.sbuf_tensor(name, shape, dt)).ap()

        wo = sb("ovw", [128, 4, SLOT])
        ix = sb("ovi", [64, 1], U32)
        xg = sb("ovx", [64, D])
        xT = sb("ovxT", [128, 8, 64])
        hb = sb("ovh", [64, 2, 512])
        hT = sb("ovhT", [128, 4, 64])
        yb = sb("ovy", [64, D])
        before = k.PE, k.V, k.A, k.G, k.SP, k.bank
        k.PE, k.V, k.A, k.G, k.SP = (Queue(nc, e, "o" + n) for e, n in (
            (nc.tensor, "pe"), (nc.vector, "v"), (nc.scalar, "a"), (nc.gpsimd, "g"), (nc.sync, "sp")))
        PE, V, A = k.PE, k.V, k.A
        d = [Dma(nc, f"ov{i}") for i in range(8)]
        count = nc.values_load(ov[0:1, 0:1], min_val=0, max_val=NOV - 1)
        with nc.Fori(0, NOV) as j:
            with nc.If(j < count):
                e = nc.sync.value_load(ov[0:1, bass.ds(j + 1, 1)], min_val=0, max_val=NE - 1)
                tw = []

                def load(c):
                    src = k.a["w_ein"][bass.ds(e, 1), c] if c < 4 else k.a["w_eout"][bass.ds(e, 1), c - 4]
                    tw.append(d[c](nc.sync.dma_start(wo[:, c % 4, :], src.rearrange("a p m -> (a p) m"))))

                for c in range(4):
                    load(c)
                t = k.cp(V, ix, idx[:, bass.ds(j + NE, 1)])
                k.G.wait(t)
                tg = d[6](nc.gpsimd.indirect_dma_start(
                    out=xg, out_offset=None, in_=vrow,
                    in_offset=bass.IndirectOffsetOnAxis(ap=ix, axis=0), bounds_check=S - 1, oob_is_err=False))
                PE.wait(tg)
                for x in range(8):
                    ins = k.tr(k.ps[:, 0, 64 * x:64 * x + 64], xg[:, 128 * x:128 * x + 128])
                t = PE(ins)
                tx = k.cp(V, xT.rearrange("p a c -> p (a c)"), k.ps[:, 0, :], t)
                PE.wait(tx)
                for c in range(4):
                    PE.wait(tw[c])
                    for x in range(4):
                        ins = k.mm(k.ps[0:64, 1 + c // 2, :], xT[:, 4 * (c % 2) + x, :],
                                   wo[:, c, 512 * x:512 * x + 512], c % 2 == 0 and x == 0, c % 2 == 1 and x == 3)
                    t = PE(ins)
                    if c < 2:
                        k.SP.wait(t)
                        load(4 + c)
                    if c == 1:
                        ta = k.act(hb[:, 0, :], k.ps[0:64, 1, :], ACT.Silu, t)
                th = k.tt(V, hb[:, 1, :], hb[:, 0, :], k.ps[0:64, 2, :], MUL, t, ta)
                PE.wait(th)
                for x in range(4):
                    ins = k.tr(k.ps[:, 3, 64 * x:64 * x + 64], hb[:, 1, 128 * x:128 * x + 128])
                t = PE(ins)
                th = k.cp(V, hT.rearrange("p a c -> p (a c)"), k.ps[:, 3, 0:256], t)
                PE.wait(th)
                for c in range(2):
                    PE.wait(tw[4 + c])
                    for x in range(4):
                        ins = k.mm(k.ps[0:64, 4 + c, :], hT[:, x, :], wo[:, c, 512 * x:512 * x + 512], x == 0, x == 3)
                    t = PE(ins)
                    t = k.cp(V, yb[:, 512 * c:512 * c + 512], k.ps[0:64, 4 + c, :], t)
                k.SP.wait(t)
                t = d[7](nc.sync.dma_start(ys[bass.ds(j * CAP + NE * CAP, CAP), :], yb))
                k.SP.wait(t)
                nc.all_engine_barrier()
                n = sem_number(d[6].sem)
                nc.gpsimd.dma_reset(range(n, n + 1))
                nc.gpsimd.sem_clear(d[6].sem)
                for q in (k.PE, k.V, k.A, k.G, k.SP):
                    if q.n:
                        nc.sync.sem_clear(q.sem)
                for x in d[:6] + d[7:]:
                    nc.sync.sem_clear(x.sem)
                nc.all_engine_barrier()
        nc.all_engine_barrier()
        k.PE, k.V, k.A, k.G, k.SP, k.bank = before


def block1_end(k):
    m2 = Dma(k.nc, "m2")
    k.G.wait(k.V.last())
    t2 = m2(k.nc.gpsimd.dma_start(k.hT[:, :, 0:NM], k.a["m2T"]))
    t = rms(k, k.hT, [k.vec["fin"][:, i:i + 1] for i in range(8)], k.hT, NM, k.V.last())
    return [t, t2]


def post(k, y, w, r0, half, after):
    V = k.V
    t = rms(k, y, w, y, r0, after)
    for m in range(8):
        if half:
            t1 = k.stt(V, k.hT[:, m, r0:L], y[:, m, r0:L], 0.5, k.hT[:, m, r0:L], MUL, ADD, t)
        else:
            t1 = k.tt(V, k.hT[:, m, r0:L], k.hT[:, m, r0:L], y[:, m, r0:L], ADD, t)
    return t1


def ffn(k, r0, w0, w1, after):
    nc, V, A, PE = k.nc, k.V, k.A, k.PE
    n = L - r0
    with ExitStack() as st:
        def sb(name, shape, dt=F32):
            return st.enter_context(nc.sbuf_tensor(f"{name}{r0}", shape, dt)).ap()

        uh = sb("fuh", [128, 8, L], F32R)
        ul = sb("ful", [128, 8, L], F32R)
        hh = sb("fhh", [128, 10, L], F32R)
        hl = sb("fhl", [128, 10, L], F32R)
        sg = sb("fsg", [128, 2, L])
        y = k.uT
        sizes = []
        for g in range(3):
            t = min(8, 22 - 8 * g)
            sizes += [(1024, False), (1024, True)] * t + [(128 * t, False), (128 * t, True)] * 4
        W = Halves(k, st, f"f{r0}", 3, sizes)
        two = (lambda x: x.rearrange("p (a c) -> p a c", a=2)) if n > 512 else (lambda x: x)
        acc = (lambda b: k.wide(b)) if n > 512 else (lambda b: k.ps[:, b, 0:n])
        tu = rms(k, k.hT, w0, k.uT, r0, after)
        for m in range(8):
            tu = part(k, k.uT[:, m, r0:L], uh[:, m, r0:L], ul[:, m, r0:L], tu)
        PE.wait(tu)
        v3 = lambda w, c: [w[:, 128 * x:128 * x + 128] for x in range(c)]
        free = [None, None]
        hfree = {}
        for g in range(3):
            nt = min(8, 22 - 8 * g)
            for j in range(8 * g, 8 * g + nt):
                bs = []
                for x in range(2):
                    i, wh, wl = W.get()
                    b = k.pair(4)
                    bs.append((b, linear3(k, b, v3(wh, 8), v3(wl, 8), tiles(uh, 8), tiles(ul, 8), r0, L)))
                    W.done(i)
                (b, t), (b2, t2) = bs
                ts = k.act(two(sg[:, j % 2, r0:L]), acc(b), ACT.Silu, t, free[j % 2])
                k.give(ts, b, b + 1)
                tv = k.tt(V, two(sg[:, j % 2, r0:L]), acc(b2), two(sg[:, j % 2, r0:L]), MUL, t2, ts)
                k.give(tv, b2, b2 + 1)
                free[j % 2] = part(k, sg[:, j % 2, r0:L], hh[:, j % 10, r0:L], hl[:, j % 10, r0:L], tv,
                                   hfree.get(j - 10))
            PE.wait(free)
            for m in range(8):
                i, wh, wl = W.get()
                b = k.pair(4)
                xs = [(8 * g + x) % 10 for x in range(nt)]
                t = linear3(k, b, v3(wh, nt), v3(wl, nt), [hh[:, x, :] for x in xs], [hl[:, x, :] for x in xs], r0, L)
                W.done(i)
                if g == 0:
                    ty = k.cp(V, two(y[:, m, r0:L]), acc(b), t)
                else:
                    ty = k.tt(V, two(y[:, m, r0:L]), acc(b), two(y[:, m, r0:L]), ADD, t, ytok[m])
                if m == 0:
                    ytok = {} if g == 0 else ytok
                ytok[m] = ty
                k.give(ty, b, b + 1)
            for x in range(nt):
                hfree[8 * g + x] = PE.last()
        t = post(k, y, w1, r0, True, [V.last(), A.last()])
        k.sync_all()
    return t


def conv(k, out, xb, w, tx, free):
    V = k.V
    t = k.ts(V, out, xb[:, 0:L], w[0], None, MUL, None, tx, free)
    t = k.stt(V, out, xb[:, 1:L + 1], w[1], out, MUL, ADD, t)
    return k.stt(V, out, xb[:, 2:L + 2], w[2], out, MUL, ADD, t)


def conv_fourier(k, sc, fo, tu):
    nc, V, A, G, PE = k.nc, k.V, k.A, k.G, k.PE
    uT = k.uT
    two = lambda x: x.rearrange("p (a c) -> p a c", a=2)
    with ExitStack() as st:
        def sb(name, shape):
            return st.enter_context(nc.sbuf_tensor(name, shape, F32)).ap()

        xb = sb("cxb", [128, 2, L + 2])
        bt = sb("cbt", [128, 2, L])
        ct = sb("cct", [128, 2, L])
        uf = sb("cuf", [128, 2, L])
        cs = sb("ccs", [C2, NC2, 4, 256])
        dfs = sb("dfs", [128, 256])
        dft = sb("dft", [128, NC2, 2, L])
        d = [Dma(nc, f"df{i}") for i in range(NC2 + 1)]
        A.wait(k.V.last(), k.PE.last())
        td = [d[i](nc.scalar.dma_start(dft[:, i].rearrange("p a c -> p (a c)"), k.a["dft"][i])) for i in range(NC2)]
        ts_ = d[NC2](nc.scalar.dma_start(dfs, k.a["dfs"]))
        tz = V(nc.vector.memset(xb, 0.0))
        PE.wait(tu)
        hist = []
        tcs = []
        for j in range(4):
            i = j % 2
            old = hist[j - 2] if j >= 2 else (None, None, None)
            c, w = k.weight()
            wv = w.rearrange("p (t c) -> p t c", t=8)
            b = k.pair()
            t = linear(k, b, [wv[:, x, 0:128] for x in range(8)], tiles(uT, 8), 0, L)
            tb = k.cp(A, two(bt[:, i]), k.wide(b), t, old[0])
            k.give(tb, b, b + 1)
            b = k.pair()
            t = linear(k, b, [wv[:, x, 128:256] for x in range(8)], tiles(uT, 8), 0, L)
            k.release(c)
            tc = k.cp(A, two(ct[:, i]), k.wide(b), t, old[1])
            k.give(tc, b, b + 1)
            c, w = k.weight()
            wv = w.rearrange("p (t c) -> p t c", t=8)
            b = k.pair()
            t = linear(k, b, [wv[:, x, 0:128] for x in range(8)], tiles(uT, 8), 0, L)
            tx = k.tt(V, two(xb[:, i, 1:L + 1]), k.wide(b), two(ct[:, i]), MUL, t, tc, tz, old[0])
            k.give(tx, b, b + 1)
            b = k.pair()
            t = linear(k, b, [wv[:, x, 128:256] for x in range(8)], tiles(uT, 8), 0, L)
            k.release(c)
            tf = k.cp(A, two(uf[:, i]), k.wide(b), t, old[2])
            k.give(tf, b, b + 1)
            wv = [k.vec["sc"][:, 4 * x + j:4 * x + j + 1] for x in range(3)]
            t = conv(k, sc[:, j, :], xb[:, i], wv, tx, None)
            t = k.tt(V, sc[:, j, :], sc[:, j, :], bt[:, i], MUL, t, tb)
            PE.wait(tf, ts_)
            for g in range(3):
                b = k.pair()
                for h in range(2):
                    n = 2 * g + h
                    tp = PE(k.mm(k.ps[0:C2, b + h, 0:256], uf[:, i, C2 * n:C2 * n + C2], dfs, True, True))
                ta = k.cp(V, cs[:, 2 * g:2 * g + 2, j, :], k.ps[0:C2, b:b + 2, 0:256], tp)
                k.give(ta, b, b + 1)
            tcs.append(ta)
            hist.append((t, tx, tp))
        PE.wait(tcs, td)
        for j in range(4):
            b = k.pair()
            for n in range(NC2):
                for p in range(2):
                    for h, (c0, c1) in enumerate(split(0, L)):
                        ins = k.mm(k.ps[:, b + h, 0:HF], cs[:, n, j, 128 * p:128 * p + 128],
                                   dft[0:C2, n, p, c0:c1], n == 0 and p == 0, n == NC2 - 1 and p == 1)
            t = PE(ins)
            t = k.cp(A, two(fo[:, j, :]), k.wide(b), t)
            k.give(t, b, b + 1)
        k.sync_all()


def deltanet(k, dn, tu):
    nc, V, A, G, PE = k.nc, k.V, k.A, k.G, k.PE
    uT = k.uT
    two = lambda x: x.rearrange("p (a c) -> p a c", a=2)
    six = lambda x: x.rearrange("p (n c) -> p n c", n=NC2)
    chunk = lambda b, n, p=128: k.ps[0:p, b + n // 3, C2 * (n % 3):C2 * (n % 3) + C2]
    with ExitStack() as st:
        def sb(name, shape):
            return st.enter_context(nc.sbuf_tensor(name, shape, F32)).ap()

        lv = sb("lv2", [128, 2, 7, 128])
        dl = Dma(nc, "lv2")
        A.wait(V.last(), PE.last())
        tlv = dl(nc.scalar.dma_start(lv.rearrange("p a b c -> p (a b c)"), k.a["lv2"]))
        g_ = sb("ng", [C2, NC2, 8])
        be = sb("nbe", [C2, NC2, 8])
        tmp = sb("ntm", [C2, 2, NC2, 8])
        gc = sb("ngc", [C2, NC2, 8])
        eg = sb("neg", [C2, NC2, 8])
        el = sb("nel", [C2, NC2, 8])
        bg = sb("nbg", [C2, NC2, 8])
        ea = sb("nea", [128, 8])
        xb = sb("nxb", [128, 2, L + 2])
        qkv = sb("nqkv", [128, 3, L])
        z_ = sb("nz", [128, L])
        kt = sb("nkt", [C2, NC2, 128])
        vt = sb("nvt", [C2, NC2, 128])
        KK = sb("nKK", [C2, 2, L])
        of = xb[:, 0, 1:L + 1]
        EG = sb("nEG", [128, 2, L])
        DT = sb("nDT", [C2, 2, L])
        MT = sb("nMT", [C2, 2, L])
        AT = DT
        wT = sb("nT", [128, 2, L])
        T = wT[0:C2]
        TT = sb("nTT", [C2, 2, L])
        CP = sb("nCP", [C2, 4, L])
        Cl, P1 = CP[:, 0:2, :], CP[:, 2:4, :]
        u_ = CP.rearrange("p a c -> p (a c)")[:, 0:2 * NC2 * 128].rearrange("p (a n c) -> p a n c", a=2, n=NC2)
        vb = sb("nvb", [C2, 2, NC2, 128])
        kb = sb("nkb", [C2, 2, NC2, 128])
        kdec = sb("nkd", [C2, 2, NC2, 128])
        vn = sb("nvn", [C2, 2, 2, 128])
        Sd = sb("nSd", [128, 2, 128])
        PE.wait(tu, k.ld_wba)
        b = k.pair()
        for n in range(NC2):
            for x in range(8):
                ins = k.mm(k.ps[0:C2, b, 16 * n:16 * n + 16], uT[:, x, C2 * n:C2 * n + C2], k.wba[:, x, :],
                           x == 0, x == 7)
        t = PE(ins)
        src = k.ps[0:C2, b, 0:96].rearrange("p (n c) -> p n c", n=NC2)
        t0 = k.act(be, src[:, :, 0:8], ACT.Sigmoid, t)
        x_, y_ = tmp[:, 0], tmp[:, 1]
        t = k.tt(V, x_, src[:, :, 8:16], k.vec["dt"][0:C2].unsqueeze(1).to_broadcast([C2, NC2, 8]), ADD, t0)
        k.give([t, t0], b, b + 1)
        ta = k.act(y_, x_, ACT.Abs, t)
        ta = k.act(y_, y_, ACT.Exp, ta, scale=-1.0)
        ta = k.act(y_, y_, ACT.Ln, ta, bias=1.0)
        t = k.stt(V, x_, x_, 0.0, y_, MAX, ADD, ta)
        te = k.act(ea, k.vec["al"], ACT.Exp)
        t = k.stt(V, g_, x_, -1.0, ea[0:C2].unsqueeze(1).to_broadcast([C2, NC2, 8]), MUL, MUL, t, te)
        PE.wait(t)
        b = k.pair()
        gf = g_.rearrange("p n c -> p (n c)")
        one = k.ones[0:C2, 0:C2]
        k.mm(k.ps[0:C2, b, 0:48], k.con["ui"][0:C2, 0:C2], gf, True, True)
        k.mm(k.ps[0:C2, b, 48:96], k.con["li"][0:C2, 0:C2], gf, True, True)
        t = PE(k.mm(k.ps[0:C2, b, 96:144], one, gf, True, True))
        v8 = lambda o: k.ps[0:C2, b, o:o + 48].rearrange("p (n c) -> p n c", n=NC2)
        t1 = k.cp(V, gc[:, :, 0:4], v8(0)[:, :, 0:4], t)
        t1 = k.cp(V, gc[:, :, 4:8], v8(48)[:, :, 4:8], t)
        t2 = k.tt(V, el, v8(96), gc, SUB, t1)
        k.give(t2, b, b + 1)
        ta = k.act(el, el, ACT.Exp, t2)
        ta = k.act(eg, gc, ACT.Exp, t1)
        tcol = k.tt(V, bg, be, eg, MUL, ta, t0)
        tz = V(nc.vector.memset(xb, 0.0))
        free = {}
        PE.wait(tcol, tlv)
        for h in range(4):
            tok = []
            for j in range(4):
                if j % 2 == 0:
                    c, w = k.weight()
                    wv = w.rearrange("p (t c) -> p t c", t=8)
                b = k.pair()
                o = 128 * (j % 2)
                t = linear(k, b, [wv[:, x, o:o + 128] for x in range(8)], tiles(uT, 8), 0, L)
                if j % 2:
                    k.release(c)
                if j == 3:
                    tz_ = k.act(two(z_), k.wide(b), ACT.Silu, t, free.get("z"))
                    k.give(tz_, b, b + 1)
                    break
                t = k.cp(A, two(xb[:, j % 2, 1:L + 1]), k.wide(b), t, tz, free.get(("xb", j % 2)))
                k.give(t, b, b + 1)
                wc = [k.vec["dc"][:, 12 * x + 4 * j + h:12 * x + 4 * j + h + 1] for x in range(3)]
                t = conv(k, qkv[:, j, :], xb[:, j % 2], wc, t, free.get(("qkv", j)))
                free[("xb", j % 2)] = t
                tok.append(k.act(qkv[:, j, :], qkv[:, j, :], ACT.Silu, t))
            for j in range(2):
                t = k.act(k.sq[:, j, :], qkv[:, j, :], ACT.Square, tok[j], k.sqfree[j])
                PE.wait(t)
                b = k.pair()
                for x, (c0, c1) in enumerate(split(0, L)):
                    ins = k.mm(k.ps[:, b + x, 0:HF], k.ones, k.sq[:, j, c0:c1], True, True)
                t = PE(ins)
                k.sqfree[j] = t
                t = k.act(two(k.rb), k.wide(b), ACT.Sqrt, t, k.rbfree, bias=k.eps[:, 0:1])
                k.give(t, b, b + 1)
                V.wait(t)
                t = V(nc.vector.reciprocal(k.rb, k.rb))
                tok[j] = k.stt(V, qkv[:, j, :], qkv[:, j, :], 128.0 ** -0.5 if j == 0 else 1.0, k.rb, MUL, MUL, t)
                k.rbfree = tok[j]
            q_, k_, v_ = (qkv[:, j, :] for j in range(3))
            tm = []
            for dst, src, tk in ((kt, k_, tok[1]), (vt, v_, tok[2])):
                PE.wait(tk)
                for g in range(2):
                    b = k.pair()
                    for n in range(3):
                        ins = k.tr(k.ps[0:C2, b, 128 * n:128 * n + 128], src[:, C2 * (3 * g + n):C2 * (3 * g + n) + C2])
                    t = PE(ins)
                    t = k.cp(V, dst[:, 3 * g:3 * g + 3, :].rearrange("p a c -> p (a c)"), k.ps[0:C2, b, 0:384], t)
                    k.give(t, b, b + 1)
                    tm.append(t)
            PE.wait(tok[0])
            for x, other in enumerate((k_, q_)):
                b = k.pair()
                for n in range(NC2):
                    ins = k.mm(chunk(b, n, C2), k_[:, C2 * n:C2 * n + C2], other[:, C2 * n:C2 * n + C2], True, True)
                t = PE(ins)
                tkk = k.cp(V if x else A, two(KK[:, x, :]), k.ps[0:C2, b:b + 2, 0:HF], t, free.get(("KK", x)))
                k.give(tkk, b, b + 1)
                tm.append(tkk)
            D = [dict(), dict()]
            for d in range(2):
                s = D[d]
                hh = 4 * d + h
                tri = k.con["ui" if d == 0 else "li"][0:C2, 0:C2]
                b = k.pair()
                PE.wait(tcol)
                for n in range(NC2):
                    ins = k.mm(chunk(b, n), g_[:, n, hh:hh + 1].to_broadcast([C2, 128]), tri, True, True)
                t = PE(ins)
                s["EG"] = k.act(two(EG[:, d, :]), k.wide(b), ACT.Exp, t)
                mask = k.con["mf" if d == 0 else "mb"][0:C2, 0:C2]
                for n in range(NC2):
                    t1 = k.stt(V, DT[:, d, C2 * n:C2 * n + C2], chunk(b, n, C2), gc[:, n, hh:hh + 1], mask, SUB, ADD, s["EG"])
                k.give([s["EG"], t1], b, b + 1)
                t1 = k.act(DT[:, d, :], DT[:, d, :], ACT.Exp, t1)
                b = k.pair()
                for n in range(NC2):
                    ins = k.mm(chunk(b, n, C2), be[:, n, hh:hh + 1].to_broadcast([C2, C2]), k.ident[0:C2, 0:C2],
                               True, True)
                t = PE(ins)
                t2 = k.tt(V, two(MT[:, d, :]), k.ps[0:C2, b:b + 2, 0:HF], two(DT[:, d, :]), MUL, t, t1)
                k.give(t2, b, b + 1)
                s["MT"] = k.tt(V, MT[:, d, :], MT[:, d, :], KK[:, 0, :], MUL, t2, tm)
                s["AT"] = k.tt(V, AT[:, d, :], DT[:, d, :], KK[:, 1, :], MUL, t2, tm)
                for n in range(NC2):
                    k.ts(V, vb[:, d, n, :], vt[:, n, :], be[:, n, hh:hh + 1], None, MUL, None, tm)
                    k.ts(V, kb[:, d, n, :], kt[:, n, :], bg[:, n, hh:hh + 1], None, MUL)
                    s["cols"] = k.ts(V, kdec[:, d, n, :], kt[:, n, :], el[:, n, hh:hh + 1], None, MUL)
                lvl = lambda m: lv[0:C2, d, m, 0:C2].unsqueeze(1).to_broadcast([C2, NC2, C2])
                t = k.tt(V, six(TT[:, d, :]), six(MT[:, d, :]), lvl(0), MUL, s["MT"])
                idn = k.ident[0:C2, 0:C2].unsqueeze(1).to_broadcast([C2, NC2, C2])
                t = k.tt(V, six(TT[:, d, :]), idn, six(TT[:, d, :]), SUB, t)
                PE.wait(t)
                b = k.pair()
                for n in range(NC2):
                    ins = k.tr(chunk(b, n, C2), TT[:, d, C2 * n:C2 * n + C2])
                t = PE(ins)
                s["T"] = k.cp(A, two(T[:, d, :]), k.ps[0:C2, b:b + 2, 0:HF], t)
                k.give(s["T"], b, b + 1)
            at = lambda X, d, n: X[:, d, C2 * n:C2 * n + C2]
            pv = lambda b: k.ps[0:C2, b:b + 2, 0:HF]
            for m in range(1, 7):
                for d in range(2):
                    s = D[d]
                    t = k.tt(V, six(Cl[:, d, :]), six(MT[:, d, :]),
                             lv[0:C2, d, m, 0:C2].unsqueeze(1).to_broadcast([C2, NC2, C2]), MUL, s.get("mm1"))
                    PE.wait(t, s["T"])
                    b = k.pair()
                    for n in range(NC2):
                        ins = k.mm(chunk(b, n, C2), at(Cl, d, n), at(T, d, n), True, True)
                    s["mm1"] = PE(ins)
                    s["P1"] = k.cp(A, two(P1[:, d, :]), pv(b), s["mm1"], s.get("mm2"))
                    k.give(s["P1"], b, b + 1)
                for d in range(2):
                    s = D[d]
                    PE.wait(s["P1"])
                    b = k.pair()
                    for n in range(NC2):
                        ins = k.mm(chunk(b, n, C2), at(P1, d, n), at(TT, d, n), True, True)
                    t = PE(ins)
                    if m < 6:
                        b2 = k.pair()
                        for n in range(NC2):
                            ins = k.mm(chunk(b2, n, C2), at(TT, d, n), at(P1, d, n), True, True)
                        t2 = PE(ins)
                        s["mm2"] = t2
                        s["T"] = k.tt(V, two(T[:, d, :]), two(T[:, d, :]), pv(b2), SUB, t2, s["mm1"])
                        k.give(s["T"], b2, b2 + 1)
                        t = t2
                    s["T"] = k.tt(V, two(TT[:, d, :]), two(TT[:, d, :]), pv(b), SUB, t)
                    k.give(s["T"], b, b + 1)
            for d in range(2):
                s = D[d]
                PE.wait(s["T"], s["cols"])
                for g in range(2):
                    b = k.pair()
                    for n in range(3):
                        ins = k.mm(k.ps[0:C2, b, 128 * n:128 * n + 128], at(TT, d, 3 * g + n), vb[:, d, 3 * g + n, :],
                                   True, True)
                    t = PE(ins)
                    s["u"] = k.cp(A, u_[:, d, 3 * g:3 * g + 3, :].rearrange("p a c -> p (a c)"),
                                  k.ps[0:C2, b, 0:384], t)
                    k.give(s["u"], b, b + 1)
                b = k.pair()
                for n in range(NC2):
                    ins = k.mm(chunk(b, n), kb[:, d, n, :], at(TT, d, n), True, True)
                t = PE(ins)
                s["w"] = k.cp(A, two(wT[:, d, :]), k.wide(b), t)
                k.give(s["w"], b, b + 1)
            tof = [None] * NC2
            for step in range(NC2):
                for d in range(2):
                    s = D[d]
                    n = step if d == 0 else NC2 - 1 - step
                    cols = slice(C2 * n, C2 * n + C2)
                    if step == 0:
                        vnew, tv = u_[:, d, n, :], s["u"]
                    else:
                        PE.wait(s["S"], s["w"])
                        b = k.pair()
                        t = PE(k.mm(k.ps[0:C2, b, 0:128], wT[:, d, cols], Sd[:, d, :], True, True))
                        tv = k.tt(V, vn[:, d, step % 2, :], u_[:, d, n, :], k.ps[0:C2, b, 0:128], SUB, t, s["u"],
                                  s.get("vfree"))
                        k.give(tv, b, b + 1)
                        vnew = vn[:, d, step % 2, :]
                    b = k.pair()
                    PE.wait(tv, s["AT"])
                    if step:
                        tq = k.tt(V, k.sq[:, d, 0:C2], q_[:, cols], EG[:, d, cols], MUL, s["EG"], s.get("o"),
                                  k.sqfree[d])
                        PE.wait(tq)
                        k.mm(k.ps[:, b, 0:C2], Sd[:, d, :], k.sq[:, d, 0:C2], True, False)
                    s["o"] = PE(k.mm(k.ps[:, b, 0:C2], vnew, AT[:, d, cols], step == 0, True))
                    if step < NC2 - 1:
                        t = PE(k.mm(k.ps[:, b + 1, 0:128], kdec[:, d, n, :], vnew, True, True))
                    s["vfree"] = PE.last()
                    if step < 3:
                        to = k.cp(A, of[:, cols], k.ps[:, b, 0:C2], s["o"])
                        tof[n] = to
                    else:
                        to = k.tt(V, of[:, cols], of[:, cols], k.ps[:, b, 0:C2], ADD, s["o"], tof[n])
                    if step < NC2 - 1:
                        if step == 0:
                            s["S"] = k.cp(V, Sd[:, d, :], k.ps[:, b + 1, 0:128], t)
                        else:
                            e = C2 * n + C2 - 1 if d == 0 else C2 * n
                            s["S"] = k.stt(V, Sd[:, d, :], Sd[:, d, :], EG[:, d, e:e + 1], k.ps[:, b + 1, 0:128],
                                           MUL, ADD, t, s["EG"])
                        k.give([to, s["S"]], b, b + 1)
                    else:
                        k.give(to, b, b + 1)
            for d in range(2):
                k.sqfree[d] = D[d]["o"]
            t = k.act(k.sq[:, 0, :], of, ACT.Square, to, k.sqfree[0])
            PE.wait(t)
            b = k.pair()
            for x, (c0, c1) in enumerate(split(0, L)):
                ins = k.mm(k.ps[:, b + x, 0:HF], k.ones128, k.sq[:, 0, c0:c1], True, True)
            t = PE(ins)
            k.sqfree[0] = t
            t = k.act(two(k.rb), k.wide(b), ACT.Sqrt, t, k.rbfree, bias=k.eps[:, 0:1])
            k.give(t, b, b + 1)
            V.wait(t)
            t = V(nc.vector.reciprocal(k.rb, k.rb))
            t = k.stt(V, k.rb, k.rb, k.vec["dn"], z_, MUL, MUL, t, tz_)
            t = k.tt(V, dn[:, h, :], of, k.rb, MUL, t)
            k.rbfree = t
            k.sync_all()


def mixer(k, w2, w3, after):
    nc, V, A, G, PE = k.nc, k.V, k.A, k.G, k.PE
    two = lambda x: x.rearrange("p (a c) -> p a c", a=2)
    tu = rms(k, k.hT, w2, k.uT, 0, after)
    with ExitStack() as st:
        def sb(name, shape):
            return st.enter_context(nc.sbuf_tensor(name, shape, F32)).ap()

        sc = sb("msc", [128, 4, L])
        fo = sb("mfo", [128, 4, L])
        dn = sb("mdn", [128, 4, L])
        conv_fourier(k, sc, fo, tu)
        deltanet(k, dn, tu)
        mg = sb("mmg", [128, 8, L])
        gt = sb("mgt", [128, 2, L])
        y = sb("my", [128, 8, L])
        gfree = [None, None]
        n = 0
        for m in range(8):
            pieces = []
            for c in range(3):
                i, w = k.weight()
                if c == 0:
                    wv = w.rearrange("p (t c) -> p t c", t=8)
                    gates = [[wv[:, x, 128 * g:128 * g + 128] for x in range(8)] for g in range(2)]
                    ops = [(gates[0], k.uT, "gf"), (gates[1], k.uT, "gs")]
                elif c == 1:
                    w8 = w[:, 0:1024].rearrange("p (t c) -> p t c", t=8)
                    wa = w[:, 1024:1536].rearrange("p (t c) -> p t c", t=4)
                    wb = w[:, 1536:2048].rearrange("p (t c) -> p t c", t=4)
                    ops = [(tiles(wa, 4), fo, "yf"), (tiles(wb, 4), sc, "ys"), (tiles(w8, 8), k.uT, "gd")]
                else:
                    wa = w[:, 0:512].rearrange("p (t c) -> p t c", t=4)
                    ops = [(tiles(wa, 4), dn, "yd")]
                for ws, x, name in ops:
                    b = k.pair()
                    t = linear(k, b, ws, tiles(x, len(ws)), 0, L)
                    if name[0] == "g":
                        j = n % 2
                        n += 1
                        t = k.act(two(gt[:, j, :]), k.wide(b), ACT.Sigmoid, t, gfree[j])
                        k.give(t, b, b + 1)
                        pieces.append((name, j, t))
                    else:
                        g, j, tg = pieces.pop(0)
                        if name == "yf":
                            t = k.tt(V, two(mg[:, m, :]), k.wide(b), two(gt[:, j, :]), MUL, t, tg)
                            gfree[j] = t
                            k.give(t, b, b + 1)
                        else:
                            t = k.tt(V, two(gt[:, j, :]), k.wide(b), two(gt[:, j, :]), MUL, t, tg)
                            k.give(t, b, b + 1)
                            t = k.tt(V, mg[:, m, :], mg[:, m, :], gt[:, j, :], ADD, t)
                            gfree[j] = t
                k.release(i)
        PE.wait(t)
        for m in range(8):
            if m % 2 == 0:
                c, w = k.weight()
                wv = w.rearrange("p (t c) -> p t c", t=8)
            b = k.pair()
            o = 128 * (m % 2)
            t = linear(k, b, [wv[:, x, o:o + 128] for x in range(8)], tiles(mg, 8), 0, L)
            if m % 2:
                k.release(c)
            ty = k.cp(A if m % 2 else V, two(y[:, m, :]), k.wide(b), t)
            k.give(ty, b, b + 1)
        t = post(k, y, w3, 0, False, [V.last(), A.last()])
        k.sync_all()
    return t


def block2(k, t):
    gain = lambda j: [k.vec["g"][:, 8 * j + i:8 * j + i + 1] for i in range(8)]
    t = ffn(k, 0, gain(0), gain(1), t)
    t = mixer(k, gain(2), gain(3), t)
    t = ffn(k, NM, gain(4), gain(5), t)
    return t


def program(nc, a, out):
    k = K(nc, a, out)
    setup(k)
    block1(k)
    moe(k)
    t = block1_end(k)
    for q in (k.V, k.A, k.PE, k.G):
        q.wait(t)
    t = block2(k, t)
    d = Dma(nc, "out")
    k.SP.wait(t, k.ysz)
    k.SP.wait(d(nc.sync.dma_start(out, k.hT[:, :, NM:L])))


def kernel(**inputs):
    import concourse.bacc as bacc
    from concourse.bass_utils import run_bass_kernel_spmd

    nc = bacc.Bacc("TRN2", target_bir_lowering=False, num_devices=1)
    arrays = {"in_" + n: v for n, v in layout(inputs).items()}
    a = {n[3:]: nc.dram_tensor(n, v.shape, mybir.dt.from_np(v.dtype), kind="ExternalInput").ap()
         for n, v in arrays.items()}
    out = nc.dram_tensor("out", (128, 8, S), F32, kind="ExternalOutput").ap()
    program(nc, a, out)
    r = run_bass_kernel_spmd(nc, [arrays], core_ids=[0])
    y = r.results[0]["out"]
    return np.ascontiguousarray(y.transpose(1, 0, 2).reshape(D, S).T)[None]
```

```python
from contextlib import ExitStack

import numpy as np
import concourse.bass as bass
from concourse import mybir

F32 = mybir.dt.float32
F32R = mybir.dt.float32r
I32 = mybir.dt.int32
U32 = mybir.dt.uint32
ALU = mybir.AluOpType
ACT = mybir.ActivationFunctionType
AX = mybir.AxisListType.X
MUL, ADD, SUB, MAX = ALU.mult, ALU.add, ALU.subtract, ALU.max

D, NM, S, L = 1024, 16, 512, 528
HF = 264
FF, NE, EFF = 2816, 32, 512
CAP = 64
NOV = 16
NBLK = NE + NOV
C2, NC2 = 88, 6
EPS = 1e-6
SLOT = 2048
NSLOT = 6
BIG = 1e30

VEC = {}
_n = 0
for _k, _w in (("mix", 8), ("lb", 16), ("hn", 1), ("ffn", 8), ("fin", 8), ("g", 48), ("sc", 12), ("dc", 36),
               ("dn", 1), ("fb", 1), ("al", 8), ("dt", 8), ("rb", 36)):
    VEC[_k] = _n
    _n += _w
NVEC = _n

CON = {}
_n = 0
for _k, _w in (("id", 128), ("u", 128), ("ui", 128), ("li", 128), ("tri", 128), ("mf", 128), ("mb", 128),
               ("lv", 7 * 64), ("rst", L), ("io", 64), ("tok", 4)):
    CON[_k] = _n
    _n += _w
NCON = _n


def constants():
    c = np.zeros((128, NCON), np.float32)
    p = np.arange(128)[:, None]
    f = np.arange(128)[None, :]

    def put(k, a):
        c[:a.shape[0], CON[k]:CON[k] + a.shape[1]] = a

    put("id", (p == f) * 1.0)
    put("u", (p < f) * 1.0)
    put("ui", (p <= f) * 1.0)
    put("li", (p >= f) * 1.0)
    put("tri", np.where(f <= p, 0.0, -BIG))
    put("mf", np.where(p <= f, 0.0, -BIG))
    put("mb", np.where(p >= f, 0.0, -BIG))
    for n in range(7):
        h = 64 >> n
        j = np.arange(64)
        t = j // h * 2 * h + h + j % h
        put_at = CON["lv"] + 64 * n
        c[:, put_at:put_at + 64] = (p // (2 * h) == t[None] // (2 * h)) & (p % (2 * h) < h)
    r = np.ones((128, L), np.float32)
    r[:, [0, 16, 144, 272, 400]] = 0.0
    put("rst", r)
    put("io", np.broadcast_to(np.arange(64.0), (128, 64)))
    put("tok", np.arange(128.0)[:, None] + 128 * np.arange(4)[None])
    lv2 = np.zeros((128, 2, 7, 128), np.float32)
    for n in range(7):
        b = 1 << n
        m = (p // (2 * b) == f // (2 * b)) & (p % (2 * b) < b) & (f % (2 * b) >= b)
        lv2[:, 0, n] = m
        lv2[:, 1, n] = m.T
    order = np.arange(L)
    k = np.outer(order, order) % L
    dft = np.stack([np.cos(2 * np.pi * k / L), -np.sin(2 * np.pi * k / L)]) / np.sqrt(L * 64.0)
    dft = dft.reshape(2, NC2, C2, L).transpose(1, 2, 0, 3)
    full = np.zeros((NC2, 128, 2, L), np.float32)
    full[:, :C2] = dft
    k = np.outer(np.arange(64), np.arange(64)) % 64
    small = np.zeros((128, 256), np.float32)
    for g in range(2):
        small[64 * g:64 * g + 64, 64 * g:64 * g + 64] = np.cos(2 * np.pi * k / 64)
        small[64 * g:64 * g + 64, 128 + 64 * g:192 + 64 * g] = np.sin(2 * np.pi * k / 64)
    return {"con": c, "lv2": np.ascontiguousarray(lv2[:, :, :, :C2]).reshape(128, -1), "dft": full.reshape(NC2, 128, 2 * L), "dfs": small}


BESIDE = [(), (0,), (1,), (2,), (), (3,), (4,), (), (5, 6, 7), ()]


class Queue:

    def __init__(self, nc, eng, name):
        self.eng, self.sem, self.n, self.name = eng, nc.alloc_semaphore("q_" + name), 0, name
        self.seen = {}

    def __call__(self, ins):
        self.n += 1
        ins.then_inc(self.sem, 1)
        return (self.sem, self.n, self.name)

    def wait(self, *toks):
        for t in toks:
            if t is None:
                continue
            if isinstance(t, list):
                self.wait(*t)
            elif self.seen.get(t[2], 0) < t[1]:
                self.eng.wait_ge(t[0], t[1])
                self.seen[t[2]] = t[1]

    def last(self):
        return (self.sem, self.n, self.name) if self.n else None


class Dma:

    def __init__(self, nc, name):
        self.sem, self.n, self.name = nc.alloc_semaphore("d_" + name), 0, "d_" + name

    def __call__(self, ins):
        ins.then_inc(self.sem, 16)
        self.n += 16
        return (self.sem, self.n, self.name)


class K:
    def __init__(self, nc, a, out):
        self.nc, self.a, self.out = nc, a, out
        self.PE = Queue(nc, nc.tensor, "pe")
        self.V = Queue(nc, nc.vector, "v")
        self.A = Queue(nc, nc.scalar, "a")
        self.G = Queue(nc, nc.gpsimd, "g")
        self.SP = Queue(nc, nc.sync, "sp")
        self.ps = nc.alloc_psum_tensor("ps", [128, 8, 512], F32).ap()
        self.bank = [None] * 8
        self.pr = self.nx = 0
        self.nsb = 0
        self.stream = []
        self.ring = nc.alloc_sbuf_tensor("ring", [128, NSLOT, SLOT], F32).ap()
        self.rd = [Dma(nc, f"r{i}") for i in range(NSLOT)]
        self.issued = self.taken = 0
        self.arrive = {}
        self.freed = {}

    def sb(self, name, shape, dt=F32):
        return self.nc.alloc_sbuf_tensor(name, shape, dt).ap()

    def mm(self, out, lhsT, rhs, start, stop):
        return self.nc.tensor.matmul(out, lhsT, rhs, start=start, stop=stop, skip_group_check=True)

    def tt(self, q, out, a, b, op, *after):
        q.wait(*after)
        return q(q.eng.tensor_tensor(out, a, b, op))

    def ts(self, q, out, a, s1, s2, op0, op1=None, *after):
        q.wait(*after)
        if op1 is None:
            return q(q.eng.tensor_scalar(out, a, s1, None, op0))
        return q(q.eng.tensor_scalar(out, a, s1, s2, op0, op1))

    def stt(self, q, out, a, s, b, op0, op1, *after):
        q.wait(*after)
        return q(q.eng.scalar_tensor_tensor(out=out, in0=a, scalar=s, in1=b, op0=op0, op1=op1))

    def cp(self, q, out, a, *after):
        q.wait(*after)
        if q is self.A:
            return q(q.eng.copy(out, a))
        return q(q.eng.tensor_copy(out, a))

    def act(self, out, a, func, *after, **kw):
        self.A.wait(*after)
        return self.A(self.nc.scalar.activation(out, a, func, **kw))

    def take(self, *banks):
        for b in banks:
            self.PE.wait(self.bank[b])
            self.bank[b] = None

    def give(self, tok, *banks):
        for b in banks:
            self.bank[b] = tok

    def pair(self, n=3):
        b = 2 * (self.pr % n)
        self.pr += 1
        self.take(b, b + 1)
        return b

    def row(self, n=1):
        b = self.nx if self.nx + n <= 5 else 0
        self.nx = (b + n) % 5
        self.take(*range(b, b + n))
        return b

    def wide(self, b, lo=0, hi=HF):
        return self.ps[:, b:b + 2, lo:hi]

    def plan(self, src, n):
        self.stream.append((src, n))

    def feed(self):
        while self.issued < len(self.stream) and self.issued < self.taken_done() + NSLOT:
            i = self.issued
            s = i % NSLOT
            src, n = self.stream[i]
            if i >= NSLOT:
                self.SP.wait(self.freed[i - NSLOT])
            self.arrive[i] = self.rd[s](self.nc.sync.dma_start(self.ring[:, s, 0:n], src))
            self.issued += 1

    def taken_done(self):
        n = 0
        while n in self.freed:
            n += 1
        return n

    def weight(self):
        i = self.taken
        self.taken += 1
        self.feed()
        self.PE.wait(self.arrive[i])
        return i, self.ring[:, i % NSLOT, :]

    def release(self, i):
        self.freed[i] = self.PE.last()
        self.feed()

    def raw(self, *readers):
        i = self.taken
        self.taken += 1
        self.feed()
        for q in readers:
            q.wait(self.arrive[i])
        return i, self.ring[:, i % NSLOT, :]

    def read(self, i, toks):
        self.freed[i] = toks
        self.feed()

    def sync_all(self):
        toks = [q.last() for q in (self.PE, self.V, self.A, self.G)]
        for q in (self.PE, self.V, self.A, self.G):
            q.wait(*[t for t in toks])


def split(r0, r1):
    return [(r0, r1)] if r1 - r0 <= 512 else [(0, HF), (HF, L)]


def plan_weights(k):
    a = k.a
    for p in range(4):
        k.plan(a["w_att"][p, :, 0:2048], 2048)
        k.plan(a["w_att"][p, :, 2048:3072], 1024)
    for h in range(10):
        if h < 8:
            k.plan(a["w_hg"][h, :, 0:2048], 2048)
            k.plan(a["w_hg"][h, :, 2048:4096], 2048)
        for m in BESIDE[h]:
            k.plan(a["w_oa"][m], 1536)
    for m in range(8):
        k.plan(a["w_oh"][m], 2048)
    for c in range(4):
        k.plan(a["w_o"][c], 2048)
    for e in range(NE + 1):
        if e < NE:
            for c in range(4):
                k.plan(a["w_ein"][e, c], 2048)
        if e:
            for c in range(2):
                k.plan(a["w_eout"][e - 1, c], 2048)
    plan_ffn(k, "1")
    for j in range(4):
        k.plan(a["w_sf"][j, :, 0:2048], 2048)
        k.plan(a["w_sf"][j, :, 2048:4096], 2048)
    for j in range(4):
        k.plan(a["w_dn"][j, :, 0:2048], 2048)
        k.plan(a["w_dn"][j, :, 2048:4096], 2048)
        for m in (2 * j, 2 * j + 1):
            k.plan(a["w_out2"][m, :, 0:2048], 2048)
            k.plan(a["w_out2"][m, :, 2048:4096], 2048)
    for j in range(2):
        k.plan(a["w_d2"][j], 2048)
    for c in range(4):
        k.plan(a["w_o2"][c], 2048)
    plan_ffn(k, "2")


def plan_ffn(k, n):
    for g in range(3):
        for j in range(8 * g, min(8 * g + 8, 22)):
            k.plan(k.a["w_fi" + n][j], 2048)
        for c in range(4):
            w = 2048 if g < 2 else 1536
            k.plan(k.a["w_fo" + n][g, c, :, 0:w], w)


def linear(k, b, w, rhs, r0, r1, start=True, stop=True, after=None):
    n = len(w)
    for t in range(n):
        if after:
            k.PE.wait(after[t])
        for j, (c0, c1) in enumerate(split(r0, r1)):
            ins = k.mm(k.ps[:w[t].shape[-1], b + j, 0:c1 - c0], w[t], rhs[t][:, c0:c1],
                       start and t == 0, stop and t == n - 1)
    return k.PE(ins)


class Halves:

    def __init__(self, k, st, name, slots, sizes, pool=0):
        sb = lambda n: st.enter_context(k.nc.sbuf_tensor(n + name, [128, slots, 1024], F32R)).ap()
        self.k, self.n, self.h, self.l = k, slots, sb("wh"), sb("wl")
        self.sizes, self.pool = sizes, pool
        self.free, self.ready = {}, {}
        self.cut, self.at, self.chunk, self.toks = 0, 0, None, []
        self.pos = 0

    def prepare(self):
        k, i = self.k, self.cut
        if self.chunk is None:
            self.chunk = k.raw(k.A)
            self.pos, self.toks = 0, []
        n, last = self.sizes[i]
        s = i % self.n
        src = self.chunk[1][:, self.pos:self.pos + n]
        ta = k.cp(k.A, self.h[:, s, 0:n], src, self.free.get(i - self.n))
        q = k.G if self.pool and i % self.pool == self.pool - 1 else k.V
        q.wait(k.arrive[self.chunk[0]])
        tv = k.tt(q, self.l[:, s, 0:n], src, self.h[:, s, 0:n].bitcast(F32), SUB, ta, self.free.get(i - self.n))
        self.ready[i] = [ta, tv]
        self.toks = self.toks + [ta, tv]
        self.pos += n
        self.cut += 1
        if last:
            k.read(self.chunk[0], self.toks)
            self.chunk = None

    def begin(self):
        while self.cut < min(self.n, len(self.sizes)):
            self.prepare()

    def get(self):
        i = self.at
        self.at += 1
        while self.cut < min(i + self.n, len(self.sizes)):
            self.prepare()
        self.k.PE.wait(self.ready[i])
        s = i % self.n
        return i, self.h[:, s, :], self.l[:, s, :]

    def done(self, i):
        self.free[i] = self.k.PE.last()


def linear3(k, b, wh, wl, xh, xl, r0, r1, after=None):
    n = len(wh)
    start = stop = True
    cols = list(enumerate(split(r0, r1)))
    for t in range(n):
        if after:
            k.PE.wait(after[t])
        for p, (w, x) in enumerate(((wh, xh), (wh, xl), (wl, xh))):
            for j, (c0, c1) in cols:
                ins = k.mm(k.ps[:, b + j, 0:c1 - c0], w[t], x[t][:, c0:c1],
                           start and t == 0 and p == 0, stop and t == n - 1 and p == 2)
    return k.PE(ins)


def part(k, src, h, l, *after):
    ta = k.cp(k.A, h, src, *after)
    return k.tt(k.V, l, src, h.bitcast(F32), SUB, ta, *after)


def tiles(ap, n):
    return [ap[:, t, :] for t in range(n)]


def squares(k, x, m, r0, after):
    sq = k.sq
    a = k.act(sq[:, m % 2, r0:L], x[:, m, r0:L], ACT.Square, after, k.sqfree[m % 2])
    if m == 0:
        k.take(6, 7)
    k.PE.wait(a)
    for j, (c0, c1) in enumerate(split(r0, L)):
        ins = k.mm(k.ps[:, 6 + j, 0:c1 - c0], k.ones, sq[:, m % 2, c0:c1], m == 0, m == 7)
    k.sqsum = k.sqfree[m % 2] = k.PE(ins)


def rms(k, x, w, out, r0, after, have=False, then=None):
    n = L - r0
    rb = k.rb
    each = []
    if not have:
        for m in range(8):
            squares(k, x, m, r0, after)
    src = k.wide(6) if n > 512 else k.ps[:, 6, 0:n]
    dst = rb[:, 0:n].rearrange("p (a c) -> p a c", a=2) if n > 512 else rb[:, 0:n]
    a = k.act(dst, src, ACT.Sqrt, k.sqsum, k.rbfree, bias=k.eps[:, 0:1], scale=1.0 / D)
    k.give(a, 6, 7)
    v = k.V
    v.wait(a)
    t0 = v(k.nc.vector.reciprocal(rb[:, 0:n], rb[:, 0:n]))
    last = None
    for m in range(8):
        before = last
        last = k.stt(v, out[:, m, r0:L], x[:, m, r0:L], w[m], rb[:, 0:n], MUL, MUL, t0, after)
        each.append(last)
        if then and m:
            then(m - 1, before)
    if then:
        then(7, last)
    k.rbfree = last
    return each


def attention(k, uT, u_tok, oaT):
    nc, V, A, G, PE = k.nc, k.V, k.A, k.G, k.PE
    with ExitStack() as st:
        def sb(name, shape):
            return st.enter_context(nc.sbuf_tensor(name, shape, F32)).ap()

        fx = sb("fx", [8, 3, L])
        one8 = sb("one8", [8, L])
        qa = sb("qa", [65, 2, 2, S])
        ka = sb("ka", [65, 2, 2, L])
        va = sb("va", [128, 2, 5, 128])
        P = sb("P", [128, 3, L])
        PT = sb("PT", [128, 3, 5, 128])
        sm = sb("sm", [128, 3, 4])
        PE.wait(k.ld_wf)
        b = k.pair()
        t = linear(k, b, tiles(k.wf, 8), tiles(uT, 8), 0, L, after=u_tok)
        f0, f1, f2 = (fx[:, i, :] for i in range(3))
        v2 = lambda x: x.rearrange("p (a c) -> p a c", a=2)
        t = k.ts(V, v2(f0), k.wide(b)[0:8], k.vec["fb"][0:8, 0:1], None, ADD, None, t, k.ld)
        k.give(t, b, b + 1)
        ta = k.act(f1, f0, ACT.Abs, t)
        ta = k.act(f1, f1, ACT.Exp, ta, scale=-1.0)
        ta = k.act(f1, f1, ACT.Ln, ta, bias=1.0)
        t = k.ts(V, f0, f0, 0.0, None, ALU.min, None, ta)
        t = k.tt(V, f0, f1, f0, SUB, t)
        t1 = V(nc.vector.memset(one8, 1.0))
        V.wait(t, t1)
        tc = V(nc.vector.tensor_tensor_scan(f2, one8, f0, 0.0, MUL, ADD))
        tq = [V(nc.vector.memset(qa[64:65, i], 1.0)) for i in range(2)]
        buf = [None, None]
        kd = [Dma(nc, "ka0"), Dma(nc, "ka1")]
        kfree = [None, None]
        units = []

        def project(p):
            i = p % 2
            c, w = k.weight()
            wv = w.rearrange("p (t c) -> p t c", t=8)
            PE.wait(u_tok)
            b = k.pair()
            t = linear(k, b, [wv[:, x, 0:128] for x in range(8)], tiles(uT, 8), NM, L)
            ts = []
            for j in range(2):
                A.wait(t, kfree[i])
                ts.append(A(nc.scalar.mul(qa[0:64, i, j, :], k.ps[64 * j:64 * j + 64, b, :], 0.125)))
            k.give(ts[-1], b, b + 1)
            b = k.pair()
            t = linear(k, b, [wv[:, x, 128:256] for x in range(8)], tiles(uT, 8), 0, L)
            k.release(c)
            for j in range(2):
                ts.append(k.cp(V, ka[0:64, i, j, :].rearrange("p (a c) -> p a c", a=2),
                               k.wide(b)[64 * j:64 * j + 64], t, kfree[i]))
            k.give(ts[-1], b, b + 1)
            G.wait(tc, kfree[i])
            ts.append(kd[i](nc.gpsimd.dma_start(ka[64:65, i], f2[2 * p:2 * p + 2, :])))
            c, w = k.weight()
            wv = w[:, 0:1024].rearrange("p (t c) -> p t c", t=8)
            b = k.pair()
            for m in range(5):
                n = NM if m == 0 else 128
                o = 0 if m == 0 else NM + 128 * (m - 1)
                dst = k.ps[0:n, b + 1, 0:128] if m == 0 else k.ps[:, b, 128 * (m - 1):128 * m]
                for x in range(8):
                    ins = k.mm(dst, uT[:, x, o:o + n], wv[:, x, :], x == 0, x == 7)
            t = PE(ins)
            k.release(c)
            ts.append(k.cp(A, va[:, i, 1:5, :].rearrange("p a c -> p (a c)"), k.ps[:, b, :], t, kfree[i]))
            ts.append(k.cp(A, va[0:NM, i, 0, :], k.ps[0:NM, b + 1, 0:128], t, kfree[i]))
            k.give(ts[-1], b, b + 1)
            buf[i] = ts

        def scores(p, j, q):
            i = p % 2
            u = len(units) % 3
            na = NM + 128 * q
            nk = na + 128
            b = k.pair()
            PE.wait(buf[i], tq[i])
            lhs = qa[:, i, j, 128 * q:128 * q + 128]
            k.mm(k.ps[:, b, 512 - na:512], lhs, ka[:, i, j, 0:na], True, True)
            k.mm(k.ps[:, b + 1, 0:128], lhs, ka[:, i, j, na:nk], True, False)
            t = PE(k.mm(k.ps[:, b + 1, 0:128], k.ident, k.con["tri"], False, True))
            src = k.ps[:, b:b + 2, :].rearrange("p a c -> p (a c)")[:, 512 - na:640]
            V.wait(t, units[-3][4] if len(units) >= 3 else None)
            t = V(nc.vector.tensor_reduce(sm[:, u, 0:1], src, AX, MAX, negate=True))
            t = k.act(P[:, u, 0:nk], src, ACT.Exp, t, bias=sm[:, u, 0:1], accum_out=sm[:, u, 1:2])
            k.give(t, b, b + 1)
            V.wait(t)
            t = V(nc.vector.reciprocal(sm[:, u, 2:3], sm[:, u, 1:2]))
            t = k.ts(V, P[:, u, 0:nk], P[:, u, 0:nk], sm[:, u, 2:3], None, MUL, None, t)
            units.append([p, j, q, t, None, u])

        def turn(n):
            p, j, q, t, _, u = units[n]
            PE.wait(t)
            b = k.pair()
            for m in range(q + 1):
                k.tr(k.ps[:, b, 128 * m:128 * m + 128], P[:, u, NM + 128 * m:NM + 128 * m + 128])
            t = PE(k.tr(k.ps[0:NM, b + 1, 0:128], P[:, u, 0:NM]))
            free = units[n - 3][4] if n >= 3 else None
            t1 = k.cp(V, PT[:, u, 1:q + 2, :].rearrange("p a c -> p (a c)"), k.ps[:, b, 0:128 * (q + 1)], t, free)
            t2 = k.cp(A, PT[0:NM, u, 0, :], k.ps[0:NM, b + 1, 0:128], t, free)
            k.give([t1, t2], b, b + 1)
            units[n][3] = [t1, t2]

        def values(n):
            p, j, q, t, _, u = units[n]
            i = p % 2
            PE.wait(t, buf[i])
            if j == 0 and q == 0:
                k.take(6)
            dst = k.ps[64 * j:64 * j + 64, 6, 128 * q:128 * q + 128]
            k.mm(dst, va[0:NM, i, 0, 64 * j:64 * j + 64], PT[0:NM, u, 0, :], True, False)
            for m in range(q + 1):
                ins = k.mm(dst, va[:, i, m + 1, 64 * j:64 * j + 64], PT[:, u, m + 1, :], False, m == q)
            t = PE(ins)
            units[n][4] = t
            if j == 1 and q == 3:
                kfree[i] = t
                t = k.cp(A, oaT[:, p, :], k.ps[:, 6, :], t)
                k.give(t, 6)
            return t

        project(0)
        todo = [(p, j, q) for p in range(4) for j in range(2) for q in range(4)]
        for n in range(len(todo) + 2):
            if n < len(todo):
                if n % 8 == 3 and todo[n][0] < 3:
                    project(todo[n][0] + 1)
                scores(*todo[n])
            if 1 <= n <= len(todo):
                turn(n - 1)
            if n >= 2:
                last = values(n - 2)
        k.sync_all()
    return last


def hgrn(k, uT, u_tok, oh, filler):
    nc, V, A, G, PE = k.nc, k.V, k.A, k.G, k.PE
    with ExitStack() as st:
        def sb(name, shape):
            return st.enter_context(nc.sbuf_tensor(name, shape, F32)).ap()

        q_ = sb("hq", [128, 2, S])
        g_ = sb("hg", [128, 3, S])
        fs = sb("hfs", [128, L])
        kk = sb("hk", [128, 2, L])
        lf = sb("hlf", [128, L])
        bb = sb("hb", [128, 2, L])
        vv = sb("hv", [128, 3, 5, 128])
        E = sb("hE", [128, 2, L])
        qe = sb("hqe", [128, 2, S])
        kd = sb("hkd", [128, 2, L])
        kdt = sb("hkdt", [128, 2, 5, 128])
        dd = sb("hdd", [128, 2, S])
        Kl = sb("hKl", [128, 7, S])
        Ql = sb("hQl", [128, 7, 256])
        sc = sb("hsc", [128, 2, S])
        St = sb("hS", [128, 2, 128])
        oo = sb("ho", [128, 2, S])
        lbv = sb("lbv", [128, 3, 8])
        omv = sb("omv", [128, 8])
        l0, l1 = k.vec["lb"][:, 0:8], k.vec["lb"][:, 8:16]
        m, x0, x1 = lbv[:, 0, :], lbv[:, 1, :], lbv[:, 2, :]
        t = k.tt(V, m, l0, l1, MAX, k.ld)
        ta = k.tt(V, x0, l0, m, SUB, t)
        tb = k.tt(V, x1, l1, m, SUB, t)
        ta = k.act(x0, x0, ACT.Exp, ta)
        tb = k.act(x1, x1, ACT.Exp, tb)
        t = k.tt(V, x1, x0, x1, ADD, ta, tb)
        V.wait(t)
        t = V(nc.vector.reciprocal(x1, x1))
        t = k.tt(V, x0, x0, x1, MUL, t)
        lb = x0
        t_lb = k.ts(V, omv, lb, -1.0, 1.0, MUL, ADD, t)
        t_z = V(nc.vector.memset(Kl, 0.0))
        t_zs = V(nc.vector.memset(sc, 0.0))
        H = [dict() for _ in range(8)]
        rest = []

        def fill(n):
            while n and rest:
                if next(rest[0], None) is None:
                    rest.pop(0)
                n -= 1


        def project(h):
            s = H[h]
            i, i3 = h % 2, h % 3
            old = H[h - 2] if h >= 2 else {}
            old3 = H[h - 3] if h >= 3 else {}
            c, w = k.weight()
            wv = w.rearrange("p (t c) -> p t c", t=8)
            PE.wait(u_tok)
            b = k.row()
            t = linear(k, b, [wv[:, x, 0:128] for x in range(8)], tiles(uT, 8), NM, L)
            A.wait(t, old.get("lvl"), old.get("qe"), old.get("diag"))
            s["q"] = A(nc.scalar.mul(q_[:, i, :], k.ps[:, b, :], 128.0 ** -0.5))
            k.give(s["q"], b)
            yield
            b = k.row(2)
            t = linear(k, b, [wv[:, x, 128:256] for x in range(8)], tiles(uT, 8), 0, L)
            k.release(c)
            fs2 = fs.rearrange("p (a c) -> p a c", a=2)
            t = k.act(fs2, k.wide(b), ACT.Sigmoid, t, H[h - 1].get("k") if h else None)
            k.give(t, b, b + 1)
            t = k.ts(V, fs, fs, omv[:, h:h + 1], lb[:, h:h + 1], MUL, ADD, t, t_lb)
            tl = k.act(lf, fs, ACT.Ln, t, H[h - 1].get("b") if h else None)
            s["k"] = k.ts(V, kk[:, i, :], fs, -1.0, 1.0, MUL, ADD, t, old.get("diag"), old.get("kd"))
            V.wait(tl, old.get("lvl"))
            s["b"] = V(nc.vector.tensor_tensor_scan(bb[:, i, :], k.con["rst"], lf, 0.0, MUL, ADD))
            yield
            c, w = k.weight()
            wv = w.rearrange("p (t c) -> p t c", t=8)
            b = k.row(2)
            for m in range(5):
                n = NM if m == 0 else 128
                o = 0 if m == 0 else NM + 128 * (m - 1)
                dst = k.ps[0:n, b + 1, 0:128] if m == 0 else k.ps[:, b, 128 * (m - 1):128 * m]
                for x in range(8):
                    ins = k.mm(dst, uT[:, x, o:o + n], wv[:, x, 0:128], x == 0, x == 7)
            t = PE(ins)
            ta = k.cp(A, vv[:, i3, 1:5, :].rearrange("p a c -> p (a c)"), k.ps[:, b, :], t, old3.get("o"))
            ta = k.cp(A, vv[0:NM, i3, 0, :], k.ps[0:NM, b + 1, 0:128], t)
            k.give(ta, b, b + 1)
            s["v"] = ta
            yield
            b = k.row()
            t = linear(k, b, [wv[:, x, 128:256] for x in range(8)], tiles(uT, 8), NM, L)
            k.release(c)
            s["g"] = k.act(g_[:, i3, :], k.ps[:, b, :], ACT.Sigmoid, t, old3.get("fin"))
            k.give(s["g"], b)
            yield

        def prepare(h):
            s = H[h]
            i = h % 2
            old = H[h - 2] if h >= 2 else {}
            s["E"] = k.act(E[:, i, :], bb[:, i, :], ACT.Exp, s["b"], old.get("S"))
            s["qe"] = k.tt(V, qe[:, i, :], q_[:, i, :], E[:, i, NM:L], MUL, s["E"], s["q"], old.get("o"))
            last = bb[:, i, NM:L].rearrange("p (c x) -> p c x", c=4)
            e = last[:, :, 127:128].to_broadcast([128, 4, 128])
            t1 = k.tt(V, kd[:, i, NM:L].rearrange("p (c x) -> p c x", c=4), e, last, SUB, s["b"], old.get("kt"))
            t2 = k.tt(V, kd[:, i, 0:NM], bb[:, i, NM - 1:NM].to_broadcast([128, NM]), bb[:, i, 0:NM], SUB, s["b"])
            t = k.act(kd[:, i, :], kd[:, i, :], ACT.Exp, t1, t2)
            s["kd"] = k.tt(V, kd[:, i, :], kd[:, i, :], kk[:, i, :], MUL, t, s["k"])
            dfree = H[h - 1].get("dfree", [None, None]) if h else [None, None]
            s["L"] = []
            prevmm = H[h - 1].get("mml") if h else None
            for n in range(7):
                hs = 64 >> n
                nb = S // (2 * hs)
                B = bb[:, i, NM:L].rearrange("p (n x) -> p n x", n=nb)
                ref = B[:, :, hs - 1:hs].to_broadcast([128, nb, hs])
                d = dd[:, n % 2, :]
                d3 = d.rearrange("p (n x) -> p n x", n=nb)
                t1 = k.tt(V, d3[:, :, 0:hs], ref, B[:, :, 0:hs], SUB, s["b"], dfree[n % 2])
                t2 = k.tt(V, d3[:, :, hs:2 * hs], B[:, :, hs:2 * hs], ref, SUB)
                t = k.act(d, d, ACT.Exp, t1, t2)
                K3 = kk[:, i, NM:L].rearrange("p (n x) -> p n x", n=nb)
                Q3 = q_[:, i, :].rearrange("p (n x) -> p n x", n=nb)
                ta = k.tt(V, Kl[:, n, :].rearrange("p (n x) -> p n x", n=nb)[:, :, 0:hs], d3[:, :, 0:hs],
                          K3[:, :, 0:hs], MUL, t, t_z, prevmm, s["k"])
                tb = k.tt(V, Ql[:, n, :].rearrange("p (n x) -> p n x", n=nb), d3[:, :, hs:2 * hs],
                          Q3[:, :, hs:2 * hs], MUL, t, s["q"])
                dfree[n % 2] = tb
                s["L"].append([ta, tb])
                s["dfree"] = dfree
                s["lvl"] = tb
                yield

        def level(h):
            s = H[h]
            i = h % 2
            old = H[h - 2] if h >= 2 else {}
            tok = [old.get("o"), t_zs]
            for n in range(7):
                hs = 64 >> n
                bk = k.row()
                fill(1)
                PE.wait(s["L"][n])
                for c in range(4):
                    ins = k.mm(k.ps[:, bk, 64 * c:64 * c + 64], Kl[:, n, 128 * c:128 * c + 128],
                               Ql[:, n, 64 * c:64 * c + 64], True, True)
                t = PE(ins)
                s["mml"] = t
                nb = 64 // hs
                V.wait(t, tok)
                dst = sc[:, i, :].rearrange("p (c n x) -> p c n x", c=4, n=nb)[:, :, :, hs:2 * hs]
                src = k.ps[:, bk, 0:256].rearrange("p (c n x) -> p c n x", c=4, n=nb)
                for c in range(4):
                    mask = k.con["lv"][:, 64 * n:64 * n + 64].rearrange("p (n x) -> p n x", n=nb).bitcast(I32)
                    tw = V(nc.vector.copy_predicated(dst[:, c], mask, src[:, c]))
                tok = tw
                k.give(tw, bk)
            b = k.row()
            PE.wait(s["q"], s["k"])
            for c in range(4):
                ins = k.mm(k.ps[:, b, 128 * c:128 * c + 128], kk[:, i, NM + 128 * c:NM + 128 * c + 128],
                           q_[:, i, 128 * c:128 * c + 128], True, True)
            t = PE(ins)
            s["diag"] = t
            V.wait(t, tok)
            for c in range(4):
                tw = V(nc.vector.copy_predicated(sc[:, i, 128 * c:128 * c + 128], k.ident.bitcast(I32),
                                                 k.ps[:, b, 128 * c:128 * c + 128]))
            k.give(tw, b)
            s["sc"] = tw
            b = k.row(2)
            fill(1)
            PE.wait(s["kd"])
            for c in range(4):
                k.tr(k.ps[:, b, 128 * c:128 * c + 128], kd[:, i, NM + 128 * c:NM + 128 * c + 128])
            t = PE(k.tr(k.ps[0:NM, b + 1, 0:128], kd[:, i, 0:NM]))
            s["kt"] = t
            ta = k.cp(A, kdt[:, i, 1:5, :].rearrange("p a c -> p (a c)"), k.ps[:, b, :], t, old.get("S"))
            ta = k.cp(A, kdt[0:NM, i, 0, :], k.ps[0:NM, b + 1, 0:128], t)
            k.give(ta, b, b + 1)
            s["kdt"] = ta

        def output(h):
            s = H[h]
            i, i3 = h % 2, h % 3
            old = H[h - 2] if h >= 2 else {}
            k.take(6, 7)
            fill(2)
            PE.wait(s["kdt"], s["v"])
            k.mm(k.ps[:, 7, 0:128], kdt[0:NM, i, 0, :], vv[0:NM, i3, 0, :], True, True)
            for c in range(3):
                o = 128 * (c + 1)
                t = PE(k.mm(k.ps[:, 7, o:o + 128], kdt[:, i, c + 1, :], vv[:, i3, c + 1, :], True, True))
            tS = k.cp(V, St[:, i, :], k.ps[:, 7, 0:128], t, old.get("o"))
            PE.wait(s["qe"], s["sc"])
            for c in range(4):
                dst = k.ps[:, 6, 128 * c:128 * c + 128]
                k.mm(dst, vv[:, i3, c + 1, :], sc[:, i, 128 * c:128 * c + 128], True, False)
                fill(1)
                PE.wait(tS)
                s["o"] = PE(k.mm(dst, St[:, i, :], qe[:, i, 128 * c:128 * c + 128], False, True))
                if c < 3:
                    o = 128 * (c + 1)
                    e = E[:, i, NM + 128 * c + 127:NM + 128 * c + 128]
                    tS = k.stt(V, St[:, i, :], St[:, i, :], e, k.ps[:, 7, o:o + 128], MUL, ADD, t, s["o"])
            s["S"] = tS
            k.give(tS, 7)
            to = k.cp(V, oo[:, i, :], k.ps[:, 6, :], s["o"], old.get("fin"))
            k.give(to, 6)
            ta = k.act(k.sq[:, 0, 0:S], oo[:, i, :], ACT.Square, to, k.sqfree[0])
            fill(2)
            PE.wait(ta)
            b = k.row()
            t = PE(k.mm(k.ps[:, b, :], k.ones, k.sq[:, 0, 0:S], True, True))
            k.sqfree[0] = t
            ta = k.act(k.rb[:, 0:S], k.ps[:, b, :], ACT.Sqrt, t, k.rbfree, bias=k.eps[:, 0:1], scale=1.0 / 128)
            k.give(ta, b)
            V.wait(ta)
            t = V(nc.vector.reciprocal(k.rb[:, 0:S], k.rb[:, 0:S]))
            t = k.stt(V, k.rb[:, 0:S], k.rb[:, 0:S], k.vec["hn"], g_[:, i3, :], MUL, MUL, t, s["g"])
            s["fin"] = k.tt(V, oh[:, h, :], oo[:, i, :], k.rb[:, 0:S], MUL, t)
            k.rbfree = s["fin"]

        for h in range(10):
            ahead = prepare(h - 1) if 1 <= h < 9 else iter(())
            if h < 8:
                fill(1000)
                for _ in project(h):
                    next(ahead, None)
                    next(ahead, None)
            for _ in ahead:
                pass
            for m in BESIDE[h]:
                rest.append(filler(m))
            if rest:
                fill(1)
            if 1 <= h < 9:
                level(h - 1)
            if h >= 2:
                output(h - 2)
        fill(1000)
        k.sync_all()


def branch(k, uT, oaT, gt, keep, ready):
    V, PE = k.V, k.PE
    free = [k.ysz, k.ysz]

    def tile(m):
        i = m % 2
        c, w = k.weight()
        for j in range(2):
            bank = 5
            k.take(bank)
            n = (8, 4)[j]
            x, x0 = ((uT, NM), (oaT, 0))[j]
            for t in range(n):
                o = 1024 * j + 128 * t
                ins = k.mm(k.ps[:, bank, :], w[:, o:o + 128], x[:, t, x0:x0 + S], t == 0, t == n - 1)
                if t < n - 1:
                    yield 1
            t = PE(ins)
            if j == 0:
                tg = k.act(gt[:, i, :], k.ps[:, bank, :], ACT.Sigmoid, t, free[i])
                k.give(tg, bank)
                yield 1
            else:
                free[i] = k.tt(V, keep[:, m, NM:L], k.ps[:, bank, :], gt[:, i, :], MUL, t, tg, ready)
                k.give(free[i], bank)
        k.release(c)

    return tile


def mix_out(k, st, uT, oh, hT, spill, dh, gt):
    nc, V, A, G, PE = k.nc, k.V, k.A, k.G, k.PE
    sb = lambda n: st.enter_context(nc.sbuf_tensor(n, [128, 8, S], F32R)).ap()
    uh, ul, oH, oL = (sb(n) for n in ("muh", "mul", "moh", "mol"))
    W = Halves(k, st, "m1", 2, [(1024, False), (1024, True)] * 12)
    v3 = lambda w: [w[:, 128 * x:128 * x + 128] for x in range(8)]
    W.begin()
    tu = [part(k, uT[:, m, NM:L], uh[:, m, :], ul[:, m, :]) for m in range(8)]

    def product(x, after):
        i, wh, wl = W.get()
        b = k.pair()
        t = linear3(k, b, v3(wh), v3(wl), tiles(x[0], 8), tiles(x[1], 8), 0, S, after)
        W.done(i)
        return b, t

    free = [None, None]
    mixed = []
    for m in range(8):
        i = m % 2
        b, t = product((uh, ul), None if m else tu)
        ta = k.act(gt[:, i, :], k.ps[:, b, :], ACT.Sigmoid, t, free[i])
        k.give(ta, b, b + 1)
        if m == 0:
            to = [part(k, oh[:, x, :], oH[:, x, :], oL[:, x, :]) for x in range(8)]
            G.wait(to, A.last())
            tr = dh(nc.gpsimd.dma_start(oh, spill[:, :, NM:L]))
        b, t = product((oH, oL), None if m else to)
        tb = k.tt(V, gt[:, i, :], k.ps[:, b, :], gt[:, i, :], MUL, t, ta)
        k.give(tb, b, b + 1)
        free[i] = k.tt(V, hT[:, m, NM:L], gt[:, i, :], hT[:, m, NM:L], ADD, tb)
        mixed.append(free[i])
    last = PE.last()
    tu = [part(k, hT[:, m, NM:L], uh[:, m, :], ul[:, m, :], mixed[m], last) for m in range(8)]
    for m in range(8):
        b, t = product((uh, ul), None if m else tu)
        before = t if m == 0 else th
        th = k.tt(V, hT[:, m, NM:L], oh[:, m, :], k.ps[:, b, :], ADD, t, tr)
        k.give(th, b, b + 1)
        if m:
            squares(k, hT, m - 1, NM, before)
    squares(k, hT, 7, NM, th)
    return th


def setup(k):
    nc = k.nc
    k.ident = None
    con = k.sb("con", [128, NCON])
    vec = k.sb("vec", [128, NVEC])
    k.wf = k.sb("wf", [128, 8, 8])
    k.wba = k.sb("wba", [128, 8, 16])
    k.wr = k.sb("wr", [128, 8, 36])
    k.hT = k.sb("hT", [128, 8, L])
    k.uT = k.sb("uT", [128, 8, L])
    k.sq = k.sb("sq", [128, 2, L])
    k.rb = k.sb("rb", [128, L])
    k.ones = k.sb("o1", [128, 128])
    k.eps = k.sb("eps", [128, 1])
    k.sqfree = [None, None]
    k.sqsum = None
    k.rbfree = None
    k.con = {n: con[:, o:o + w] for n, o, w in
             ((n, CON[n], w) for n, w in (("id", 128), ("u", 128), ("ui", 128), ("li", 128), ("tri", 128),
                                          ("mf", 128), ("mb", 128), ("lv", 448), ("rst", L), ("io", 64),
                                          ("tok", 4)))}
    k.vec = {n: vec[:, VEC[n]:VEC[n] + w] for n, w in
             (("mix", 8), ("lb", 16), ("hn", 1), ("ffn", 8), ("fin", 8), ("g", 48), ("sc", 12), ("dc", 36),
              ("dn", 1), ("fb", 1), ("al", 8), ("dt", 8), ("rb", 36))}
    k.ident = k.con["id"]
    k.tr = lambda out, in_: nc.tensor.transpose(out, in_, k.ident[:in_.shape[0], :in_.shape[0]])
    d = [Dma(nc, f"ld{i}") for i in range(6)]
    a = k.a
    t2 = d[1](nc.scalar.dma_start(vec, a["vec"]))
    t1 = []
    for m in range(4):
        dm = Dma(nc, f"ldh{m}")
        t1.append(dm(nc.sync.dma_start(k.hT[:, 2 * m:2 * m + 2, :], a["hT"][:, 2 * m:2 * m + 2, :])))
    t3 = d[2](nc.scalar.dma_start(con, a["con"]))
    t4 = d[3](nc.scalar.dma_start(k.wf, a["w_f"]))
    t5 = d[4](nc.scalar.dma_start(k.wba, a["w_ba"]))
    t6 = d[5](nc.scalar.dma_start(k.wr, a["w_r"]))
    k.ld_h, k.ld, k.ld_wf, k.ld_wr, k.ld_wba = t1, [t2, t3], t4, t6, t5
    V = k.V
    toks = [V(nc.vector.memset(k.ones, 1.0)), V(nc.vector.memset(k.eps, EPS))]
    for q in (k.PE, k.V, k.A, k.G):
        q.wait(toks, t2)
    k.ys = nc.dram_tensor("ys", [NBLK * CAP, D], F32, kind="Internal").ap()
    k.ysz = []
    plan_weights(k)
    k.feed()


def zero_rows(k, zero):
    nc = k.nc
    z = k.V(nc.vector.memset(zero, 0.0))
    k.SP.wait(z)
    for j in range(NOV * CAP // 128):
        dz = Dma(nc, f"ysz{j}")
        r = NE * CAP + 128 * j
        k.ysz.append(dz(nc.sync.dma_start(k.ys[r:r + 128, :].rearrange("p (a c) -> p a c", c=256),
                                          zero.unsqueeze(1).to_broadcast([128, 4, 256]))))


def block1(k):
    for m in range(8):
        squares(k, k.hT, m, 0, k.ld_h[m // 2])
    t = rms(k, k.hT, [k.vec["mix"][:, i:i + 1] for i in range(8)], k.uT, 0, k.ld_h, True)
    for q in (k.PE, k.V, k.A, k.G):
        q.wait(k.ld)
    with ExitStack() as st:
        oaT = st.enter_context(k.nc.sbuf_tensor("oaT", [128, 4, S], F32)).ap()
        attention(k, k.uT, t, oaT)
        spill = k.nc.dram_tensor("hspill1", [128, 8, L], F32, kind="Internal").ap()
        dh = Dma(k.nc, "hs1")
        k.G.wait(k.V.last(), k.A.last())
        ths = dh(k.nc.gpsimd.dma_start(spill, k.hT))
        gt = st.enter_context(k.nc.sbuf_tensor("gt", [128, 2, S], F32)).ap()
        zero_rows(k, gt[:, 0, 0:256])
        oh = st.enter_context(k.nc.sbuf_tensor("oh", [128, 8, S], F32)).ap()
        hgrn(k, k.uT, t, oh, branch(k, k.uT, oaT, gt, k.hT, ths))
        mix_out(k, st, k.uT, oh, k.hT, spill, dh, gt)
        k.sync_all()


def ktiles(w):
    return w.reshape(w.shape[0] // 128, 128, w.shape[1]).transpose(1, 0, 2)


def side(*parts):
    a = np.concatenate(parts, axis=2)
    return a.reshape(128, -1)


def layout(i):
    A = np.asarray
    i = {n: A(v) for n, v in i.items()}
    o = {}
    o["hT"] = np.concatenate([i["meta_tokens"], i["x"][0]], 0).T.reshape(8, 128, L).transpose(1, 0, 2)
    o["m2T"] = i["meta_tokens_2"].T.reshape(8, 128, NM).transpose(1, 0, 2)
    col = lambda v: v.reshape(-1, 128).T
    vec = np.zeros((128, NVEC), np.float32)

    def put(n, a):
        vec[:a.shape[0], VEC[n]:VEC[n] + a.shape[1]] = a

    put("mix", col(i["norm_mix_w"][0]))
    put("lb", np.concatenate([col(i["hgrn_lb_logits"][0]), col(i["hgrn_lb_logits"][1])], 1))
    put("hn", col(i["hgrn_norm_w"][0]))
    put("ffn", col(i["norm_ffn_w"][0]))
    put("fin", col(i["norm_final_w"]))
    put("g", np.concatenate([col(i["norm_gains_2"][0, j]) for j in range(6)], 1))
    put("sc", np.concatenate([col(i["sconv_w_2"][0, j]) for j in range(3)], 1))
    put("dc", np.concatenate([col(i["dn_conv_w_2"][0, j]) for j in range(3)], 1))
    put("dn", col(i["dn_norm_2"][0]))
    put("fb", i["attn_forget_b"][0][:, None])
    put("al", np.broadcast_to(i["dn_A_log_2"][0].reshape(1, 8), (128, 8)))
    put("dt", np.broadcast_to(i["dn_dt_bias_2"][0].reshape(1, 8), (128, 8)))
    put("rb", np.broadcast_to(np.concatenate([i["b_router_group"][0], i["b_router_expert"][0]])[None], (128, 36)))
    o["vec"] = vec
    w = ktiles(i["w_in"][0])
    s = np.cumsum([0, 512, 512, 512, 8, 1024, 1024, 1024, 1024, 1024, 1024])
    at = lambda j, t: w[:, :, s[j] + 128 * t:s[j] + 128 * t + 128]
    o["w_att"] = np.stack([np.concatenate([side(at(0, p), at(1, p)), side(at(2, p))], 1) for p in range(4)])
    o["w_f"] = w[:, :, s[3]:s[4]]
    o["w_hg"] = np.stack([np.concatenate([side(at(4, h), at(5, h)), side(at(6, h), at(7, h))], 1) for h in range(8)])
    wa, wh = ktiles(i["w_attn_out"][0]), ktiles(i["w_hgrn_out"][0])
    t = lambda x, m: x[:, :, 128 * m:128 * m + 128]
    o["w_oa"] = np.stack([np.concatenate([side(at(8, m)), side(t(wa, m))], 1) for m in range(8)])
    o["w_oh"] = np.stack([np.concatenate([side(at(9, m)), side(t(wh, m))], 1) for m in range(8)])
    two = lambda x: np.stack([np.concatenate([side(t(x, 2 * c)), side(t(x, 2 * c + 1))], 1) for c in range(4)])
    o["w_o"] = two(ktiles(i["w_o"][0]))
    o["w_r"] = np.concatenate([ktiles(i["w_router_group"][0]), ktiles(i["w_router_expert"][0])], 2)
    e = i["w_expert_in"][0]
    o["w_ein"] = e.reshape(NE, 2, 4, 128, 2, 512).transpose(0, 4, 1, 3, 2, 5).reshape(NE, 4, 128, 2048)
    e = i["w_expert_out"][0]
    o["w_eout"] = e.reshape(NE, 4, 128, 2, 512).transpose(0, 3, 2, 1, 4).reshape(NE, 2, 128, 2048)
    for n in "12":
        wi = ktiles(i[f"ffn{n}_wi_2"][0])
        o["w_fi" + n] = np.stack([np.concatenate([side(t(wi, j)), side(t(wi, 22 + j))], 1) for j in range(22)])
        wo = ktiles(i[f"ffn{n}_wo_2"][0])
        f = np.zeros((3, 4, 128, 2048), np.float32)
        for g in range(3):
            for c in range(4):
                x = np.concatenate([side(t(wo[:, 8 * g:8 * g + 8], 2 * c + m)) for m in range(2)], 1)
                f[g, c, :, :x.shape[1]] = x
        o["w_fo" + n] = f
    w = ktiles(i["w_in_2"][0])
    s2 = {"f": 0, "b": 512, "c": 1024, "h": 1536, "q": 2048, "k": 2560, "v": 3072, "z": 3584,
          "gf": 4112, "gs": 5136, "gd": 6160}
    at = lambda j, m: w[:, :, s2[j] + 128 * m:s2[j] + 128 * m + 128]
    o["w_ba"] = w[:, :, 4096:4112]
    o["w_sf"] = np.stack([np.concatenate([side(at("b", j), at("c", j)), side(at("h", j), at("f", j))], 1)
                          for j in range(4)])
    o["w_dn"] = np.stack([np.concatenate([side(at("q", j), at("k", j)), side(at("v", j), at("z", j))], 1)
                          for j in range(4)])
    f, c, d = (ktiles(i[n][0]) for n in ("w_fourier_2", "w_sconv_out_2", "w_dn_out_2"))
    o["w_out2"] = np.stack([np.concatenate([side(at("gf", m), at("gs", m)), side(at("gd", m)), side(t(f, m)),
                                            side(t(c, m))], 1) for m in range(8)])
    o["w_d2"] = np.stack([np.concatenate([side(t(d, 4 * j + m)) for m in range(4)], 1) for j in range(2)])
    o["w_o2"] = two(ktiles(i["w_out_2"][0]))
    o.update(constants())
    return {n: np.ascontiguousarray(v) for n, v in o.items()}


def route(k, sb, uT, b, tv, beside):
    nc, V, A, G, PE = k.nc, k.V, k.A, k.G, k.PE
    lg = sb("lg", [128, 4, 36])
    oh = sb("roh", [128, 2, 4, 32])
    ee = sb("ree", [128, 4, 32])
    e2 = sb("re2", [128, 4, 32])
    g4 = sb("rg4", [128, 3, 16])
    s = sb("rs", [128, 16, 8])
    nb = sb("rnb", [128, 3, 32])
    io = sb("rio", [128, 2, 64])
    gate = sb("gate", [128, 2, 4])
    dst = sb("dst", [128, 2, 4], U32)
    R = sb("rR", [128, 8, 64])
    B = sb("rB", [128, 8, NBLK])
    idx = sb("idx", [64, NBLK], U32)
    ov = sb("ov", [1, 1 + NOV], I32)
    cmp_ = sb("rcmp", [1, NOV, 32])
    ovf = sb("rovf", [1, NOV])

    def red(out, in_, op, *after):
        V.wait(*after)
        return V(nc.vector.tensor_reduce(out, in_, AX, op))

    def first(out, eq, w, m, t):
        t = k.tt(V, eq, eq, w, MUL, t)
        t = red(m, eq, MAX, t)
        return k.tt(V, out, eq, m.unsqueeze(2).to_broadcast(list(eq.shape)), ALU.is_equal, t)

    lgT = sb("lgT", [36, S])
    t = k.cp(A, lgT, k.ps[0:36, b, :], tv)
    k.give(t, b, b + 1)
    PE.wait(t)
    b = k.pair()
    for i in range(4):
        ins = k.tr(k.ps[:, b, 36 * i:36 * i + 36], lgT[:, 128 * i:128 * i + 128])
    t = PE(ins)
    t = k.tt(V, lg, k.ps[:, b, 0:144].rearrange("p (a c) -> p a c", a=4),
             k.vec["rb"].unsqueeze(1).to_broadcast([128, 4, 36]), ADD, t)
    k.give(t, b, b + 1)
    down, iota = io[:, 0, :], k.con["io"]
    tw = k.ts(V, down, iota, -1.0, 64.0, MUL, ADD)
    gl = lg[:, :, 0:4]
    gm, gsum, pg, m = (s[:, j, 0:4] for j in range(4))
    up = lambda x, n: x.unsqueeze(2).to_broadcast([128, 4, n])
    row = lambda x, n: x[:, 0:n].unsqueeze(1).to_broadcast([128, 4, n])
    g1, gx, gd = (g4[:, j, :].rearrange("p (a c) -> p a c", a=4) for j in range(3))
    t = red(gm, gl, MAX, t, tw)
    t1 = k.tt(V, gd, gl, up(gm, 4), SUB, t)
    t2 = k.act(gd, gd, ACT.Exp, t1)
    t = k.tt(V, gx, gl, up(gm, 4), ALU.is_equal, t)
    t = first(g1, gx, row(down, 4), m, t)
    ts_ = red(gsum, gd, ADD, t2)
    V.wait(ts_)
    tp = V(nc.vector.reciprocal(pg, gsum))
    t = k.ts(V, gx, g1, -1.0, BIG, ADD, MUL, t)
    for i in range(4):
        t0 = k.tt(V, ee[:, i, :].rearrange("p (g e) -> p g e", g=4),
                  lg[:, i, 4:36].rearrange("p (g e) -> p g e", g=4),
                  gx[:, i, :].unsqueeze(2).to_broadcast([128, 4, 8]), ADD, t)
    t = t0
    v1, v2 = s[:, 4, 0:4], s[:, 5, 0:4]
    t = red(v1, ee, MAX, t)
    t = k.tt(V, e2, ee, up(v1, 32), ALU.is_equal, t)
    t = first(oh[:, 0], e2, row(down, 32), m, t)
    t = k.stt(V, ee, oh[:, 0], -BIG, ee, MUL, ADD, t)
    t = red(v2, ee, MAX, t)
    t = k.tt(V, e2, ee, up(v2, 32), ALU.is_equal, t)
    t = first(oh[:, 1], e2, row(down, 32), m, t)
    ta = k.tt(V, v2, v2, v1, SUB, t)
    ta = k.act(v2, v2, ACT.Exp, ta)
    ta = k.ts(V, v1, v2, 1.0, None, ADD, None, ta)
    V.wait(ta)
    ta = V(nc.vector.reciprocal(v1, v1))
    ta = k.tt(V, gate[:, 0, :], v1, pg, MUL, ta, tp)
    t_gate = k.tt(V, gate[:, 1, :], v2, gate[:, 0, :], MUL, ta)
    beside()
    t = k.tt(V, e2, oh[:, 0], oh[:, 1], ADD, t)
    PE.wait(t)
    b = k.pair()
    for i in range(4):
        for j in range(i):
            k.mm(k.ps[:, b, 32 * i:32 * i + 32], k.ones, e2[:, j, :], j == 0, False)
        k.mm(k.ps[:, b, 32 * i:32 * i + 32], k.con["u"], e2[:, i, :], i == 0, True)
    for j in range(4):
        ins = k.mm(k.ps[:, b + 1, 0:32], k.ones, e2[:, j, :], j == 0, j == 3)
    t = PE(ins)
    rank = k.ps[:, b, 0:128].rearrange("p (a e) -> p a e", a=4)
    two = lambda j: s[:, j, :].rearrange("p (k a) -> p k a", k=2)
    rk, eid, obk, q, blk, u1 = (two(j) for j in (6, 7, 8, 9, 10, 11))
    cnt, nob, end = (nb[:, j, :] for j in range(3))
    t1 = k.cp(V, cnt, k.ps[:, b + 1, 0:32], t)
    for c in range(2):
        t = k.tt(V, ee, oh[:, c], rank, MUL, t, t1)
        t = red(rk[:, c, :], ee, ADD, t)
    k.give(t, b, b + 1)
    t = k.ts(V, nob, cnt, 64.0, None, ALU.is_gt, None, t)
    for n in range(2, 8):
        t = k.stt(V, nob, cnt, 64.0 * n, nob, ALU.is_gt, ADD, t)
    V.wait(t)
    t = V(nc.vector.tensor_tensor_scan(end, k.ones[:, 0:32], nob, 0.0, MUL, ADD))
    t = k.tt(V, nob, end, nob, SUB, t)
    for c in range(2):
        t = k.tt(V, ee, oh[:, c], row(nob, 32), MUL, t)
        t = red(obk[:, c, :], ee, ADD, t)
        t = k.tt(V, ee, oh[:, c], row(iota, 32), MUL, t)
        t = red(eid[:, c, :], ee, ADD, t)
    f = lambda j: s[:, j, :]
    t = k.ts(V, f(9), f(6), 64.0, None, ALU.is_ge, None, t)
    for n in range(2, 8):
        t = k.stt(V, f(9), f(6), 64.0 * n, f(9), ALU.is_ge, ADD, t)
    t = k.stt(V, f(6), f(9), -64.0, f(6), MUL, ADD, t)
    t = k.tt(V, f(11), f(9), f(8), ADD, t)
    t = k.stt(V, f(11), f(11), NE - 1.0, f(7), ADD, SUB, t)
    t = k.ts(V, f(10), f(9), 1.0, None, ALU.min, None, t)
    t = k.tt(V, f(10), f(10), f(11), MUL, t)
    t = k.tt(V, f(10), f(10), f(7), ADD, t)
    t_d = k.stt(V, dst.rearrange("p a c -> p (a c)"), f(10), 64.0, f(6), MUL, ADD, t)
    for j in range(8):
        ta = k.ts(V, R[:, j, :], iota, f(6)[:, j:j + 1], None, ALU.is_equal, None, t)
        tb = k.ts(V, B[:, j, :], iota[:, 0:NBLK], f(10)[:, j:j + 1], k.con["tok"][:, j % 4:j % 4 + 1],
                  ALU.is_equal, MUL)
    PE.wait(tb)
    b = k.pair()
    for j in range(8):
        ins = k.mm(k.ps[0:64, b, 0:NBLK], R[:, j, :], B[:, j, :], j == 0, j == 7)
    tp = PE(ins)
    t_i = k.cp(V, idx, k.ps[0:64, b, 0:NBLK], tp)
    k.give(t_i, b, b + 1)
    t = k.tt(V, cmp_, end[0:1].unsqueeze(1).to_broadcast([1, NOV, 32]),
             iota[0:1, 0:NOV].unsqueeze(2).to_broadcast([1, NOV, 32]), ALU.is_le, t)
    t = red(ovf, cmp_, ADD, t)
    t = k.ts(V, ov[:, 1:1 + NOV], ovf, NE - 1.0, None, ALU.min, None, t)
    t_o = k.cp(V, ov[:, 0:1], end[0:1, 31:32], t)
    return gate, dst, idx, ov, [t_gate, t_d, t_i, t_o]


def expert_rows(k, xg, tg, xS, free):
    PE = k.PE
    PE.wait(tg)
    b = k.pair(4)
    for x in range(8):
        ins = k.tr(k.ps[:, b, 64 * x:64 * x + 64], xg[:, 128 * x:128 * x + 128])
    t = PE(ins)
    tx = part(k, k.ps[:, b, :].rearrange("p (a c) -> p a c", a=8), xS[:, :, 0:64], xS[:, :, 64:128], t, free)
    k.give(tx, b, b + 1)
    return t, tx


def expert_in(k, W, xS, tx, tmp, act, free):
    nc, V, A, PE = k.nc, k.V, k.A, k.PE
    b = k.pair(4)
    PE.wait(tx)
    ts = []
    for c in range(2):
        for p in range(4):
            i, wh, wl = W.get()
            for y in range(2):
                for w in (wh, wl):
                    ins = k.mm(k.ps[:, b + c, :], xS[:, 2 * p + y, :], w[:, 512 * y:512 * y + 512],
                               p == 0 and y == 0 and w is wh, p == 3 and y == 1 and w is wl)
            t = PE(ins)
            W.done(i)
        t = k.cp(A, tmp[:, c, :], k.ps[64:128, b + c, :], t, free)
        t = k.tt(V, act[:, c, :], k.ps[0:64, b + c, :], tmp[:, c, :], ADD, t, free)
        ts.append(t)
        if c == 0:
            ta = k.act(tmp[:, 0, :], act[:, 0, :], ACT.Silu, t)
    th = k.tt(V, act[:, 0, :], tmp[:, 0, :], act[:, 1, :], MUL, t, ta)
    k.give(ts, b, b + 1)
    return th


def expert_turn(k, act, th, hS, free):
    b = k.pair(4)
    k.PE.wait(th)
    for x in range(4):
        ins = k.tr(k.ps[:, b, 64 * x:64 * x + 64], act[:, 0, 128 * x:128 * x + 128])
    t = k.PE(ins)
    tx = part(k, k.ps[:, b, 0:256].rearrange("p (a c) -> p a c", a=4), hS[:, :, 0:64], hS[:, :, 64:128], t, free)
    k.give(tx, b, b + 1)
    return t, tx


def expert_out(k, W, hS, th, tmp, yb, free):
    nc, V, A, PE = k.nc, k.V, k.A, k.PE
    b = k.pair(4)
    PE.wait(th)
    ts = []
    for c in range(2):
        for p in range(2):
            i, wh, wl = W.get()
            for y in range(2):
                for w in (wh, wl):
                    ins = k.mm(k.ps[:, b + c, :], hS[:, 2 * p + y, :], w[:, 512 * y:512 * y + 512],
                               p == 0 and y == 0 and w is wh, p == 1 and y == 1 and w is wl)
            t = PE(ins)
            W.done(i)
        tp = t
        t = k.cp(A, tmp[:, c, :], k.ps[64:128, b + c, :], t, free)
        ts.append(k.tt(V, yb[:, 512 * c:512 * c + 512], k.ps[0:64, b + c, :], tmp[:, c, :], ADD, t, free))
    k.give(ts, b, b + 1)
    return tp, ts


def moe(k):
    nc, V, A, G, PE = k.nc, k.V, k.A, k.G, k.PE
    uT, hT = k.uT, k.hT
    vrow = nc.dram_tensor("vrow", [S, D], F32, kind="Internal").ap()
    ys = k.ys
    with ExitStack() as st:
        def sb(name, shape, dt=F32):
            return st.enter_context(nc.sbuf_tensor(name, shape, dt)).ap()

        PE.wait(k.ld_wr)
        lb = k.pair()

        def logits(m, t):
            PE.wait(t)
            ins = k.mm(k.ps[0:36, lb, :], k.wr[:, m, :], uT[:, m, NM:L], m == 0, m == 7)
            if m == 7:
                PE(ins)

        tv = rms(k, hT, [k.vec["ffn"][:, i:i + 1] for i in range(8)], uT, NM, k.ld_h, k.sqsum is not None, logits)
        xg = sb("xg", [128, 4, D])
        dv = [Dma(nc, f"vr{i}") for i in range(4)]
        tok = []

        def rows():
            for i in range(4):
                b = k.pair()
                for x in range(8):
                    ins = k.tr(k.ps[:, b + x // 4, 128 * (x % 4):128 * (x % 4) + 128],
                               uT[:, x, NM + 128 * i:NM + 128 * i + 128])
                t = PE(ins)
                t1 = k.cp(A, xg[:, i, 0:512], k.ps[:, b, :], t)
                t2 = k.cp(A, xg[:, i, 512:1024], k.ps[:, b + 1, :], t)
                k.give(t2, b, b + 1)
                G.wait(t1, t2)
                tok.append(dv[i](nc.gpsimd.dma_start(vrow[128 * i:128 * i + 128, :], xg[:, i, :])))

        gate, dst, idx, ov, rt = route(k, sb, uT, lb, PE.last(), rows)
        for q in (V, A, PE):
            q.wait(tok)
        G.wait(rt, tok)
        with ExitStack() as st2:
            def sb2(name, shape, dt=F32):
                return st2.enter_context(nc.sbuf_tensor(name, shape, dt)).ap()

            xS = sb2("exS", [128, 2, 8, 128], F32R)
            hS = sb2("ehS", [128, 2, 4, 128], F32R)
            tmp = sb2("etmp", [64, 2, 512])
            tmo = sb2("etmo", [64, 2, 512])
            ac = sb2("eact", [64, 2, 2, 512])
            yb = sb2("yb", [64, 2, D])
            dg = [Dma(nc, f"xg{i}") for i in range(4)]
            dy = [Dma(nc, f"yb{i}") for i in range(2)]
            W = Halves(k, st2, "e", 5, [(1024, i % 2) for i in range(12 * NE)], 4)

            def gather(e, free):
                G.wait(free)
                return dg[e % 4](nc.gpsimd.indirect_dma_start(
                    out=xg[0:64, e % 4, :], out_offset=None, in_=vrow,
                    in_offset=bass.IndirectOffsetOnAxis(ap=idx[:, e:e + 1], axis=0),
                    bounds_check=S - 1, oob_is_err=False))

            tg = [gather(e, None) for e in range(4)]
            ty = [None] * 2
            turned = [None, None]
            hfree = [None, None]
            th = [None, None]
            gone, rows = [], []
            rows.append(expert_rows(k, xg[0:64, 0, :], tg[0], xS[:, 0], None))
            out = None
            for e in range(NE + 1):
                if e < NE:
                    if e + 4 < NE:
                        tg.append(gather(e + 4, rows[e][0]))
                    th[e % 2] = expert_in(k, W, xS[:, e % 2], rows[e][1], tmp, ac[:, e % 2],
                                          [turned[e % 2], th[(e + 1) % 2]])
                    gone.append(PE.last())
                if e + 1 < NE:
                    rows.append(expert_rows(k, xg[0:64, (e + 1) % 4, :], tg[e + 1], xS[:, (e + 1) % 2],
                                            gone[e - 1] if e else None))
                if e:
                    i = (e - 1) % 2
                    turned[i], t = expert_turn(k, ac[:, i], th[i], hS[:, i], hfree[i])
                    hfree[i], out = expert_out(k, W, hS[:, i], t, tmo, yb[:, i, :], [ty[i], out])
                    A.wait(out)
                    r = CAP * (e - 1)
                    ty[i] = dy[i](nc.scalar.dma_start(ys[r:r + CAP, :], yb[:, i, :]))
            k.sync_all()
            G.wait(tg)
            for q in (V, PE, A, G, k.SP):
                q.wait(rt[3], ty, k.ysz)
        overflow(k, idx, ov, vrow, ys)
        with ExitStack() as st2:
            gy = st2.enter_context(nc.sbuf_tensor("gy", [128, 4, 2, D], F32)).ap()
            dc = [[Dma(nc, f"gy{i}{c}") for c in range(2)] for i in range(4)]
            got = []
            for i in range(4):
                got.append([dc[i][c](nc.gpsimd.indirect_dma_start(
                    out=gy[:, i, c, :], out_offset=None, in_=ys,
                    in_offset=bass.IndirectOffsetOnAxis(ap=dst[:, c, i:i + 1], axis=0),
                    bounds_check=NBLK * CAP - 1, oob_is_err=False)) for c in range(2)])
            square = k.sq.rearrange("p a c -> p (a c)")[:, 0:1024].rearrange("p (t c) -> p t c", t=8)
            sfree = [k.sqfree[0], k.sqfree[1]]
            pend = []

            def sums():
                i, t = pend.pop()
                PE.wait(t)
                for x in range(8):
                    ins = k.mm(k.ps[:, 6, 128 * i:128 * i + 128], k.ones, square[:, x, :], x == 0, x == 7)
                k.sqsum = k.sqfree[0] = k.sqfree[1] = PE(ins)
                sfree[:] = [k.sqsum]

            k.take(6, 7)
            for i in range(4):
                j, tc = i, got[i]
                t = k.ts(V, gy[:, j, 0, :], gy[:, j, 0, :], gate[:, 0, i:i + 1], None, MUL, None, tc[0])
                t = k.stt(V, gy[:, j, 0, :], gy[:, j, 1, :], gate[:, 1, i:i + 1], gy[:, j, 0, :], MUL, ADD, t, tc[1])
                PE.wait(t)
                for g in range(2):
                    b = k.pair()
                    for x in range(4):
                        ins = k.tr(k.ps[:, b, 128 * x:128 * x + 128],
                                   gy[:, j, 0, 512 * g + 128 * x:512 * g + 128 * x + 128])
                    t = PE(ins)
                    h = hT[:, 4 * g:4 * g + 4, NM + 128 * i:NM + 128 * i + 128]
                    th = k.tt(V, h, h, k.ps[:, b, :].rearrange("p (a c) -> p a c", a=4), ADD, t)
                    k.give(th, b, b + 1)
                if pend:
                    sums()
                c0 = NM + 128 * i
                pend.append((i, k.act(square, hT[:, :, c0:c0 + 128], ACT.Square, th, sfree)))
            sums()
            k.sync_all()


def sem_number(sem):
    return sem.num


def overflow(k, idx, ov, vrow, ys):
    nc = k.nc
    with ExitStack() as st:
        def sb(name, shape, dt=F32):
            return st.enter_context(nc.sbuf_tensor(name, shape, dt)).ap()

        wo = sb("ovw", [128, 4, SLOT])
        ix = sb("ovi", [64, 1], U32)
        xg = sb("ovx", [64, D])
        xT = sb("ovxT", [128, 8, 64])
        hb = sb("ovh", [64, 2, 512])
        hT = sb("ovhT", [128, 4, 64])
        yb = sb("ovy", [64, D])
        before = k.PE, k.V, k.A, k.G, k.SP, k.bank
        k.PE, k.V, k.A, k.G, k.SP = (Queue(nc, e, "o" + n) for e, n in (
            (nc.tensor, "pe"), (nc.vector, "v"), (nc.scalar, "a"), (nc.gpsimd, "g"), (nc.sync, "sp")))
        PE, V, A = k.PE, k.V, k.A
        d = [Dma(nc, f"ov{i}") for i in range(8)]
        count = nc.values_load(ov[0:1, 0:1], min_val=0, max_val=NOV - 1)
        with nc.If(count > 0):
            with nc.Fori(0, NOV) as j:
                with nc.If(j < count):
                    e = nc.sync.value_load(ov[0:1, bass.ds(j + 1, 1)], min_val=0, max_val=NE - 1)
                    tw = []

                    def load(c):
                        src = k.a["w_ein"][bass.ds(e, 1), c] if c < 4 else k.a["w_eout"][bass.ds(e, 1), c - 4]
                        tw.append(d[c](nc.sync.dma_start(wo[:, c % 4, :], src.rearrange("a p m -> (a p) m"))))

                    for c in range(4):
                        load(c)
                    t = k.cp(V, ix, idx[:, bass.ds(j + NE, 1)])
                    k.G.wait(t)
                    tg = d[6](nc.gpsimd.indirect_dma_start(
                        out=xg, out_offset=None, in_=vrow,
                        in_offset=bass.IndirectOffsetOnAxis(ap=ix, axis=0), bounds_check=S - 1, oob_is_err=False))
                    PE.wait(tg)
                    for x in range(8):
                        ins = k.tr(k.ps[:, 0, 64 * x:64 * x + 64], xg[:, 128 * x:128 * x + 128])
                    t = PE(ins)
                    tx = k.cp(V, xT.rearrange("p a c -> p (a c)"), k.ps[:, 0, :], t)
                    PE.wait(tx)
                    for c in range(4):
                        PE.wait(tw[c])
                        for x in range(4):
                            ins = k.mm(k.ps[0:64, 1 + c // 2, :], xT[:, 4 * (c % 2) + x, :],
                                       wo[:, c, 512 * x:512 * x + 512], c % 2 == 0 and x == 0, c % 2 == 1 and x == 3)
                        t = PE(ins)
                        if c < 2:
                            k.SP.wait(t)
                            load(4 + c)
                        if c == 1:
                            ta = k.act(hb[:, 0, :], k.ps[0:64, 1, :], ACT.Silu, t)
                    th = k.tt(V, hb[:, 1, :], hb[:, 0, :], k.ps[0:64, 2, :], MUL, t, ta)
                    PE.wait(th)
                    for x in range(4):
                        ins = k.tr(k.ps[:, 3, 64 * x:64 * x + 64], hb[:, 1, 128 * x:128 * x + 128])
                    t = PE(ins)
                    th = k.cp(V, hT.rearrange("p a c -> p (a c)"), k.ps[:, 3, 0:256], t)
                    PE.wait(th)
                    for c in range(2):
                        PE.wait(tw[4 + c])
                        for x in range(4):
                            ins = k.mm(k.ps[0:64, 4 + c, :], hT[:, x, :], wo[:, c, 512 * x:512 * x + 512], x == 0, x == 3)
                        t = PE(ins)
                        t = k.cp(V, yb[:, 512 * c:512 * c + 512], k.ps[0:64, 4 + c, :], t)
                    k.SP.wait(t)
                    t = d[7](nc.sync.dma_start(ys[bass.ds(j * CAP + NE * CAP, CAP), :], yb))
                    k.SP.wait(t)
                    nc.all_engine_barrier()
                    n = sem_number(d[6].sem)
                    nc.gpsimd.dma_reset(range(n, n + 1))
                    nc.gpsimd.sem_clear(d[6].sem)
                    for q in (k.PE, k.V, k.A, k.G, k.SP):
                        if q.n:
                            nc.sync.sem_clear(q.sem)
                    for x in d[:6] + d[7:]:
                        nc.sync.sem_clear(x.sem)
                    nc.all_engine_barrier()
        nc.all_engine_barrier()
        k.PE, k.V, k.A, k.G, k.SP, k.bank = before


def block1_end(k):
    m2 = Dma(k.nc, "m2")
    k.G.wait(k.V.last())
    t2 = m2(k.nc.gpsimd.dma_start(k.hT[:, :, 0:NM], k.a["m2T"]))
    rms(k, k.hT, [k.vec["fin"][:, i:i + 1] for i in range(8)], k.hT, NM, k.V.last(), True,
        lambda m, t: squares(k, k.hT, m, 0, [t, t2]))
    return [k.V.last(), t2]


def post(k, y, w, r0, half, after, then):
    V = k.V

    def add(m, t):
        if half:
            t = k.stt(V, k.hT[:, m, r0:L], y[:, m, r0:L], 0.5, k.hT[:, m, r0:L], MUL, ADD, t)
        else:
            t = k.tt(V, k.hT[:, m, r0:L], k.hT[:, m, r0:L], y[:, m, r0:L], ADD, t)
        then(m, t)

    rms(k, y, w, y, r0, after, True, add)
    return V.last()


def ffn(k, r0, w0, w1, after, then):
    nc, V, A, PE = k.nc, k.V, k.A, k.PE
    n = L - r0
    with ExitStack() as st:
        def sb(name, shape, dt=F32):
            return st.enter_context(nc.sbuf_tensor(f"{name}{r0}", shape, dt)).ap()

        uh = sb("fuh", [128, 8, L], F32R)
        ul = sb("ful", [128, 8, L], F32R)
        hh = sb("fhh", [128, 10, L], F32R)
        hl = sb("fhl", [128, 10, L], F32R)
        sg = sb("fsg", [128, 2, L])
        y = k.uT
        sizes = []
        for g in range(3):
            t = min(8, 22 - 8 * g)
            sizes += [(1024, False), (1024, True)] * t + [(128 * t, False), (128 * t, True)] * 4
        W = Halves(k, st, f"f{r0}", 3, sizes)
        two = (lambda x: x.rearrange("p (a c) -> p a c", a=2)) if n > 512 else (lambda x: x)
        acc = (lambda b: k.wide(b)) if n > 512 else (lambda b: k.ps[:, b, 0:n])
        W.begin()
        tu = []
        rms(k, k.hT, w0, k.uT, r0, after, True,
            lambda m, t: tu.append(part(k, k.uT[:, m, r0:L], uh[:, m, r0:L], ul[:, m, r0:L], t)))
        v3 = lambda w, c: [w[:, 128 * x:128 * x + 128] for x in range(c)]
        free = [None, None]
        hfree = {}
        for g in range(3):
            nt = min(8, 22 - 8 * g)
            for j in range(8 * g, 8 * g + nt):
                bs = []
                for x in range(2):
                    i, wh, wl = W.get()
                    b = k.pair(4)
                    bs.append((b, linear3(k, b, v3(wh, 8), v3(wl, 8), tiles(uh, 8), tiles(ul, 8), r0, L, tu)))
                    tu = None
                    W.done(i)
                (b, t), (b2, t2) = bs
                ts = k.act(two(sg[:, j % 2, r0:L]), acc(b), ACT.Silu, t, free[j % 2])
                k.give(ts, b, b + 1)
                tv = k.tt(V, two(sg[:, j % 2, r0:L]), acc(b2), two(sg[:, j % 2, r0:L]), MUL, t2, ts)
                k.give(tv, b2, b2 + 1)
                free[j % 2] = part(k, sg[:, j % 2, r0:L], hh[:, j % 10, r0:L], hl[:, j % 10, r0:L], tv,
                                   hfree.get(j - 10))
            PE.wait(free)
            for m in range(8):
                i, wh, wl = W.get()
                b = k.pair(4 if g < 2 else 3)
                xs = [(8 * g + x) % 10 for x in range(nt)]
                t = linear3(k, b, v3(wh, nt), v3(wl, nt), [hh[:, x, :] for x in xs], [hl[:, x, :] for x in xs], r0, L)
                W.done(i)
                if g == 0:
                    ty = k.cp(V, two(y[:, m, r0:L]), acc(b), t)
                else:
                    ty = k.tt(V, two(y[:, m, r0:L]), acc(b), two(y[:, m, r0:L]), ADD, t, ytok[m])
                if m == 0:
                    ytok = {} if g == 0 else ytok
                ytok[m] = ty
                k.give(ty, b, b + 1)
                if g == 2 and m:
                    squares(k, y, m - 1, r0, ytok[m - 1])
            for x in range(nt):
                hfree[8 * g + x] = PE.last()
        squares(k, y, 7, r0, ty)
        t = post(k, y, w1, r0, True, [V.last(), A.last()], then)
        k.sync_all()
    return t


def conv(k, out, xb, w, tx, free):
    V = k.V
    t = k.ts(V, out, xb[:, 0:L], w[0], None, MUL, None, tx, free)
    t = k.stt(V, out, xb[:, 1:L + 1], w[1], out, MUL, ADD, t)
    return k.stt(V, out, xb[:, 2:L + 2], w[2], out, MUL, ADD, t)


def conv_fourier(k, sc, fo, tu, beside):
    nc, V, A, G, PE = k.nc, k.V, k.A, k.G, k.PE
    uT = k.uT
    two = lambda x: x.rearrange("p (a c) -> p a c", a=2)
    with ExitStack() as st:
        def sb(name, shape):
            return st.enter_context(nc.sbuf_tensor(name, shape, F32)).ap()

        xb = sb("cxb", [128, 2, L + 2])
        bt = sb("cbt", [128, 2, L])
        ct = sb("cct", [128, 2, L])
        uf = sb("cuf", [128, 2, L])
        cs = sb("ccs", [C2, NC2, 4, 256])
        dfs = sb("dfs", [128, 256])
        dft = sb("dft", [128, NC2, 2, L])
        d = [Dma(nc, f"df{i}") for i in range(NC2 + 1)]
        A.wait(k.V.last(), k.PE.last())
        td = [d[i](nc.scalar.dma_start(dft[:, i].rearrange("p a c -> p (a c)"), k.a["dft"][i])) for i in range(NC2)]
        ts_ = d[NC2](nc.scalar.dma_start(dfs, k.a["dfs"]))
        tz = V(nc.vector.memset(xb, 0.0))
        hist = []
        tcs = []
        for j in range(4):
            i = j % 2
            old = hist[j - 2] if j >= 2 else (None, None, None)
            c, w = k.weight()
            wv = w.rearrange("p (t c) -> p t c", t=8)
            b = k.pair()
            t = linear(k, b, [wv[:, x, 0:128] for x in range(8)], tiles(uT, 8), 0, L, after=None if j else tu)
            tb = k.cp(A, two(bt[:, i]), k.wide(b), t, old[0])
            k.give(tb, b, b + 1)
            b = k.pair()
            t = linear(k, b, [wv[:, x, 128:256] for x in range(8)], tiles(uT, 8), 0, L)
            k.release(c)
            tc = k.cp(A, two(ct[:, i]), k.wide(b), t, old[1])
            k.give(tc, b, b + 1)
            c, w = k.weight()
            wv = w.rearrange("p (t c) -> p t c", t=8)
            b = k.pair()
            t = linear(k, b, [wv[:, x, 0:128] for x in range(8)], tiles(uT, 8), 0, L)
            tx = k.tt(V, two(xb[:, i, 1:L + 1]), k.wide(b), two(ct[:, i]), MUL, t, tc, tz, old[0])
            k.give(tx, b, b + 1)
            b = k.pair()
            t = linear(k, b, [wv[:, x, 128:256] for x in range(8)], tiles(uT, 8), 0, L)
            k.release(c)
            tf = k.cp(A, two(uf[:, i]), k.wide(b), t, old[2])
            k.give(tf, b, b + 1)
            wv = [k.vec["sc"][:, 4 * x + j:4 * x + j + 1] for x in range(3)]
            t = conv(k, sc[:, j, :], xb[:, i], wv, tx, None)
            t = k.tt(V, sc[:, j, :], sc[:, j, :], bt[:, i], MUL, t, tb)
            if j < 2:
                next(beside)
            PE.wait(tf, ts_)
            for g in range(3):
                b = k.pair()
                for h in range(2):
                    n = 2 * g + h
                    tp = PE(k.mm(k.ps[0:C2, b + h, 0:256], uf[:, i, C2 * n:C2 * n + C2], dfs, True, True))
                ta = k.cp(V, cs[:, 2 * g:2 * g + 2, j, :], k.ps[0:C2, b:b + 2, 0:256], tp)
                k.give(ta, b, b + 1)
            tcs.append(ta)
            hist.append((t, tx, tp))
        PE.wait(tcs, td)
        for j in range(4):
            b = k.pair()
            for n in range(NC2):
                for p in range(2):
                    for h, (c0, c1) in enumerate(split(0, L)):
                        ins = k.mm(k.ps[:, b + h, 0:HF], cs[:, n, j, 128 * p:128 * p + 128],
                                   dft[0:C2, n, p, c0:c1], n == 0 and p == 0, n == NC2 - 1 and p == 1)
            t = PE(ins)
            t = k.cp(A, two(fo[:, j, :]), k.wide(b), t)
            k.give(t, b, b + 1)
        k.sync_all()


def decays(k, sb, tu, res):
    nc, V, A, G, PE = k.nc, k.V, k.A, k.G, k.PE
    uT = k.uT
    g_ = sb("ng", [C2, NC2, 8])
    be = sb("nbe", [C2, NC2, 8])
    tmp = sb("ntm", [C2, 2, NC2, 8])
    gc = sb("ngc", [C2, NC2, 8])
    eg = sb("neg", [C2, NC2, 8])
    el = sb("nel", [C2, NC2, 8])
    bg = sb("nbg", [C2, NC2, 8])
    ea = sb("nea", [128, 8])
    def turns():
        PE.wait(tu, k.ld_wba)
        b = k.pair()
        for n in range(NC2):
            for x in range(8):
                ins = k.mm(k.ps[0:C2, b, 16 * n:16 * n + 16], uT[:, x, C2 * n:C2 * n + C2], k.wba[:, x, :],
                           x == 0, x == 7)
        t = PE(ins)
        src = k.ps[0:C2, b, 0:96].rearrange("p (n c) -> p n c", n=NC2)
        t0 = k.act(be, src[:, :, 0:8], ACT.Sigmoid, t)
        x_, y_ = tmp[:, 0], tmp[:, 1]
        t = k.tt(V, x_, src[:, :, 8:16], k.vec["dt"][0:C2].unsqueeze(1).to_broadcast([C2, NC2, 8]), ADD, t0)
        k.give([t, t0], b, b + 1)
        ta = k.act(y_, x_, ACT.Abs, t)
        ta = k.act(y_, y_, ACT.Exp, ta, scale=-1.0)
        ta = k.act(y_, y_, ACT.Ln, ta, bias=1.0)
        t = k.stt(V, x_, x_, 0.0, y_, MAX, ADD, ta)
        te = k.act(ea, k.vec["al"], ACT.Exp)
        t = k.stt(V, g_, x_, -1.0, ea[0:C2].unsqueeze(1).to_broadcast([C2, NC2, 8]), MUL, MUL, t, te)
        yield
        PE.wait(t)
        b = k.pair()
        gf = g_.rearrange("p n c -> p (n c)")
        one = k.ones[0:C2, 0:C2]
        k.mm(k.ps[0:C2, b, 0:48], k.con["ui"][0:C2, 0:C2], gf, True, True)
        k.mm(k.ps[0:C2, b, 48:96], k.con["li"][0:C2, 0:C2], gf, True, True)
        t = PE(k.mm(k.ps[0:C2, b, 96:144], one, gf, True, True))
        v8 = lambda o: k.ps[0:C2, b, o:o + 48].rearrange("p (n c) -> p n c", n=NC2)
        t1 = k.cp(V, gc[:, :, 0:4], v8(0)[:, :, 0:4], t)
        t1 = k.cp(V, gc[:, :, 4:8], v8(48)[:, :, 4:8], t)
        t2 = k.tt(V, el, v8(96), gc, SUB, t1)
        k.give(t2, b, b + 1)
        ta = k.act(el, el, ACT.Exp, t2)
        ta = k.act(eg, gc, ACT.Exp, t1)
        tcol = k.tt(V, bg, be, eg, MUL, ta, t0)
        res.extend([g_, be, gc, eg, el, bg, tcol])
        yield

    return turns()


def deltanet(k, dn, tu, dec, fillers):
    nc, V, A, G, PE = k.nc, k.V, k.A, k.G, k.PE
    uT = k.uT
    two = lambda x: x.rearrange("p (a c) -> p a c", a=2)
    six = lambda x: x.rearrange("p (n c) -> p n c", n=NC2)
    chunk = lambda b, n, p=128: k.ps[0:p, b + n // 3, C2 * (n % 3):C2 * (n % 3) + C2]
    with ExitStack() as st:
        def sb(name, shape):
            return st.enter_context(nc.sbuf_tensor(name, shape, F32)).ap()

        lv = sb("lv2", [128, 2, 7, C2])
        dl = Dma(nc, "lv2")
        A.wait(V.last(), PE.last())
        tlv = dl(nc.scalar.dma_start(lv.rearrange("p a b c -> p (a b c)"), k.a["lv2"]))
        xb = sb("nxb", [128, 2, L + 2])
        qkv = sb("nqkv", [128, 3, L])
        z_ = sb("nz", [128, L])
        kt = sb("nkt", [C2, NC2, 128])
        vt = sb("nvt", [C2, NC2, 128])
        KK = sb("nKK", [C2, 2, L])
        of = xb[:, 0, 1:L + 1]
        EG = sb("nEG", [128, 2, L])
        DT = sb("nDT", [C2, 2, L])
        MT = sb("nMT", [C2, 2, L])
        AT = DT
        wT = sb("nT", [128, 2, L])
        T = wT[0:C2]
        TT = sb("nTT", [C2, 2, L])
        CP = sb("nCP", [C2, 4, L])
        Cl, P1 = CP[:, 0:2, :], CP[:, 2:4, :]
        u_ = CP.rearrange("p a c -> p (a c)")[:, 0:2 * NC2 * 128].rearrange("p (a n c) -> p a n c", a=2, n=NC2)
        vb = sb("nvb", [C2, 2, NC2, 128])
        kb = sb("nkb", [C2, 2, NC2, 128])
        kdec = sb("nkd", [C2, 2, NC2, 128])
        vn = xb[0:C2, 1, 1:513].rearrange("p (d s c) -> p d s c", d=2, s=2)
        Sd = sb("nSd", [128, 2, 128])
        g_, be, gc, eg, el, bg, tcol = dec
        tz = V(nc.vector.memset(xb, 0.0))
        free = {}
        PE.wait(tcol, tlv)
        for h in range(4):
            rest = [None]

            def fill(n):
                while n and rest[0] is not None:
                    if next(rest[0], None) is None:
                        rest[0] = None
                    n -= 1

            tok = []
            for j in range(4):
                if j % 2 == 0:
                    c, w = k.weight()
                    wv = w.rearrange("p (t c) -> p t c", t=8)
                b = k.pair()
                o = 128 * (j % 2)
                t = linear(k, b, [wv[:, x, o:o + 128] for x in range(8)], tiles(uT, 8), 0, L)
                if j % 2:
                    k.release(c)
                if j == 3:
                    tz_ = k.act(two(z_), k.wide(b), ACT.Silu, t, free.get("z"))
                    k.give(tz_, b, b + 1)
                    break
                t = k.cp(A, two(xb[:, j % 2, 1:L + 1]), k.wide(b), t, tz, free.get(("xb", j % 2)))
                k.give(t, b, b + 1)
                wc = [k.vec["dc"][:, 12 * x + 4 * j + h:12 * x + 4 * j + h + 1] for x in range(3)]
                t = conv(k, qkv[:, j, :], xb[:, j % 2], wc, t, free.get(("qkv", j)))
                free[("xb", j % 2)] = t
                tok.append(k.act(qkv[:, j, :], qkv[:, j, :], ACT.Silu, t))
            rest[0] = fillers(h)
            tq = [k.act(k.sq[:, j, :], qkv[:, j, :], ACT.Square, tok[j], k.sqfree[j]) for j in range(2)]
            for j in range(2):
                fill(2)
                PE.wait(tq[j])
                b = k.pair()
                for x, (c0, c1) in enumerate(split(0, L)):
                    ins = k.mm(k.ps[:, b + x, 0:HF], k.ones, k.sq[:, j, c0:c1], True, True)
                t = PE(ins)
                k.sqfree[j] = t
                t = k.act(two(k.rb), k.wide(b), ACT.Sqrt, t, k.rbfree, bias=k.eps[:, 0:1])
                k.give(t, b, b + 1)
                V.wait(t)
                t = V(nc.vector.reciprocal(k.rb, k.rb))
                tok[j] = k.stt(V, qkv[:, j, :], qkv[:, j, :], 128.0 ** -0.5 if j == 0 else 1.0, k.rb, MUL, MUL, t)
                k.rbfree = tok[j]
            q_, k_, v_ = (qkv[:, j, :] for j in range(3))
            tm = []
            for dst, src, tk in ((vt, v_, tok[2]), (kt, k_, tok[1])):
                fill(3)
                PE.wait(tk)
                for g in range(2):
                    b = k.pair()
                    for n in range(3):
                        ins = k.tr(k.ps[0:C2, b, 128 * n:128 * n + 128], src[:, C2 * (3 * g + n):C2 * (3 * g + n) + C2])
                    t = PE(ins)
                    t = k.cp(V, dst[:, 3 * g:3 * g + 3, :].rearrange("p a c -> p (a c)"), k.ps[0:C2, b, 0:384], t)
                    k.give(t, b, b + 1)
                    tm.append(t)
            fill(2)
            PE.wait(tok[0])
            for x, other in enumerate((k_, q_)):
                b = k.pair()
                for n in range(NC2):
                    ins = k.mm(chunk(b, n, C2), k_[:, C2 * n:C2 * n + C2], other[:, C2 * n:C2 * n + C2], True, True)
                t = PE(ins)
                tkk = k.cp(V if x else A, two(KK[:, x, :]), k.ps[0:C2, b:b + 2, 0:HF], t, free.get(("KK", x)))
                k.give(tkk, b, b + 1)
                tm.append(tkk)
            D = [dict(), dict()]
            for d in range(2):
                s = D[d]
                hh = 4 * d + h
                tri = k.con["ui" if d == 0 else "li"][0:C2, 0:C2]
                b = k.pair()
                PE.wait(tcol)
                for n in range(NC2):
                    ins = k.mm(chunk(b, n), g_[:, n, hh:hh + 1].to_broadcast([C2, 128]), tri, True, True)
                t = PE(ins)
                fill(1)
                s["EG"] = k.act(two(EG[:, d, :]), k.wide(b), ACT.Exp, t)
                mask = k.con["mf" if d == 0 else "mb"][0:C2, 0:C2]
                for n in range(NC2):
                    t1 = k.stt(V, DT[:, d, C2 * n:C2 * n + C2], chunk(b, n, C2), gc[:, n, hh:hh + 1], mask, SUB, ADD, s["EG"])
                k.give([s["EG"], t1], b, b + 1)
                t1 = k.act(DT[:, d, :], DT[:, d, :], ACT.Exp, t1)
                b = k.pair()
                for n in range(NC2):
                    ins = k.mm(chunk(b, n, C2), be[:, n, hh:hh + 1].to_broadcast([C2, C2]), k.ident[0:C2, 0:C2],
                               True, True)
                t = PE(ins)
                t2 = k.tt(V, two(MT[:, d, :]), k.ps[0:C2, b:b + 2, 0:HF], two(DT[:, d, :]), MUL, t, t1)
                k.give(t2, b, b + 1)
                s["MT"] = k.tt(V, MT[:, d, :], MT[:, d, :], KK[:, 0, :], MUL, t2, tm)
                s["AT"] = k.tt(V, AT[:, d, :], DT[:, d, :], KK[:, 1, :], MUL, t2, tm)
                for n in range(NC2):
                    k.ts(G, vb[:, d, n, :], vt[:, n, :], be[:, n, hh:hh + 1], None, MUL, None, tm, tcol)
                    k.ts(G, kb[:, d, n, :], kt[:, n, :], bg[:, n, hh:hh + 1], None, MUL)
                    s["cols"] = k.ts(G, kdec[:, d, n, :], kt[:, n, :], el[:, n, hh:hh + 1], None, MUL)
                lvl = lambda m: lv[0:C2, d, m, 0:C2].unsqueeze(1).to_broadcast([C2, NC2, C2])
                t = k.tt(V, six(TT[:, d, :]), six(MT[:, d, :]), lvl(0), MUL, s["MT"])
                idn = k.ident[0:C2, 0:C2].unsqueeze(1).to_broadcast([C2, NC2, C2])
                t = k.tt(V, six(TT[:, d, :]), idn, six(TT[:, d, :]), SUB, t)
                fill(4)
                PE.wait(t)
                b = k.pair()
                for n in range(NC2):
                    ins = k.tr(chunk(b, n, C2), TT[:, d, C2 * n:C2 * n + C2])
                t = PE(ins)
                s["T"] = k.cp(A, two(T[:, d, :]), k.ps[0:C2, b:b + 2, 0:HF], t)
                k.give(s["T"], b, b + 1)
            at = lambda X, d, n: X[:, d, C2 * n:C2 * n + C2]
            pv = lambda b: k.ps[0:C2, b:b + 2, 0:HF]
            for m in range(1, 7):
                for d in range(2):
                    if d == 0:
                        fill(1)
                    s = D[d]
                    t = k.tt(V, six(Cl[:, d, :]), six(MT[:, d, :]),
                             lv[0:C2, d, m, 0:C2].unsqueeze(1).to_broadcast([C2, NC2, C2]), MUL, s.get("mm1"))
                    PE.wait(t, s["T"])
                    b = k.pair()
                    for n in range(NC2):
                        ins = k.mm(chunk(b, n, C2), at(Cl, d, n), at(T, d, n), True, True)
                    s["mm1"] = PE(ins)
                    s["P1"] = k.cp(A, two(P1[:, d, :]), pv(b), s["mm1"], s.get("mm2"))
                    k.give(s["P1"], b, b + 1)
                for d in range(2):
                    s = D[d]
                    PE.wait(s["P1"])
                    b = k.pair()
                    for n in range(NC2):
                        ins = k.mm(chunk(b, n, C2), at(P1, d, n), at(TT, d, n), True, True)
                    s["mm2"] = PE(ins)
                    s["T"] = k.tt(V, two(TT[:, d, :]), two(TT[:, d, :]), pv(b), SUB, s["mm2"])
                    k.give(s["T"], b, b + 1)
                for d in range(2 if m < 6 else 0):
                    s = D[d]
                    if d == 0:
                        fill(1)
                    PE.wait(s["T"])
                    b = k.pair()
                    for n in range(NC2):
                        ins = k.tr(chunk(b, n, C2), at(TT, d, n))
                    t = PE(ins)
                    s["T"] = k.cp(A, two(T[:, d, :]), pv(b), t)
                    k.give(s["T"], b, b + 1)
            for d in range(2):
                s = D[d]
                PE.wait(s["T"], s["cols"])
                for g in range(2):
                    b = k.pair()
                    for n in range(3):
                        ins = k.mm(k.ps[0:C2, b, 128 * n:128 * n + 128], at(TT, d, 3 * g + n), vb[:, d, 3 * g + n, :],
                                   True, True)
                    t = PE(ins)
                    s["u"] = k.cp(A, u_[:, d, 3 * g:3 * g + 3, :].rearrange("p a c -> p (a c)"),
                                  k.ps[0:C2, b, 0:384], t)
                    k.give(s["u"], b, b + 1)
                b = k.pair()
                for n in range(NC2):
                    ins = k.mm(chunk(b, n), kb[:, d, n, :], at(TT, d, n), True, True)
                t = PE(ins)
                s["w"] = k.cp(A, two(wT[:, d, :]), k.wide(b), t)
                k.give(s["w"], b, b + 1)
            tof = [None] * NC2
            for step in range(NC2):
                for d in range(2):
                    s = D[d]
                    n = step if d == 0 else NC2 - 1 - step
                    cols = slice(C2 * n, C2 * n + C2)
                    if step == 0:
                        vnew, tv = u_[:, d, n, :], s["u"]
                    else:
                        fill(1)
                        PE.wait(s["S"], s["w"])
                        b = k.pair()
                        t = PE(k.mm(k.ps[0:C2, b, 0:128], wT[:, d, cols], Sd[:, d, :], True, True))
                        tv = k.tt(V, vn[:, d, step % 2, :], u_[:, d, n, :], k.ps[0:C2, b, 0:128], SUB, t, s["u"],
                                  s.get("vfree"))
                        k.give(tv, b, b + 1)
                        vnew = vn[:, d, step % 2, :]
                    b = k.pair()
                    fill(1)
                    PE.wait(tv, s["AT"])
                    if step:
                        tq = k.tt(V, k.sq[:, d, 0:C2], q_[:, cols], EG[:, d, cols], MUL, s["EG"], s.get("o"),
                                  k.sqfree[d])
                        PE.wait(tq)
                        k.mm(k.ps[:, b, 0:C2], Sd[:, d, :], k.sq[:, d, 0:C2], True, False)
                    s["o"] = PE(k.mm(k.ps[:, b, 0:C2], vnew, AT[:, d, cols], step == 0, True))
                    if step < NC2 - 1:
                        t = PE(k.mm(k.ps[:, b + 1, 0:128], kdec[:, d, n, :], vnew, True, True))
                    s["vfree"] = PE.last()
                    if step < 3:
                        to = k.cp(A, of[:, cols], k.ps[:, b, 0:C2], s["o"])
                        tof[n] = to
                    else:
                        to = k.tt(V, of[:, cols], of[:, cols], k.ps[:, b, 0:C2], ADD, s["o"], tof[n])
                    if step < NC2 - 1:
                        if step == 0:
                            s["S"] = k.cp(V, Sd[:, d, :], k.ps[:, b + 1, 0:128], t)
                        else:
                            e = C2 * n + C2 - 1 if d == 0 else C2 * n
                            s["S"] = k.stt(V, Sd[:, d, :], Sd[:, d, :], EG[:, d, e:e + 1], k.ps[:, b + 1, 0:128],
                                           MUL, ADD, t, s["EG"])
                        k.give([to, s["S"]], b, b + 1)
                    else:
                        k.give(to, b, b + 1)
            for d in range(2):
                k.sqfree[d] = D[d]["o"]
            t = k.act(k.sq[:, 0, :], of, ACT.Square, to, k.sqfree[0])
            fill(1)
            PE.wait(t)
            b = k.pair()
            for x, (c0, c1) in enumerate(split(0, L)):
                ins = k.mm(k.ps[:, b + x, 0:HF], k.ones, k.sq[:, 0, c0:c1], True, True)
            t = PE(ins)
            k.sqfree[0] = t
            t = k.act(two(k.rb), k.wide(b), ACT.Sqrt, t, k.rbfree, bias=k.eps[:, 0:1], scale=1.0 / 128)
            k.give(t, b, b + 1)
            V.wait(t)
            t = V(nc.vector.reciprocal(k.rb, k.rb))
            t = k.stt(V, k.rb, k.rb, k.vec["dn"], z_, MUL, MUL, t, tz_)
            t = k.tt(V, dn[:, h, :], of, k.rb, MUL, t)
            k.rbfree = t
            fill(1000)
            k.sync_all()


def mixer(k, w2, w3, after):
    nc, V, A, G, PE = k.nc, k.V, k.A, k.G, k.PE
    two = lambda x: x.rearrange("p (a c) -> p a c", a=2)
    tu = rms(k, k.hT, w2, k.uT, 0, after, True)
    with ExitStack() as st:
        def sb(name, shape):
            return st.enter_context(nc.sbuf_tensor(name, shape, F32)).ap()

        sc = sb("msc", [128, 4, L])
        fo = sb("mfo", [128, 4, L])
        dn = sb("mdn", [128, 4, L])
        dec = []
        conv_fourier(k, sc, fo, tu, decays(k, sb, tu, dec))
        spill = nc.dram_tensor("hspill", [128, 8, L], F32, kind="Internal").ap()
        gd = nc.dram_tensor("gspill", [128, 8, L], F32, kind="Internal").ap()
        dh = Dma(nc, "hs")
        G.wait(V.last(), A.last())
        th = dh(nc.gpsimd.dma_start(spill, k.hT))
        mg = k.hT
        gt = sb("mgt", [128, 3, L])
        dg = Dma(nc, "gs")
        gfree = [None, None, None]

        def product(ws, x):
            k.take(6, 7)
            n = len(ws)
            for t in range(n):
                for j, (c0, c1) in enumerate(split(0, L)):
                    ins = k.mm(k.ps[:, 6 + j, 0:HF], ws[t], x[:, t, c0:c1], t == 0, t == n - 1)
                if t < n - 1:
                    yield 1
            return PE(ins)

        def fillers(h):
            for m in (2 * h, 2 * h + 1):
                i, w = k.weight()
                wv = w.rearrange("p (t c) -> p t c", t=8)
                tg = []
                for j in range(2):
                    t = yield from product([wv[:, x, 128 * j:128 * j + 128] for x in range(8)], k.uT)
                    tg.append(k.act(two(gt[:, j, :]), k.wide(6), ACT.Sigmoid, t, gfree[j]))
                    k.give(tg[j], 6, 7)
                    yield 1
                k.release(i)
                i, w = k.weight()
                t = yield from product(tiles(w[:, 1024:1536].rearrange("p (t c) -> p t c", t=4), 4), fo)
                ta = k.tt(V, two(mg[:, m, :]), k.wide(6), two(gt[:, 0, :]), MUL, t, tg[0], th)
                gfree[0] = ta
                k.give(ta, 6, 7)
                yield 1
                t = yield from product(tiles(w[:, 1536:2048].rearrange("p (t c) -> p t c", t=4), 4), sc)
                t = k.tt(V, two(gt[:, 1, :]), k.wide(6), two(gt[:, 1, :]), MUL, t, tg[1])
                k.give(t, 6, 7)
                gfree[1] = k.tt(V, mg[:, m, :], mg[:, m, :], gt[:, 1, :], ADD, t, ta)
                yield 1
                wv = w[:, 0:1024].rearrange("p (t c) -> p t c", t=8)
                t = yield from product(tiles(wv, 8), k.uT)
                k.release(i)
                t = k.act(two(gt[:, 2, :]), k.wide(6), ACT.Sigmoid, t, gfree[2])
                k.give(t, 6, 7)
                G.wait(t)
                gfree[2] = dg(nc.gpsimd.dma_start(gd[:, m, :], gt[:, 2, :]))
                yield 1

        deltanet(k, dn, tu, dec, fillers)
        gb = y = sb("mgb", [128, 8, L])
        dl = Dma(nc, "gl")
        G.wait(gfree)
        tl = dl(nc.gpsimd.dma_start(gb, gd))
        tm = []
        for m in range(8):
            if m % 4 == 0:
                i, w = k.weight()
            b = k.pair()
            o = 512 * (m % 4)
            t = linear(k, b, tiles(w[:, o:o + 512].rearrange("p (t c) -> p t c", t=4), 4), tiles(dn, 4), 0, L)
            if m % 4 == 3:
                k.release(i)
            t = k.tt(V, two(gb[:, m, :]), k.wide(b), two(gb[:, m, :]), MUL, t, tl)
            k.give(t, b, b + 1)
            tm.append(k.tt(V, mg[:, m, :], mg[:, m, :], gb[:, m, :], ADD, t))
        mh = st.enter_context(nc.sbuf_tensor("mmh", [128, 8, L], F32R)).ap()
        ml = st.enter_context(nc.sbuf_tensor("mml", [128, 8, L], F32R)).ap()
        W = Halves(k, st, "m2", 2, [(1024, False), (1024, True)] * 4)
        W.begin()
        tp = [part(k, mg[:, m, :], mh[:, m, :], ml[:, m, :], tm[m]) for m in range(8)]
        G.wait(tp)
        th = dh(nc.gpsimd.dma_start(k.hT, spill))
        for m in range(8):
            i, wh, wl = W.get()
            b = k.pair()
            v3 = lambda w: [w[:, 128 * x:128 * x + 128] for x in range(8)]
            t = linear3(k, b, v3(wh), v3(wl), tiles(mh, 8), tiles(ml, 8), 0, L, None if m else tp)
            W.done(i)
            before = ty if m else None
            ty = k.cp(A if m % 2 else V, two(y[:, m, :]), k.wide(b), t)
            k.give(ty, b, b + 1)
            if m:
                squares(k, y, m - 1, 0, before)
        V.wait(th)
        squares(k, y, 7, 0, ty)
        t = post(k, y, w3, 0, False, [V.last(), A.last()], lambda m, t: squares(k, k.hT, m, NM, t))
        k.sync_all()
    return t


def block2(k, t):
    gain = lambda j: [k.vec["g"][:, 8 * j + i:8 * j + i + 1] for i in range(8)]
    t = ffn(k, 0, gain(0), gain(1), t, lambda m, t: squares(k, k.hT, m, 0, t))
    t = mixer(k, gain(2), gain(3), t)
    done = []

    def give_out(m, t):
        q = k.SP
        q.wait(t)
        done.append(Dma(k.nc, f"out{m}")(k.nc.sync.dma_start(k.out[:, m, :], k.hT[:, m, NM:L])))

    ffn(k, NM, gain(4), gain(5), t, give_out)
    return done


def program(nc, a, out):
    k = K(nc, a, out)
    setup(k)
    block1(k)
    moe(k)
    t = block1_end(k)
    t = block2(k, t)
    k.SP.wait(t, k.ysz)


def kernel(**inputs):
    import concourse.bacc as bacc
    from concourse.bass_utils import run_bass_kernel_spmd

    nc = bacc.Bacc("TRN2", target_bir_lowering=False, num_devices=1)
    arrays = {"in_" + n: v for n, v in layout(inputs).items()}
    a = {n[3:]: nc.dram_tensor(n, v.shape, mybir.dt.from_np(v.dtype), kind="ExternalInput").ap()
         for n, v in arrays.items()}
    out = nc.dram_tensor("out", (128, 8, S), F32, kind="ExternalOutput").ap()
    program(nc, a, out)
    r = run_bass_kernel_spmd(nc, [arrays], core_ids=[0])
    y = r.results[0]["out"]
    return np.ascontiguousarray(y.transpose(1, 0, 2).reshape(D, S).T)[None]
```
